# Optimizing a Trainium2 kernel written in Bass

```python
import math
import jax, jax.numpy as jnp
from jax import lax
import numpy as np
import jax
import jax.numpy as jnp

D_MODEL = 1024
BATCH = 1
SEQ = 256
DEPTH = 2

GRID_W = 64
N_EVEN = (DEPTH + 1) // 2
N_ODD = DEPTH // 2
D_FF = 4 * D_MODEL
NORM_EPS = 1e-6

SSD_HEAD_DIM = 64
SSD_WIDTH = D_MODEL
SSD_HEADS = SSD_WIDTH // SSD_HEAD_DIM
SSD_GROUPS = 2
SSD_STATE = 128
SSD_CONV = 5
SSD_CHUNK = 128
SSD_CONV_CH = SSD_WIDTH + 2 * SSD_GROUPS * SSD_STATE

NA_HEAD_DIM = 64
NA_WIDTH = D_MODEL
NA_HEADS = NA_WIDTH // NA_HEAD_DIM
NA_KH_MAX = 8
NA_KW = 16

AB_IN = SSD_WIDTH + SSD_CONV_CH + 2 * SSD_HEADS + 3 * NA_WIDTH
AB_MIX = SSD_WIDTH + NA_WIDTH

ML_HEADS = 8
ML_DV = 2 * D_MODEL // ML_HEADS
ML_DK = ML_DV // 2
ML_CHUNK = 128
ML_WIDTH = ML_HEADS * ML_DV
ML_QK = ML_HEADS * ML_DK
ML_IN = 2 * ML_QK + 2 * ML_WIDTH + 4 * ML_HEADS


def rmsnorm(x, g):
    xf = x.astype(jnp.float32)
    y = xf * lax.rsqrt(jnp.mean(xf * xf, axis=-1, keepdims=True) + NORM_EPS)
    return (y * g.astype(jnp.float32)).astype(x.dtype)

def modulate(h, shift, scale):
    return h * (1 + scale[:, None, :]) + shift[:, None, :]

def centred_dwconv(u, w, b):
    pad = w.shape[0] // 2
    out = lax.conv_general_dilated(u, w[:, None, :].astype(u.dtype), window_strides=(1,),
                                   padding=[(pad, pad)], dimension_numbers=('NWC', 'WIO', 'NWC'),
                                   feature_group_count=u.shape[-1])
    return out + b

def segsum(a):
    T = a.shape[-1]
    cs = jnp.cumsum(a, axis=-1)
    diff = cs[..., :, None] - cs[..., None, :]
    mask = jnp.tril(jnp.ones((T, T), dtype=bool))
    return jnp.where(mask, diff, -jnp.inf)

def ssd_scan(xh, dt, a, bm, cm):
    Bsz, L, H, P = xh.shape
    G, N = bm.shape[-2:]
    R = H // G
    T = SSD_CHUNK
    nc = L // T
    X = (xh * dt[..., None]).reshape(Bsz, nc, T, G, R, P)
    adt = (dt * a).reshape(Bsz, nc, T, G, R).transpose(0, 3, 4, 1, 2)
    Bc = bm.reshape(Bsz, nc, T, G, N)
    Cc = cm.reshape(Bsz, nc, T, G, N)
    a_cs = jnp.cumsum(adt, axis=-1)
    Lmat = jnp.exp(segsum(adt))
    cb = jnp.einsum('bctgn,bcsgn->bgcts', Cc, Bc)
    y_diag = jnp.einsum('bgrcts,bcsgrp->bctgrp', cb[:, :, None] * Lmat, X)
    decay_states = jnp.exp(a_cs[..., -1:] - a_cs)
    states = jnp.einsum('bctgn,bgrct,bctgrp->bcgrpn', Bc, decay_states, X)
    states = jnp.concatenate([jnp.zeros_like(states[:, :1]), states], axis=1)
    chunk_decay = jnp.exp(segsum(jnp.pad(a_cs[..., -1], ((0, 0), (0, 0), (0, 0), (1, 0)))))
    new_states = jnp.einsum('bgrzc,bcgrpn->bzgrpn', chunk_decay, states)
    states = new_states[:, :-1]
    y_off = jnp.einsum('bctgn,bcgrpn,bgrct->bctgrp', Cc, states, jnp.exp(a_cs))
    return (y_diag + y_off).reshape(Bsz, L, H, P)

def ssd_branch(z, xbc, dt_raw, conv_w, conv_b, dt_bias, a_log, d_skip, norm_g):
    f32 = jnp.float32
    xbc = jax.nn.silu(centred_dwconv(xbc, conv_w, conv_b)).astype(f32)
    xs, bm, cm = jnp.split(xbc, [SSD_WIDTH, SSD_WIDTH + SSD_GROUPS * SSD_STATE], axis=-1)
    Bsz, L, _ = xs.shape
    xh = xs.reshape(Bsz, L, SSD_HEADS, SSD_HEAD_DIM)
    bm = bm.reshape(Bsz, L, SSD_GROUPS, SSD_STATE)
    cm = cm.reshape(Bsz, L, SSD_GROUPS, SSD_STATE)
    dt = jax.nn.softplus(dt_raw.astype(f32).reshape(Bsz, L, 2, SSD_HEADS) + dt_bias.astype(f32))
    a = -jnp.exp(a_log.astype(f32))
    y_f = ssd_scan(xh, dt[:, :, 0], a[0], bm, cm)
    fl = lambda t: jnp.flip(t, axis=1)
    y_b = fl(ssd_scan(fl(xh), fl(dt[:, :, 1]), a[1], fl(bm), fl(cm)))
    y = y_f + y_b + d_skip.astype(f32)[:, None] * xh
    y = y.reshape(Bsz, L, SSD_WIDTH)
    return rmsnorm(y * jax.nn.silu(z.astype(f32)), norm_g)

def na_branch(qkv, rpb):
    Bsz, L, _ = qkv.shape
    rows = L // GRID_W
    kh = min(NA_KH_MAX, rows)
    q, k, v = jnp.split(qkv.astype(jnp.float32), 3, axis=-1)
    grid = lambda t: t.reshape(Bsz, rows, GRID_W, NA_HEADS, NA_HEAD_DIM)
    q = grid(q) * (NA_HEAD_DIM ** -0.5)
    k = grid(k)
    v = grid(v)
    r_idx = np.arange(rows)
    row_start = np.clip(r_idx - kh // 2, 0, rows - kh)
    c_idx = np.arange(GRID_W)
    col_start = np.clip(c_idx - NA_KW // 2, 0, GRID_W - NA_KW)
    col_keys = col_start[:, None] + np.arange(NA_KW)[None, :]
    row_off = row_start[:, None] + np.arange(kh)[None, :] - r_idx[:, None] + NA_KH_MAX - 1
    col_off = col_keys - c_idx[:, None] + NA_KW - 1
    rpb = rpb.astype(jnp.float32)

    def one_row(args):
        q_r, rs, ro = args
        k_band = lax.dynamic_slice_in_dim(k, rs, kh, axis=1)
        v_band = lax.dynamic_slice_in_dim(v, rs, kh, axis=1)
        k_win = jnp.take(k_band, col_keys, axis=2)
        v_win = jnp.take(v_band, col_keys, axis=2)
        bias = rpb[:, ro[:, None, None], col_off[None, :, :]]
        s = jnp.einsum('bwhd,biwjhd->bhwij', q_r, k_win) + bias.transpose(0, 2, 1, 3)[None]
        p = jax.nn.softmax(s.reshape(Bsz, NA_HEADS, GRID_W, kh * NA_KW), axis=-1).reshape(s.shape)
        return jnp.einsum('bhwij,biwjhd->bwhd', p, v_win)

    out = lax.map(one_row, (q.transpose(1, 0, 2, 3, 4),
                            jnp.asarray(row_start, jnp.int32), jnp.asarray(row_off, jnp.int32)))
    return out.transpose(1, 0, 2, 3, 4).reshape(Bsz, L, NA_WIDTH)

def mlstm_chunkwise(q, k, v, i_pre, f_pre):
    Bsz, H, L, DK = q.shape
    DV = v.shape[-1]
    T = ML_CHUNK
    nc = L // T
    q = q.reshape(Bsz, H, nc, T, DK)
    k = k.reshape(Bsz, H, nc, T, DK)
    v = v.reshape(Bsz, H, nc, T, DV)
    ig = i_pre.reshape(Bsz, H, nc, T)
    b = jnp.cumsum(jax.nn.log_sigmoid(f_pre).reshape(Bsz, H, nc, T), axis=-1)
    g = b[..., -1]
    a = g[..., None] - b + ig
    m_loc = jnp.max(a, axis=-1)
    w = jnp.exp(a - m_loc[..., None])
    S_loc = jnp.einsum('bhct,bhctk,bhctv->bhckv', w, k, v)
    n_loc = jnp.einsum('bhct,bhctk->bhck', w, k)

    def step(carry, inp):
        C, n, m = carry
        S_c, n_c, m_c, g_c = inp
        m_new = jnp.maximum(g_c + m, m_c)
        s_old = jnp.exp(g_c + m - m_new)
        s_new = jnp.exp(m_c - m_new)
        C_new = s_old[..., None, None] * C + s_new[..., None, None] * S_c
        n_new = s_old[..., None] * n + s_new[..., None] * n_c
        return (C_new, n_new, m_new), (C, n, m)

    init = (jnp.zeros((Bsz, H, DK, DV), jnp.float32), jnp.zeros((Bsz, H, DK), jnp.float32),
            jnp.zeros((Bsz, H), jnp.float32))
    mv = lambda t: jnp.moveaxis(t, 2, 0)
    _, (C_prev, n_prev, m_prev) = lax.scan(step, init, (mv(S_loc), mv(n_loc), mv(m_loc), mv(g)))
    C_prev = jnp.moveaxis(C_prev, 0, 2)
    n_prev = jnp.moveaxis(n_prev, 0, 2)
    m_prev = jnp.moveaxis(m_prev, 0, 2)
    mask = jnp.tril(jnp.ones((T, T), dtype=bool))
    Dm = jnp.where(mask, b[..., :, None] - b[..., None, :] + ig[..., None, :], -jnp.inf)
    m_inter = b + m_prev[..., None]
    m_t = jnp.maximum(m_inter, jnp.max(Dm, axis=-1))
    sc = jnp.einsum('bhctk,bhcsk->bhcts', q, k) * jnp.exp(Dm - m_t[..., None])
    inter_scale = jnp.exp(m_inter - m_t)
    num = jnp.einsum('bhcts,bhcsv->bhctv', sc, v) + inter_scale[..., None] * jnp.einsum('bhctk,bhckv->bhctv', q, C_prev)
    den = jnp.sum(sc, axis=-1) + inter_scale * jnp.einsum('bhctk,bhck->bhct', q, n_prev)
    h = num / jnp.maximum(jnp.abs(den), jnp.exp(-m_t))[..., None]
    return h.reshape(Bsz, H, L, DV)

def mlstm_branch(proj, gate_b, head_g):
    Bsz, L, _ = proj.shape
    q, k, v, o, gates = jnp.split(proj.astype(jnp.float32),
                                  [ML_QK, 2 * ML_QK, 2 * ML_QK + ML_WIDTH, 2 * ML_QK + 2 * ML_WIDTH], axis=-1)
    heads = lambda t, d: t.reshape(Bsz, L, ML_HEADS, d).transpose(0, 2, 1, 3)
    q = heads(q, ML_DK) * (ML_DK ** -0.5)
    k = heads(k, ML_DK)
    v = heads(v, ML_DV)
    gates = (gates.reshape(Bsz, L, 4, ML_HEADS) + gate_b.astype(jnp.float32)).transpose(0, 2, 3, 1)
    h_f = mlstm_chunkwise(q, k, v, gates[:, 0], gates[:, 1])
    fl = lambda t: jnp.flip(t, axis=2)
    h_b = fl(mlstm_chunkwise(fl(q), fl(k), fl(v), fl(gates[:, 2]), fl(gates[:, 3])))
    h = (h_f + h_b).transpose(0, 2, 1, 3)
    h = rmsnorm(h, head_g.reshape(ML_HEADS, ML_DV))
    return jax.nn.sigmoid(o) * h.reshape(Bsz, L, ML_WIDTH)

def ssd_na_mixer(h, w_in, conv_w, conv_b, dt_bias, a_log, d_skip, ssd_norm, rpb, w_out):
    proj = h @ w_in
    s1 = SSD_WIDTH
    s2 = s1 + SSD_CONV_CH
    s3 = s2 + 2 * SSD_HEADS
    z, xbc, dt_raw, qkv = jnp.split(proj, [s1, s2, s3], axis=-1)
    y_ssd = ssd_branch(z, xbc, dt_raw, conv_w, conv_b, dt_bias, a_log, d_skip, ssd_norm)
    y_na = na_branch(qkv, rpb)
    y = jnp.concatenate([y_ssd.astype(jnp.float32), y_na], axis=-1)
    return y.astype(h.dtype) @ w_out

def mlstm_mixer(h, w_in, gate_b, head_g, w_out):
    y = mlstm_branch(h @ w_in, gate_b, head_g)
    return y.astype(h.dtype) @ w_out

def first_inputs(seed: int = 0) -> dict:
    key = jax.random.key(seed)
    ks = jax.random.split(key, 20)
    nrm = lambda k, shape, s: jax.random.normal(k, shape, jnp.float32) * s
    x = nrm(ks[0], (BATCH, SEQ, D_MODEL), 1.0)
    c = nrm(ks[1], (BATCH, D_MODEL), 1.0)
    ada_w = nrm(ks[2], (DEPTH, D_MODEL, 6 * D_MODEL), 0.5 * D_MODEL ** -0.5)
    ada_b = nrm(ks[3], (DEPTH, 6 * D_MODEL), 0.02)
    norm_g = 1.0 + nrm(ks[4], (DEPTH, 4, D_MODEL), 0.02)
    mlp_w1 = nrm(ks[5], (DEPTH, D_MODEL, D_FF), D_MODEL ** -0.5)
    mlp_w2 = nrm(ks[6], (DEPTH, D_FF, D_MODEL), D_FF ** -0.5)
    ab_w_in = nrm(ks[7], (N_EVEN, D_MODEL, AB_IN), D_MODEL ** -0.5)
    ab_conv_w = nrm(ks[8], (N_EVEN, SSD_CONV, SSD_CONV_CH), SSD_CONV ** -0.5)
    ab_conv_b = nrm(ks[9], (N_EVEN, SSD_CONV_CH), 0.02)
    dt0 = jnp.exp(jax.random.uniform(ks[10], (N_EVEN, 2, SSD_HEADS), jnp.float32,
                                     minval=math.log(1e-3), maxval=math.log(1e-1)))
    ab_dt_bias = dt0 + jnp.log(-jnp.expm1(-dt0))
    ab_a_log = jnp.log(jax.random.uniform(ks[11], (N_EVEN, 2, SSD_HEADS), jnp.float32, minval=1.0, maxval=16.0))
    ab_d_skip = 1.0 + nrm(ks[12], (N_EVEN, SSD_HEADS), 0.02)
    ab_ssd_norm = 1.0 + nrm(ks[13], (N_EVEN, SSD_WIDTH), 0.02)
    ab_rpb = nrm(ks[14], (N_EVEN, NA_HEADS, 2 * NA_KH_MAX - 1, 2 * NA_KW - 1), 0.1)
    ab_w_out = nrm(ks[15], (N_EVEN, AB_MIX, D_MODEL), AB_MIX ** -0.5)
    ml_w_in = nrm(ks[16], (N_ODD, D_MODEL, ML_IN), D_MODEL ** -0.5)
    gate_base = jnp.array([0.0, 4.0, 0.0, 4.0], jnp.float32)[None, :, None]
    ml_gate_b = gate_base + nrm(ks[17], (N_ODD, 4, ML_HEADS), 0.1)
    ml_head_norm = 1.0 + nrm(ks[18], (N_ODD, ML_WIDTH), 0.02)
    ml_w_out = nrm(ks[19], (N_ODD, ML_WIDTH, D_MODEL), ML_WIDTH ** -0.5)
    return {"x": x, "c": c, "ada_w": ada_w, "ada_b": ada_b, "norm_g": norm_g,
            "mlp_w1": mlp_w1, "mlp_w2": mlp_w2,
            "ab_w_in": ab_w_in, "ab_conv_w": ab_conv_w, "ab_conv_b": ab_conv_b,
            "ab_dt_bias": ab_dt_bias, "ab_a_log": ab_a_log, "ab_d_skip": ab_d_skip,
            "ab_ssd_norm": ab_ssd_norm, "ab_rpb": ab_rpb, "ab_w_out": ab_w_out,
            "ml_w_in": ml_w_in, "ml_gate_b": ml_gate_b, "ml_head_norm": ml_head_norm, "ml_w_out": ml_w_out}

def first_block(x, c, ada_w, ada_b, norm_g, mlp_w1, mlp_w2,
              ab_w_in, ab_conv_w, ab_conv_b, ab_dt_bias, ab_a_log, ab_d_skip, ab_ssd_norm, ab_rpb, ab_w_out,
              ml_w_in, ml_gate_b, ml_head_norm, ml_w_out):
    cond = jax.nn.silu(c)
    for layer in range(DEPTH):
        mod = cond @ ada_w[layer] + ada_b[layer]
        sh1, sc1, g1, sh2, sc2, g2 = jnp.split(mod, 6, axis=-1)
        h = modulate(rmsnorm(x, norm_g[layer, 0]), sh1, sc1)
        if layer % 2 == 0:
            j = layer // 2
            mixed = ssd_na_mixer(h, ab_w_in[j], ab_conv_w[j], ab_conv_b[j], ab_dt_bias[j], ab_a_log[j],
                                 ab_d_skip[j], ab_ssd_norm[j], ab_rpb[j], ab_w_out[j])
        else:
            j = layer // 2
            mixed = mlstm_mixer(h, ml_w_in[j], ml_gate_b[j], ml_head_norm[j], ml_w_out[j])
        x = x + g1[:, None, :] * rmsnorm(mixed, norm_g[layer, 1])
        h = modulate(rmsnorm(x, norm_g[layer, 2]), sh2, sc2)
        u = jnp.square(jax.nn.relu(h @ mlp_w1[layer])) @ mlp_w2[layer]
        x = x + g2[:, None, :] * rmsnorm(u, norm_g[layer, 3])
    return x


_first_inputs = first_inputs


def first_inputs(seed=0):
    import zlib

    import numpy as np

    out = dict(_first_inputs(seed))
    spreads = {}
    factors = {'ab_conv_b': 5.268,
     'ab_d_skip': 8.0,
     'ab_ssd_norm': 7.986,
     'ab_rpb': 8.0,
     'ml_head_norm': 8.0}
    for name, (base, spread) in spreads.items():
        noise = np.random.default_rng([zlib.crc32(name.encode()), seed]).standard_normal(out[name].shape)
        drawn = base * np.exp(spread * noise) if base else spread * noise
        out[name] = __import__('jax').numpy.asarray(drawn.astype(out[name].dtype))
    for name, factor in factors.items():
        out[name] = (out[name] * factor).astype(out[name].dtype)
    return out


_narrow_inputs = first_inputs


def first_inputs(seed=0):

    out = dict(_narrow_inputs(seed))
    wider = {'ab_d_skip': 11.51, 'ab_ssd_norm': 8.58, 'ab_rpb': 7.96, 'ml_head_norm': 11.4}
    for name, times in wider.items():
        mean = out[name].mean()
        out[name] = (mean + times * (out[name] - mean)).astype(out[name].dtype)
    return out


MEM_LEN = 256
D_FF_2 = 2816
FFN_RES = 0.5
EPS = 1e-6
MIX_W = D_MODEL
CONV_W = D_MODEL // 4
CONV_LEN = 3
HG_HEAD_DIM = 64
HG_W = 3 * D_MODEL // 8
HG_HEADS = HG_W // HG_HEAD_DIM
HG_EXP_CLIP = 80.0
RW_HEAD_DIM = 64
RW_W = MIX_W - CONV_W - HG_W
RW_HEADS = RW_W // RW_HEAD_DIM
RW_DECAY_RANK = 64
RW_A_RANK = 64
RW_G_RANK = 128
RW_PROJ = 3 * RW_W + RW_DECAY_RANK + RW_A_RANK + RW_G_RANK
RW_SPLITS = (RW_W, 2 * RW_W, 3 * RW_W, 3 * RW_W + RW_DECAY_RANK, 3 * RW_W + RW_DECAY_RANK + RW_A_RANK)
RW_DECAY_SCALE = 0.606531
RW_GN_EPS = 64e-5
CONV_PROJ = 3 * CONV_W
HG_PROJ = 4 * HG_W
IN_W = CONV_PROJ + HG_PROJ + RW_PROJ
CHUNK = 64
XA_HEADS = 4
XA_HEAD_DIM = D_MODEL // XA_HEADS


def rmsnorm_2(x, g):
    xf = x.astype(jnp.float32)
    xf = xf * lax.rsqrt(jnp.mean(xf * xf, axis=-1, keepdims=True) + EPS)
    return (xf * g.astype(jnp.float32)).astype(x.dtype)

def swiglu_ffn(x, w_in, w_out):
    gate, up = jnp.split(x @ w_in, 2, axis=-1)
    return (jax.nn.silu(gate) * up) @ w_out

def short_conv_mixer(p, conv_w, conv_b):
    b_gate, c_gate, x_in = jnp.split(p, 3, axis=-1)
    z = c_gate * x_in
    zc = lax.conv_general_dilated(
        z, conv_w[:, None, :], window_strides=(1,), padding=[(CONV_LEN - 1, 0)],
        dimension_numbers=('NWC', 'WIO', 'NWC'), feature_group_count=CONV_W)
    return b_gate * (zc + conv_b)

def hgrn2_mixer(p, lb, norm_g):
    bsz, seqlen, _ = p.shape
    n_chunks = seqlen // CHUNK
    f32 = jnp.float32
    q, f_logit, i_in, g = jnp.split(p.astype(f32), 4, axis=-1)
    log_f = jax.nn.log_sigmoid(f_logit) + jnp.log1p(lb * jnp.exp(jnp.minimum(-f_logit, HG_EXP_CLIP)))
    k = (1.0 - lb) * jax.nn.sigmoid(-f_logit)
    q = jax.nn.silu(q)

    def to_chunks(t):
        return t.reshape(bsz, n_chunks, CHUNK, HG_HEADS, -1).transpose(1, 0, 3, 2, 4)

    causal = jnp.tril(jnp.ones((CHUNK, CHUNK), dtype=bool))[:, :, None]

    def chunk_step(state, inp):
        qc, kc, vc, lfc = inp
        b = jnp.cumsum(lfc, axis=2)
        o_inter = jnp.einsum('bhtd,bhde->bhte', qc * jnp.exp(b), state)
        diff = b[:, :, :, None, :] - b[:, :, None, :, :]
        dec = jnp.where(causal, jnp.exp(jnp.minimum(diff, 0.0)), 0.0)
        att = jnp.einsum('bhtd,bhsd,bhtsd->bhts', qc, kc, dec)
        o = o_inter + jnp.einsum('bhts,bhse->bhte', att, vc)
        b_last = b[:, :, -1:, :]
        state = (jnp.exp(b_last[:, :, 0, :])[..., None] * state
                 + jnp.einsum('bhsd,bhse->bhde', kc * jnp.exp(b_last - b), vc))
        return state, o

    state0 = jnp.zeros((bsz, HG_HEADS, HG_HEAD_DIM, HG_HEAD_DIM), f32)
    _, o = lax.scan(chunk_step, state0,
                    (to_chunks(q), to_chunks(k), to_chunks(i_in), to_chunks(log_f)))
    o = o.transpose(1, 0, 3, 2, 4).reshape(bsz, seqlen, HG_HEADS, HG_HEAD_DIM)
    o = o * lax.rsqrt(jnp.mean(o * o, axis=-1, keepdims=True) + EPS)
    o = o.reshape(bsz, seqlen, HG_W) * norm_g.astype(f32) * jax.nn.silu(g)
    return o.astype(p.dtype)

def rwkv7_mixer(p, mu, w0, w2, a0, a2, g2, k_k, k_a, r_k, ln_w, ln_b):
    bsz, seqlen, _ = p.shape
    f32 = jnp.float32
    cast = lambda t: t.astype(f32)
    pf = cast(p)
    p_prev = jnp.pad(pf, ((0, 0), (1, 0), (0, 0)))[:, :-1]
    pf = pf + (p_prev - pf) * cast(mu)
    r, k, v, wd, ad, gd = jnp.split(pf, RW_SPLITS, axis=-1)
    log_w = -RW_DECAY_SCALE * jax.nn.sigmoid(cast(w0) + jnp.tanh(wd) @ cast(w2))
    a = jax.nn.sigmoid(cast(a0) + ad @ cast(a2))
    g = jax.nn.sigmoid(gd) @ cast(g2)
    heads = lambda t: t.reshape(bsz, seqlen, RW_HEADS, RW_HEAD_DIM)
    kk = heads(k * cast(k_k))
    kk = kk / jnp.maximum(jnp.sqrt(jnp.sum(kk * kk, axis=-1, keepdims=True)), 1e-12)
    k = k * (1.0 + (a - 1.0) * cast(k_a))
    rh, kh, vh = heads(r), heads(k), heads(v)
    a_vec = -kk
    b_vec = kk * heads(a)
    tm = lambda t: jnp.swapaxes(t, 0, 1)

    def step(state, inp):
        r_t, w_t, k_t, v_t, a_t, b_t = inp
        sa = jnp.einsum('bhij,bhj->bhi', state, a_t)
        state = (state * w_t[:, :, None, :] + sa[..., None] * b_t[:, :, None, :]
                 + v_t[..., None] * k_t[:, :, None, :])
        return state, jnp.einsum('bhij,bhj->bhi', state, r_t)

    state0 = jnp.zeros((bsz, RW_HEADS, RW_HEAD_DIM, RW_HEAD_DIM), f32)
    _, y = lax.scan(step, state0, (tm(rh), tm(heads(jnp.exp(log_w))), tm(kh), tm(vh), tm(a_vec), tm(b_vec)))
    y = jnp.swapaxes(y, 0, 1)
    mean = jnp.mean(y, axis=-1, keepdims=True)
    var = jnp.mean(jnp.square(y - mean), axis=-1, keepdims=True)
    y = ((y - mean) * lax.rsqrt(var + RW_GN_EPS)).reshape(bsz, seqlen, RW_W) * cast(ln_w) + cast(ln_b)
    bonus = jnp.sum(rh * kh * cast(r_k), axis=-1, keepdims=True) * vh
    out = (y + bonus.reshape(bsz, seqlen, RW_W)) * g
    return out.astype(p.dtype)

def memory_cross_attention(h_n, mem_n, wq, wkv, wo):
    bsz, seqlen, _ = h_n.shape
    q = (h_n @ wq).reshape(bsz, seqlen, XA_HEADS, XA_HEAD_DIM)
    mk, mv = jnp.split(mem_n @ wkv, 2, axis=-1)
    mk = mk.reshape(bsz, -1, XA_HEADS, XA_HEAD_DIM)
    mv = mv.reshape(bsz, -1, XA_HEADS, XA_HEAD_DIM)
    s = jnp.einsum('bshd,bmhd->bhsm', q, mk).astype(jnp.float32) * (XA_HEAD_DIM ** -0.5)
    pr = jax.nn.softmax(s, axis=-1).astype(mv.dtype)
    o = jnp.einsum('bhsm,bmhd->bshd', pr, mv).reshape(bsz, seqlen, D_MODEL)
    return o @ wo

def second_inputs(seed: int = 0) -> dict:
    key = jax.random.key(seed)
    ks = iter(jax.random.split(key, 40))
    nrm = lambda shape, scale: jax.random.normal(next(ks), shape, jnp.float32) * scale
    gain = lambda shape: 1.0 + nrm(shape, 0.02)
    L, D = DEPTH, D_MODEL
    return {
        'x': nrm((BATCH, SEQ, D), 1.0),
        'mem': nrm((BATCH, MEM_LEN, D), 1.0),
        'ffn1_norm': gain((L, D)),
        'ffn1_w_in': nrm((L, D, 2 * D_FF_2), D ** -0.5),
        'ffn1_w_out': nrm((L, D_FF_2, D), D_FF_2 ** -0.5),
        'mix_norm': gain((L, D)),
        'w_mix_in': nrm((L, D, IN_W), D ** -0.5),
        'w_mix_out': nrm((L, MIX_W, D), MIX_W ** -0.5),
        'conv_w': nrm((L, CONV_LEN, CONV_W), CONV_LEN ** -0.5),
        'conv_b': nrm((L, CONV_W), 0.02),
        'hgrn_lb_logits': nrm((L, HG_W), 0.1),
        'hgrn_norm': gain((L, HG_W)),
        'rwkv_mu': jax.random.uniform(next(ks), (L, RW_PROJ), jnp.float32),
        'rwkv_w0': nrm((L, RW_W), 0.5),
        'rwkv_w2': nrm((L, RW_DECAY_RANK, RW_W), RW_DECAY_RANK ** -0.5),
        'rwkv_a0': nrm((L, RW_W), 0.1),
        'rwkv_a2': nrm((L, RW_A_RANK, RW_W), RW_A_RANK ** -0.5),
        'rwkv_g2': nrm((L, RW_G_RANK, RW_W), RW_G_RANK ** -0.5),
        'rwkv_k_k': 0.85 + nrm((L, RW_W), 0.05),
        'rwkv_k_a': 1.0 + nrm((L, RW_W), 0.05),
        'rwkv_r_k': nrm((L, RW_HEADS, RW_HEAD_DIM), 0.1),
        'rwkv_ln_w': gain((L, RW_W)),
        'rwkv_ln_b': nrm((L, RW_W), 0.02),
        'xattn_norm': gain((L, D)),
        'mem_norm': gain((L, D)),
        'xattn_wq': nrm((L, D, D), D ** -0.5),
        'xattn_wkv': nrm((L, D, 2 * D), D ** -0.5),
        'xattn_wo': nrm((L, D, D), D ** -0.5),
        'ffn2_norm': gain((L, D)),
        'ffn2_w_in': nrm((L, D, 2 * D_FF_2), D ** -0.5),
        'ffn2_w_out': nrm((L, D_FF_2, D), D_FF_2 ** -0.5),
        'final_norm': gain((D,)),
    }

def second_block(x, mem, ffn1_norm, ffn1_w_in, ffn1_w_out, mix_norm, w_mix_in, w_mix_out,
              conv_w, conv_b, hgrn_lb_logits, hgrn_norm, rwkv_mu, rwkv_w0, rwkv_w2, rwkv_a0,
              rwkv_a2, rwkv_g2, rwkv_k_k, rwkv_k_a, rwkv_r_k, rwkv_ln_w, rwkv_ln_b,
              xattn_norm, mem_norm, xattn_wq, xattn_wkv, xattn_wo,
              ffn2_norm, ffn2_w_in, ffn2_w_out, final_norm):
    lb_sm = jax.nn.softmax(hgrn_lb_logits.astype(jnp.float32), axis=0)
    lb_all = jnp.maximum(jnp.cumsum(lb_sm, axis=0) - lb_sm[0], 0.0)
    h = x
    for l in range(DEPTH):
        h = h + FFN_RES * swiglu_ffn(rmsnorm_2(h, ffn1_norm[l]), ffn1_w_in[l], ffn1_w_out[l])
        u = rmsnorm_2(h, mix_norm[l])
        p = u @ w_mix_in[l]
        p_conv, p_hg, p_rw = jnp.split(p, (CONV_PROJ, CONV_PROJ + HG_PROJ), axis=-1)
        y = jnp.concatenate([
            short_conv_mixer(p_conv, conv_w[l], conv_b[l]),
            hgrn2_mixer(p_hg, lb_all[l], hgrn_norm[l]),
            rwkv7_mixer(p_rw, rwkv_mu[l], rwkv_w0[l], rwkv_w2[l], rwkv_a0[l], rwkv_a2[l],
                        rwkv_g2[l], rwkv_k_k[l], rwkv_k_a[l], rwkv_r_k[l], rwkv_ln_w[l], rwkv_ln_b[l]),
        ], axis=-1)
        h = h + y @ w_mix_out[l]
        h = h + memory_cross_attention(rmsnorm_2(h, xattn_norm[l]), rmsnorm_2(mem, mem_norm[l]),
                                       xattn_wq[l], xattn_wkv[l], xattn_wo[l])
        h = h + FFN_RES * swiglu_ffn(rmsnorm_2(h, ffn2_norm[l]), ffn2_w_in[l], ffn2_w_out[l])
    return rmsnorm_2(h, final_norm)


def setup_inputs(seed=0):
    out = dict(first_inputs(seed))
    for name, value in second_inputs(seed + 1).items():
        if name != "x":
            out[name + "_2"] = value
    return out


def reference(
    x, c, ada_w, ada_b, norm_g, mlp_w1, mlp_w2, ab_w_in, ab_conv_w, ab_conv_b, ab_dt_bias,
    ab_a_log, ab_d_skip, ab_ssd_norm, ab_rpb, ab_w_out, ml_w_in, ml_gate_b, ml_head_norm,
    ml_w_out, mem_2, ffn1_norm_2, ffn1_w_in_2, ffn1_w_out_2, mix_norm_2, w_mix_in_2,
    w_mix_out_2, conv_w_2, conv_b_2, hgrn_lb_logits_2, hgrn_norm_2, rwkv_mu_2, rwkv_w0_2,
    rwkv_w2_2, rwkv_a0_2, rwkv_a2_2, rwkv_g2_2, rwkv_k_k_2, rwkv_k_a_2, rwkv_r_k_2, rwkv_ln_w_2,
    rwkv_ln_b_2, xattn_norm_2, mem_norm_2, xattn_wq_2, xattn_wkv_2, xattn_wo_2, ffn2_norm_2,
    ffn2_w_in_2, ffn2_w_out_2, final_norm_2,
):
    x = first_block(
        x, c, ada_w, ada_b, norm_g, mlp_w1, mlp_w2, ab_w_in, ab_conv_w, ab_conv_b, ab_dt_bias,
        ab_a_log, ab_d_skip, ab_ssd_norm, ab_rpb, ab_w_out, ml_w_in, ml_gate_b, ml_head_norm,
        ml_w_out,
    )
    return second_block(
        x, mem_2, ffn1_norm_2, ffn1_w_in_2, ffn1_w_out_2, mix_norm_2, w_mix_in_2, w_mix_out_2,
        conv_w_2, conv_b_2, hgrn_lb_logits_2, hgrn_norm_2, rwkv_mu_2, rwkv_w0_2, rwkv_w2_2,
        rwkv_a0_2, rwkv_a2_2, rwkv_g2_2, rwkv_k_k_2, rwkv_k_a_2, rwkv_r_k_2, rwkv_ln_w_2,
        rwkv_ln_b_2, xattn_norm_2, mem_norm_2, xattn_wq_2, xattn_wkv_2, xattn_wo_2, ffn2_norm_2,
        ffn2_w_in_2, ffn2_w_out_2, final_norm_2,
    )


_drawn_inputs = setup_inputs


def setup_inputs(seed=0):
    import zlib

    import numpy as np

    out = dict(_drawn_inputs(seed))
    spreads = {}
    factors = {'ffn1_norm_2': 4.512,
     'conv_b_2': 5.649,
     'hgrn_lb_logits_2': 8.0,
     'hgrn_norm_2': 6.655,
     'rwkv_a0_2': 3.425,
     'rwkv_k_k_2': 8.0,
     'rwkv_ln_w_2': 8.0,
     'rwkv_ln_b_2': 8.0,
     'xattn_norm_2': 8.0,
     'mem_norm_2': 8.0,
     'ffn2_norm_2': 6.203,
     'final_norm_2': 2.806}
    for name, (base, spread) in spreads.items():
        noise = np.random.default_rng([zlib.crc32(name.encode()), seed]).standard_normal(out[name].shape)
        drawn = base * np.exp(spread * noise) if base else spread * noise
        out[name] = jnp.asarray(drawn.astype(out[name].dtype))
    for name, factor in factors.items():
        out[name] = (out[name] * factor).astype(out[name].dtype)
    return out
```

```python
import concourse.bass as bass
from concourse import mybir

F32 = mybir.dt.float32
I32 = mybir.dt.int32
ALU = mybir.AluOpType
ACT = mybir.ActivationFunctionType
AX = mybir.AxisListType

P = 128
L = 256
TB = L // P
D = 1024
DB = D // P
FF = 4 * D
NEG = -1.0e30
EPS = 1e-6
R = 4
SLOT = 4096

SSD_H, SSD_P = 16, 64
CONV_B = 12
NA_H, NA_D, GW, KH = 16, 64, 64, 4
ML_H, ML_DV = 8, 256

ADA_T = 6 * D // 512
POS_ADA = [0, 24]
POS_ZX = 12
POS_DT = POS_ZX + 5
POS_QK = POS_DT + 1
POS_V = POS_QK + 4
POS_AOUT = 36
POS_MLP = [40, 73]
POS_MQK = 56
POS_MG = POS_MQK + 4
POS_MVO = POS_MG + 1
POS_MOUT = POS_MVO + 8
POS_C = 89
C_TILES = 52

EV_ZX, EV_DT, EV_QK, EV_V = 0, 5, 6, 10
EV_MLP = [12, 33]
EV_MQK = 20
EV_MG = 24
EV_MVO = 25
EV_C = 41

O_F1, O_F1O, O_MIX, O_MO, O_K, O_V, O_Q, O_WO, O_F2, O_F2O = 0, 11, 17, 25, 27, 29, 31, 33, 35, 46
E_F1, E_MIX, E_K, E_V, E_Q, E_F2, C_EVS = 0, 11, 19, 21, 23, 25, 36
FB = 22
PACK = {}
for _name, _n in (("ffn1_norm", 8), ("mix_norm", 8), ("xattn_norm", 8), ("mem_norm", 8), ("ffn2_norm", 8),
                  ("conv_w", 6), ("conv_b", 2), ("hgrn_norm", 3), ("rwkv_mu", 11), ("rwkv_w0", 3), ("rwkv_a0", 3),
                  ("rwkv_k_k", 3), ("rwkv_k_a", 3), ("rwkv_r_k", 3), ("rwkv_ln_w", 3), ("rwkv_ln_b", 3)):
    PACK[_name] = (sum(n for _, n in PACK.values()), _n)
PACK_LB = 83
PACK_N = 89
LEVELS = (128, 64, 32, 16, 8, 4, 2, 1)
RW_C = 0.606531
HP = 3

PE_MARKS = ["tokens"] + [f"level{m}" for m in LEVELS] + \
    ["level0", "hg_o", "hg_ss", "low_rank", "tokens2", "kk_ss", "bonus", "bk_tok", "LabT", "Lab", "LakT", "LrbT", "LrkT"] + \
    [f"{k}{p}" for p in range(3) for k in (("N", "NT", "dX", "dXT") if p < 2 else ("N", "dX", "dXT"))] + \
    [f"{k}{p}" for p in range(3) for k in (("W", "mX", "mXT") if p < 2 else ("W", "mXT"))] + \
    ["Z0", "P0", "state", "y0", "Z1", "P1", "y1", "mean", "var"]
ACT_MARKS = ["lb_exp", "hg_exp", "hg_k", "hg_g", "hg_ln", "i_tok", "exp128", "exp64", "att2", "exp32", "exp16", "low_in",
             "exp8", "exp4", "exp2", "exp1", "hg_sq", "hg_rs", "sig", "gate", "v_tok", "kk_sq", "decays", "kk_norm",
             "bk_tok", "LabT", "N0", "N1", "N2", "W0", "W1", "W2", "Z0", "P0", "Z1", "P1", "y", "y_sq", "y_rs"]
DVE_MARKS = ["lb_arg", "hg_in", "hg_mix", "diff128", "diff64", "qk128", "diff32", "qk64", "diff16", "qk32", "shifted",
             "att64", "diff8", "qk16", "att32", "diff4", "qk8", "att16", "diff2", "qk4", "att8", "diff1", "qk2", "att4",
             "qk1", "att2", "att1", "att0", "kk_raw", "o_norm", "y_hg", "centred", "rk", "kk_ss", "operands", "Lab",
             "LakT", "base", "NT0", "XT0", "NT1", "XT1", "XT2", "B0", "B1", "mXT0", "B2", "mXT1", "mXT2", "state",
             "y_centred", "y_rw"]


def loaded(pos):
    gated = lambda q: q >= POS_C and ((q - POS_C) % C_TILES < O_F1O or O_F2 <= (q - POS_C) % C_TILES < O_F2O)
    return 16 * sum(2 if gated(q) else 1 for q in range(pos % R, pos + 1, R))


class Marks:

    def __init__(self, sem, names):
        self.sem, self.names, self.k = sem, list(names), 0

    def at(self, name, l):
        return l * len(self.names) + self.names.index(name) + 1

    def done(self, ins, name):
        assert self.names[self.k % len(self.names)] == name, (self.names[self.k % len(self.names)], name)
        self.k += 1
        ins.then_inc(self.sem, 1)


def build(nc, ctx, a, out):

    def sb(name, shape, dt=F32):
        return nc.alloc_sbuf_tensor(name, shape, dt)

    s = {}

    def sem(*names):
        for n in names:
            s[n] = nc.alloc_semaphore(n)

    sem("const", "packs", "pack_zero", "small", "x_in", "cols_T", "cols", "cond",
        "dve_chain", "act_chain", "pool_chain", "mod_in",
        "ada_ev", "mod_rows", "mod_T", "coef", "gain_in", "gate_bc", "gate_done",
        "x_ready", "ssq", "xn_ready", "xn_T", "hT_act", "hT_dve",
        "ev_act", "ev_dve", "hid",
        "bias_mm", "bias_ev",
        "dt_ln", "U_ready", "U_T", "U_cols", "alog_e",
        "conv", "conv_silu", "z_silu", "X_T", "X_ev", "CB", "ss_arg", "ss_exp", "ss_M", "ss_y", "y_gated",
        "y_sq", "y_sum", "y_rs", "y_ssd",
        "na_s", "na_max", "na_exp", "na_p", "na_pT", "na_pT_ev", "na_o", "na_y",
        "gate_small", "perm", "g_rows", "g_IF", "g_neg", "g_ln", "g_rows2", "g_T", "g_cols", "head_gain",
        "o_sig", "o_gain", "ml_arg", "ml_S", "ml_exp", "ml_M", "ml_num", "ml_h", "ml_sq", "ml_rs", "ml_y", "ml_yT",
        "ml_yT_act", "ml_yT_dve",
        "stored")
    sem("masks", "c_packs", "c_lowrank", "c_cols_T", "c_cols", "mem_in", "mem_ss", "mem_xn", "mem_T", "memT_act",
        "memT_dve", "final_in", "pe_mix", "act_mix", "dve_mix", "pool_mix", "xa_s", "xa_max", "xa_exp", "xa_p", "xa_pT",
        "xa_pT_act", "xa_pT_dve", "xa_o", "xa_y_act", "xa_y_dve", "out_ready")
    w_loaded = [nc.alloc_semaphore(f"w_loaded{i}") for i in range(R)]
    w_used = [nc.alloc_semaphore(f"w_used{i}") for i in range(R)]

    ring = sb("ring", [P, R, SLOT])
    x = sb("x", [P, TB, D])
    hT = sb("hT", [P, DB, L])
    xn = sb("xn", [P, TB, D])
    hid = sb("hid", [P, FF // P, L])
    gains = sb("gains", [P, 2, D])
    modrow = sb("modrow", [P, 3, 512])
    modpack = sb("modpack", [48, P])
    modT = sb("modT", [P, 2, 48])
    coef = sb("coef", [P, 2, 2, DB])
    cols = sb("cols", [P, 248])
    stat = sb("stat", [P, 16])
    ident = sb("ident", [P, P])
    ones = sb("ones", [P, P])
    tri = sb("tri", [P, 2, P])
    eps_c = sb("eps_c", [P, 1])
    dirs = sb("dirs", [32, 2])
    small = sb("small", [P, 16])
    Urow = sb("Urow", [32, L])
    Ucol = sb("Ucol", [P, TB, 2, 32])
    arena = sb("arena", [P, 68, L])
    ps = nc.alloc_psum_tensor("ps", [P, 8, 512], F32)

    def ring_k(slot, n):
        return ring[:, slot, 0:8 * n].rearrange("p (k n) -> p k n", n=n)

    def ring_o(slot, kb):
        return ring[:, slot, 0:kb * D].rearrange("p (k n) -> p k n", n=D)

    pT = arena[:, 0:36, :]
    v_na = arena[:, 36:44, :].rearrange("p b n -> p (b n)").rearrange("p (t n) -> p t n", t=TB)
    bias = arena[:, 44:68, :].rearrange("p b n -> p (b n)").rearrange("p (h x c) -> p h x c", h=NA_H, x=6)
    biasf = arena[:, 44:68, :].rearrange("p b n -> p (b n)").rearrange("p (h n) -> p h n", h=NA_H)
    cvT = hid[:, 16:28, :]
    relu = xn[:, :, :].rearrange("p b (u n) -> p (b u) n", u=2)
    X = xn[:, :, :]
    ssE = arena[:, 8:11, :].rearrange("p b n -> p (b n)").rearrange("p (u n) -> p u n", u=2)
    ssM = arena[:, 11:14, :].rearrange("p b n -> p (b n)").rearrange("p (u n) -> p u n", u=2)
    naS = arena[:, 14:18, :].rearrange("p b n -> p (b n)").rearrange("p (u n) -> p u n", u=2)
    naPT = arena[:, 18:20, :].rearrange("p b n -> p (b n)").rearrange("p (c t) -> p c t", c=2)
    dtw = hid[0:32, 28:32, :]
    naM = sb("naM", [P, 2, 4])
    packs = [hid[0:96, 0, 0:P], hid[0:124, 1, 0:P], hid[0:28, 2, 0:P]]
    rpb_pack = hid[0:96, 3, 0:64]
    rpbT = hid[0:64, 4, 0:96]
    band = hid[0:64, 5, 0:191]
    wmask = hid[:, 6, 0:64]


    C_ADAB, C_NG, C_CW, C_CB, C_SN, C_C = 0, 96, 160, 220, 232, 240
    cT = cols[:, C_C:C_C + 8]

    aa = lambda lo, n: arena[:, lo:lo + n, :]
    flat = lambda v: v.rearrange("p b n -> p (b n)")
    hh = lambda lo, n: hid[:, lo:lo + n, :]
    mk = aa(60, 8).rearrange("p b (u n) -> p (b u) n", u=2)
    LV_MASK = {m: mk[:, i, :] for i, m in enumerate((1, 2, 4, 8, 16, 32, 64))}
    m_bd, m_bdT, m_su, m_iu, blk = (mk[:, 7 + i, :] for i in range(5))
    gn_eps = mk[:, 12, 0:1]
    i32 = lambda v: v.bitcast(I32)
    cpT = aa(0, 29)
    hgA, hgB, hgC, hgD = aa(41, 3), aa(44, 3), aa(47, 3), aa(50, 3)
    hgQ = [aa(29, 3), aa(32, 3)]
    hgK = [aa(35, 3), aa(38, 3)]
    hgAtt = hh(8, 6).rearrange("p b (u n) -> p (b u) n", u=2)
    hgAtt2 = hh(14, 3).rearrange("p b (u n) -> p (b u) n", u=2)
    i_tok = flat(hh(17, 3)).rearrange("p (b n) -> p b n", b=TB)
    hgSG = hh(20, 3)
    lbc = hh(23, 1)[:, 0, 0:24].rearrange("p (u n) -> p u n", n=3)
    rwS = aa(29, 3)
    rwSig, rwA = hh(24, 3), hh(27, 3)
    rwEN, rwKK = hT[:, 0:3, :], hT[:, 3:6, :]
    rwT0, rwT1 = aa(41, 3), aa(44, 3)
    v_tok = flat(aa(53, 3)).rearrange("p (b n) -> p b n", b=TB)
    bk_tok = flat(aa(56, 3)).rearrange("p (b n) -> p b n", b=2)
    rwG, rwBonus = aa(47, 3), aa(50, 3)
    six = lambda v: v.rearrange("p b (u n) -> p (b u) n", u=2)
    LakT, LrbT, LrkT = six(aa(0, 6)), six(aa(6, 6)), six(aa(12, 6))
    at_, bh_, kh_, rt_ = aa(29, 3), aa(32, 3), aa(35, 3), aa(38, 3)
    iX, iXT, iN, iNT, LabT = six(hh(8, 6)), six(hh(14, 6)), six(hh(20, 6)), six(hh(26, 6)), six(aa(41, 6))
    xnf = flat(xn[:, :, :])
    rwP = xnf[:, 0:768].rearrange("p (c n) -> p c n", c=2)
    rwZ = xnf[:, 768:1536].rearrange("p (c n) -> p c n", c=2)
    rwState = xnf[:, 1536:1728].rearrange("p (j n) -> p j n", j=HP)
    rwScal = xnf[:, 1728:1740]
    rwSc, rwEX = (xnf[:, 768 * i:768 * i + 768].rearrange("p (b n) -> p b n", n=L) for i in range(2))
    psf = ps[:, :, :].rearrange("p b n -> p (b n)")
    memT, xqT, xkT = aa(0, 8), aa(8, 8), aa(16, 8)
    xv = flat(aa(24, 8)).rearrange("p (b n) -> p b n", b=TB)
    xP = aa(32, 8).rearrange("p (h b) n -> p h b n", b=TB)
    xPT = aa(40, 8).rearrange("p (h c) n -> p h c n", c=2)
    xM = aa(48, 1)[:, 0, 0:16].rearrange("p (h n) -> p h n", h=4)
    memn = gains
    packC = [modrow[0:PACK_N, i, 0:P] for i in range(2)]
    lowA, lowG = modrow[:, 0, P:512], modrow[:, 1, P:512]
    pc = lambda name, k=0, n=None: cols[:, PACK[name][0] + k:PACK[name][0] + k + (n or 1)]

    marks = {"pe": Marks(s["pe_mix"], PE_MARKS), "act": Marks(s["act_mix"], ACT_MARKS), "dve": Marks(s["dve_mix"], DVE_MARKS)}
    at = {e: m.at for e, m in marks.items()}
    kpn = lambda v: v.rearrange("(k p) n -> p k n", p=P)

    w_in = a["ab_w_in"][0].rearrange("(k p) n -> p k n", p=P)
    ada_w = [a["ada_w"][i].rearrange("(k p) n -> p k n", p=P) for i in range(2)]
    w1 = [a["mlp_w1"][i].rearrange("(k p) n -> p k n", p=P) for i in range(2)]
    w2 = [a["mlp_w2"][i].rearrange("(k p) n -> p k n", p=P) for i in range(2)]
    w_outA = a["ab_w_out"][0].rearrange("(k p) n -> p k n", p=P)
    QKV0 = 2592
    w_ml = a["ml_w_in"][0].rearrange("(k p) n -> p k n", p=P)
    w_outB = a["ml_w_out"][0].rearrange("(k p) n -> p k n", p=P)

    mqT, mkT = arena[:, 0:8, :], arena[:, 8:16, :]
    af = arena[:, :, :].rearrange("p b n -> p (b n)")
    mv = af[:, 4096:4096 + TB * ML_H * 257].rearrange("p (b h n) -> p b h n", b=TB, h=ML_H)
    mo = af[:, 8212:8212 + 4096].rearrange("p (b n) -> p b n", b=TB)
    mh = af[:, 12310:12310 + 4096].rearrange("p (b n) -> p b n", b=TB)
    gw = hid[0:32, 16:22, :]
    hf = hid[:, 22:28, :].rearrange("p b n -> p (b n)")
    mE = hf[:, 0:768].rearrange("p (u n) -> p u n", u=2)
    mM = hf[:, 768:1536].rearrange("p (u n) -> p u n", u=2)
    gate_bias = sb("gate_bias", [32, 1])
    dirsB = sb("dirsB", [16, 2])
    perm = hid[0:32, 29, 0:32].rearrange("p (w n) -> p w n", w=2)
    mtot = sb("mtot", [16, 1])
    nMrow = Urow[0:16, :]
    mcol = hid[:, 30, 0:64].rearrange("p (b w n) -> p b w n", b=TB, w=2)
    mden = hid[:, 30, 80:84].rearrange("p (w n) -> p w n", w=2)
    mstat = hid[:, 30, 64:80].rearrange("p (b n) -> p b n", b=TB)

    def rounds(eng, n, body):
        full = n // R
        if full > 1:
            with eng.Fori(0, full) as i:
                for j in range(R):
                    body(j, i, i * R + j)
        rest = range(full * R if full > 1 else 0, n)
        for t in rest:
            body(t, 0, t)

    ctx.enter_context(nc.allow_non_contiguous_dma(reason="a few hundred parameters of one head or row each"))
    block = ctx.enter_context(nc.Block())

    @block.sync
    def _(sp):
        def load(pos, i, dst, src, skip_wait=False):
            if pos >= R or not isinstance(i, int):
                sp.wait_ge(w_used[pos % R], pos // R + i)
            sp.dma_start(dst, src).then_inc(w_loaded[pos % R], 16)

        def cols_tiles(pos, n, w, c0=0):
            rounds(sp, n, lambda j, i, t: load(pos + j, i, ring_k((pos + j) % R, 512),
                                               w[:, :, bass.ds(t * 512 + c0, 512)]))

        def out_tiles(pos, n, w, kblocks=4):
            rounds(sp, n, lambda j, i, t: load(pos + j, i, ring_o((pos + j) % R, 4),
                                               w[:, bass.ds(t * 4, 4), :]))

        for t in range(R):
            load(t, 0, ring_k(t, 512), ada_w[0][:, :, t * 512:t * 512 + 512])
        cols_tiles(R, ADA_T - R, ada_w[0], R * 512)
        cols_tiles(POS_ZX, 5, w_in)
        load(POS_DT, 0, ring_k(POS_DT % R, 32), w_in[:, :, 2560:2592])
        cols_tiles(POS_QK, 4, w_in, QKV0)
        cols_tiles(POS_V, 2, w_in, QKV0 + 2048)
        cols_tiles(POS_ADA[1], ADA_T, ada_w[1])
        out_tiles(POS_AOUT, 4, w_outA)
        cols_tiles(POS_MLP[0], 8, w1[0])
        out_tiles(POS_MLP[0] + 8, 8, w2[0])
        cols_tiles(POS_MQK, 4, w_ml)
        load(POS_MG, 0, ring_k(POS_MG % R, 32), w_ml[:, :, 6144:6176])
        cols_tiles(POS_MVO, 8, w_ml, 2048)
        out_tiles(POS_MOUT, 4, w_outB)
        cols_tiles(POS_MLP[1], 8, w1[1])
        out_tiles(POS_MLP[1] + 8, 8, w2[1])
        def gated_tiles(pos, w):
            v = w.rearrange("(k p) (g n) -> p k g n", p=P, g=2)

            def one(j, i, t):
                sp.wait_ge(w_used[(pos + j) % R], (pos + j) // R + i)
                for g in range(2):
                    sp.dma_start(ring_k((pos + j) % R, 512)[:, :, 256 * g:256 * g + 256],
                                 v[:, :, g, bass.ds(t * 256, 256)]).then_inc(w_loaded[(pos + j) % R], 16)
            rounds(sp, FB // 2, one)

        def down_tiles(pos, w):
            out_tiles(pos, 5, w)
            load(pos + 5, 0, ring_o((pos + 5) % R, 2), w[:, 20:22, :])

        for l in range(2):
            p0 = POS_C + C_TILES * l
            gated_tiles(p0 + O_F1, a["ffn1_w_in_2"][l])
            down_tiles(p0 + O_F1O, kpn(a["ffn1_w_out_2"][l]))
            cols_tiles(p0 + O_MIX, 7, kpn(a["w_mix_in_2"][l]))
            load(p0 + O_MIX + 7, 0, ring_k((p0 + O_MIX + 7) % R, P), kpn(a["w_mix_in_2"][l])[:, :, 3584:3712])
            out_tiles(p0 + O_MO, 2, kpn(a["w_mix_out_2"][l]))
            cols_tiles(p0 + O_K, 4, kpn(a["xattn_wkv_2"][l]))
            cols_tiles(p0 + O_Q, 2, kpn(a["xattn_wq_2"][l]))
            out_tiles(p0 + O_WO, 2, kpn(a["xattn_wo_2"][l]))
            gated_tiles(p0 + O_F2, a["ffn2_w_in_2"][l])
            down_tiles(p0 + O_F2O, kpn(a["ffn2_w_out_2"][l]))
        sp.wait_ge(s["out_ready"], 1)
        sp.dma_start(out.rearrange("(b p) n -> p b n", p=P), xn[:, :, :]).then_inc(s["stored"], 16)
        sp.wait_ge(s["stored"], 16)

    @block.gpsimd
    def _(pool):
        chain = [0]

        def link(ins):
            chain[0] += 1
            ins.then_inc(s["pool_chain"], 1)
            pool.wait_ge(s["pool_chain"], chain[0])

        def keep(t, pattern, base, mult, fill, cmp=ALU.is_ge):
            link(pool.affine_select(out=t, in_=t, compare_op=cmp, fill=fill, base=base, pattern=pattern,
                                    channel_multiplier=mult))

        pool.memset(rpb_pack, 0.0).then_inc(s["pack_zero"], 1)
        pool.wait_ge(s["pack_zero"], 1)
        link(pool.memset(ident[:, :], 0.0))
        link(pool.memset(ones[:, :], 1.0))
        link(pool.memset(tri[:, :, :], 0.0))
        link(pool.memset(eps_c[:, :], EPS))
        link(pool.memset(dirs[:, 0:1], -1.0))
        link(pool.memset(dirs[:, 1:2], 1.0))
        link(pool.memset(band, 0.0))
        link(pool.memset(wmask, 0.0))
        keep(ident[:, :], [[-1, P]], 0, 1, 1.0, ALU.not_equal)
        keep(tri[:, 0, :], [[1, P]], 0, -1, NEG)
        keep(tri[:, 1, :], [[-1, P]], 0, 1, NEG)
        keep(dirs[:, 0:1], [[0, 1]], -16, 1, 1.0)
        keep(dirs[:, 1:2], [[0, 1]], -16, 1, 0.0)
        link(pool.memset(dirsB[:, 0:1], -1.0))
        link(pool.memset(dirsB[:, 1:2], 1.0))
        keep(dirsB[:, 0:1], [[0, 1]], -8, 1, 1.0)
        keep(dirsB[:, 1:2], [[0, 1]], -8, 1, 0.0)
        for half in range(2):
            keep(band[32 * half:32 * half + 31, :], [[1, 191]], -78 - 64 * half, 1, 1.0, ALU.not_equal)
        for half in range(2):
            v = wmask[64 * half:64 * half + 64, :]
            keep(v[:, 0:48], [[1, 48]], 8, -1, NEG)
            keep(v[:, 16:64], [[-1, 48]], 7 - 16, 1, NEG)
        pool.sem_inc(s["const"], 1)
        for l in range(2):
            pool.wait_ge(s["ada_ev"], ADA_T * (l + 1))
            for c in range(3):
                for q in range(4):
                    pool.dma_start(modpack[16 * c + 4 * q:16 * c + 4 * q + 4, :],
                                   modrow[32 * q:32 * q + 1, c, :].rearrange("o (r n) -> o r n", n=P))\
                        .then_inc(s["mod_rows"], 16)
        pool.wait_ge(s["x_ready"], 2)
        pool.memset(mv[:, :, :, 256:257], 1.0).then_inc(s["g_cols"], 1)
        pool.wait_ge(s["o_sig"], 1)
        pool.wait_ge(s["head_gain"], 16)
        for b in range(TB):
            ins = pool.tensor_tensor(mo[:, b, :], mo[:, b, :], xn[:, :, :].rearrange("p b n -> p (b n)"), ALU.mult)
        ins.then_inc(s["o_gain"], 1)
        pool.wait_ge(s["x_ready"], 3)
        for m, t in LV_MASK.items():
            v = t.rearrange("p (i u r) -> p i u r", u=2, r=m)
            link(pool.memset(t, 0.0))
            link(pool.memset(v[:, :, 1, :], 1.0))
            keep(v[:, :, 1, :], [[-2 * m, 64 // m], [0, m]], 0, 1, 0.0)
            keep(v[:, :, 1, :], [[2 * m, 64 // m], [0, m]], m - 1, -1, 0.0)
        for t in (m_bd, m_bdT, m_su, m_iu, blk):
            link(pool.memset(t, 1.0))
        keep(m_bd, [[1, P]], -1, -1, 0.0)
        keep(m_bd, [[-16, 8], [0, 16]], 0, 1, 0.0)
        keep(m_bdT, [[-1, P]], -1, 1, 0.0)
        keep(m_bdT, [[16, 8], [0, 16]], 15, -1, 0.0)
        keep(m_su, [[1, P]], -1, -1, 0.0)
        keep(m_iu, [[1, P]], 0, -1, 0.0)
        keep(blk[:, 0:64], [[0, 64]], 63, -1, 0.0)
        keep(blk[:, 64:128], [[0, 64]], -64, 1, 0.0)
        link(pool.memset(gn_eps, 64e-5))
        pool.sem_inc(s["masks"], 1)
        for l in range(2):
            pool.wait_ge(s["dve_mix"], at["dve"]("y_hg", l))
            pool.memset(flat(aa(0, 18)), 0.0).then_inc(s["pool_mix"], 1)

    @block.scalar
    def _(act):
        chain = [0]

        def link(ins):
            chain[0] += 1
            ins.then_inc(s["act_chain"], 1)
            act.wait_ge(s["act_chain"], chain[0])

        def rsqrt(dst, src, scale):
            link(act.activation(dst, src, ACT.Ln, bias=eps_c[0:dst.shape[0], :], scale=scale))
            return act.activation(dst, dst, ACT.Exp, scale=-0.5)

        def load_mod_bias(l):
            v = a["ada_b"][l].rearrange("(c q n) -> q c n", c=3, q=4)
            for q in range(4):
                act.dma_start(modrow[32 * q:32 * q + 1, :, :], v[q:q + 1]).then_inc(s["mod_in"], 16)

        act.dma_start(packs[0], a["ada_b"].rearrange("l (r n) -> (l r) n", n=P)).then_inc(s["packs"], 16)
        act.dma_start(packs[1][0:64], a["norm_g"].rearrange("l s (r n) -> (l s r) n", n=P)).then_inc(s["packs"], 16)
        act.dma_start(packs[1][64:124], a["ab_conv_w"][0].rearrange("t (r n) -> (t r) n", n=P)).then_inc(s["packs"], 16)
        act.dma_start(packs[2][0:12], a["ab_conv_b"][0].rearrange("(r n) -> r n", n=P)).then_inc(s["packs"], 16)
        act.dma_start(packs[2][12:20], a["ab_ssd_norm"][0].rearrange("(r n) -> r n", n=P)).then_inc(s["packs"], 16)
        act.dma_start(packs[2][20:28], a["c"][0].rearrange("(r n) -> r n", n=P)).then_inc(s["packs"], 16)
        act.wait_ge(s["pack_zero"], 1)
        rpb = a["ab_rpb"][0]
        for h in range(NA_H):
            act.dma_start(rpb_pack[6 * h:6 * h + 6, 0:31], rpb[h, 5:11, :]).then_inc(s["packs"], 16)
            act.dma_start(rpb_pack[6 * h:6 * h + 6, 32:63], rpb[h, 4:10, :]).then_inc(s["packs"], 16)
        load_mod_bias(0)
        act.dma_start(x[:, :, :], a["x"][0].rearrange("(b p) n -> p b n", p=P)).then_inc(s["x_in"], 16)
        act.dma_start(small[0:32, 0:1], a["ab_dt_bias"].rearrange("o d h -> (d h) o")).then_inc(s["small"], 16)
        act.dma_start(small[0:32, 1:2], a["ab_a_log"].rearrange("o d h -> (d h) o")).then_inc(s["small"], 16)
        for u in range(2):
            act.dma_start(small[64 * u:64 * u + 64, 4:12],
                          a["ab_d_skip"].rearrange("o (j u) -> u o j", u=2)[u].to_broadcast([64, 8]))\
                .then_inc(s["small"], 16)
        for i in range(2):
            act.dma_start(gains[:, i, :], a["norm_g"][0, 1 + 2 * i:2 + 2 * i, :].to_broadcast([P, D]))\
                .then_inc(s["gain_in"], 16)
        act.wait_ge(s["cols"], 1)
        act.activation(cT, cT, ACT.Silu).then_inc(s["cond"], 1)

        def norm_stats(site, l=0):
            if site == 0:
                act.wait_ge(s["x_in"], 16)
            else:
                act.wait_ge(s["x_ready"], site)
            for b in range(TB):
                last = act.activation(xn[:, b, :], x[:, b, :], ACT.Square, accum_out=stat[:, b:b + 1])
            link(last)
            rsqrt(stat[:, 2:4], stat[:, 0:2], 1.0 / D).then_inc(s["ssq"], 1)

        def norm_out(site, A, B, last=False):
            for b in range(2):
                act.wait_ge(s["xn_T"], 4 * site + b + 1)
                for u in range(2):
                    k = 2 * b + u
                    ins = act.activation(hT[:, k, :], ps[:, 4 + b, u * L:(u + 1) * L], ACT.Identity,
                                         scale=A[:, k:k + 1], bias=B[:, k:k + 1] if B is not None else 0.0)
            ins.then_inc(s["hT_act"], 1)

        def tile_out(pos, ev, dst):
            act.wait_ge(w_used[pos % R], pos // R + 1)
            act.activation(dst, ps[:, 2 * (ev % 2), 0:512], ACT.Copy).then_inc(s["ev_act"], 1)

        def chan(t0, t):
            return pT[:, t0 + 4 * t:t0 + 4 * t + 2, :].rearrange("p b n -> p (b n)")

        norm_stats(0)
        act.wait_ge(s["coef"], 1)
        norm_out(0, coef[:, 0, 0, :], modT[:, 0, 0:8])
        for t in range(5):
            tile_out(POS_ZX + t, EV_ZX + t, chan(0, t))
        act.wait_ge(s["small"], 64)
        act.activation(small[0:32, 2:3], small[0:32, 1:2], ACT.Exp).then_inc(s["alog_e"], 1)
        act.wait_ge(w_used[POS_DT % R], POS_DT // R + 1)
        act.activation(dtw[:, 0, :], ps[0:32, 2 * (EV_DT % 2), 0:L], ACT.Identity, bias=small[0:32, 0:1])\
            .then_inc(s["ev_act"], 1)
        act.wait_ge(s["ev_dve"], EV_DT + 1)
        link(act.activation(dtw[:, 1, :], dtw[:, 1, :], ACT.Exp))
        act.activation(dtw[:, 1, :], dtw[:, 1, :], ACT.Ln, bias=1.0).then_inc(s["dt_ln"], 1)
        for t in range(4):
            tile_out(POS_QK + t, EV_QK + t, chan(20, t))
            if t > 0:
                act.wait_ge(s["conv"], t)
                act.activation(cvT[:, 4 * t - 4:4 * t, :], cvT[:, 4 * t - 4:4 * t, :], ACT.Silu)\
                    .then_inc(s["conv_silu"], 1)
        for t in range(2):
            tile_out(POS_V + t, EV_V + t, v_na[:, 0, 512 * t:512 * t + 512])
        act.wait_ge(s["ev_dve"], EV_ZX + 5)
        act.activation(pT[:, 0:8, :], pT[:, 0:8, :], ACT.Silu).then_inc(s["z_silu"], 1)
        for b in range(2):
            act.wait_ge(s["X_T"], b + 1)
            act.activation(X[:, 0, 512 * b:512 * b + 512], ps[:, 2 + b, :], ACT.Copy).then_inc(s["X_ev"], 1)
        act.wait_ge(s["mod_rows"], 192)
        act.wait_ge(s["gate_done"], 1)
        load_mod_bias(1)
        act.wait_ge(s["U_cols"], 1)
        for i in range(2 * SSD_H):
            h, d = i // 2, i % 2
            r = d * 16 + h
            n0 = L if d == 0 else P
            act.wait_ge(s["ss_arg"], i + 1)
            if i >= 2:
                act.wait_ge(s["ss_M"], i - 1)
            act.activation(ssE[:, i % 2, 0:n0], ps[:, i % 2, 0:n0], ACT.Exp, bias=Ucol[:, 0, 0, r:r + 1])
            act.activation(ssE[:, i % 2, n0:384], ps[:, i % 2, n0:384], ACT.Exp, bias=Ucol[:, 1, 0, r:r + 1])\
                .then_inc(s["ss_exp"], 1)
        act.wait_ge(s["y_gated"], 8)
        act.activation(cvT[:, 0:8, :], pT[:, 0:8, :], ACT.Square).then_inc(s["y_sq"], 1)
        act.wait_ge(s["y_sum"], 1)
        rsqrt(cvT[:, 8, :], ps[:, 4, 0:L], 1.0 / D).then_inc(s["y_rs"], 1)

        def na_probs(h):
            act.wait_ge(s["na_max"], h + 1)
            for b in range(TB):
                ins = act.activation(naS[:, h % 2, b * L:(b + 1) * L], naS[:, h % 2, b * L:(b + 1) * L], ACT.Exp,
                                     bias=naM[:, h % 2, b:b + 1], accum_out=naM[:, h % 2, 2 + b:3 + b])
            ins.then_inc(s["na_exp"], 1)

        def na_transposed(h):
            act.wait_ge(s["na_pT"], h + 1)
            if h >= 1:
                act.wait_ge(s["na_o"], h)
            act.activation(naPT[:, :, :], ps[:, 2 + h % 2, :], ACT.Copy).then_inc(s["na_pT_ev"], 1)

        for h in range(NA_H + 1):
            if h < NA_H:
                na_probs(h)
            if h >= 1:
                na_transposed(h - 1)

        def gated_stats(pos):
            act.wait_ge(w_used[pos % R], pos // R + 1)
            for b in range(TB):
                last = act.activation(xn[:, b, :], ps[:, 2 * b:2 * b + 2, :], ACT.Square, accum_out=stat[:, 4 + b:5 + b])
            link(last)
            rsqrt(stat[:, 6:8], stat[:, 4:6], 1.0 / D).then_inc(s["ssq"], 1)

        def mlp_out_act(l):
            def body(j, i, t):
                pos, ev = POS_MLP[l] + j, EV_MLP[l] + j
                act.wait_ge(w_used[pos % R], pos // R + 1 + i)
                act.activation(relu[:, j, :], ps[:, 2 * (ev % 2), :], ACT.Relu).then_inc(s["ev_act"], 1)
            rounds(act, 8, body)

        gated_stats(POS_AOUT + 3)
        norm_stats(1)
        norm_out(1, coef[:, 0, 1, :], modT[:, 0, 24:32])
        mlp_out_act(0)
        gated_stats(POS_MLP[0] + 15)

        act.wait_ge(s["x_ready"], 2)
        for i in range(2):
            act.dma_start(gains[:, i, :], a["norm_g"][1, 1 + 2 * i:2 + 2 * i, :].to_broadcast([P, D]))\
                .then_inc(s["gain_in"], 16)
        act.dma_start(gate_bias[:, :], a["ml_gate_b"].rearrange("o g h -> (g h) o")).then_inc(s["gate_small"], 16)
        norm_stats(2)
        norm_out(2, coef[:, 1, 0, :], modT[:, 1, 0:8])
        act.wait_ge(s["hT_dve"], 3)
        act.dma_start(xn[:, :, :].rearrange("p b n -> p (b n)"), a["ml_head_norm"].to_broadcast([P, 2 * D]))\
            .then_inc(s["head_gain"], 16)
        for t in range(4):
            tile_out(POS_MQK + t, EV_MQK + t, arena[:, 4 * t:4 * t + 2, :].rearrange("p b n -> p (b n)"))
        act.wait_ge(s["gate_small"], 16)
        act.wait_ge(w_used[POS_MG % R], POS_MG // R + 1)
        act.activation(gw[:, 0, :], ps[0:32, 2 * (EV_MG % 2), 0:L], ACT.Identity, bias=gate_bias[:, :])\
            .then_inc(s["ev_act"], 1)
        act.wait_ge(s["g_cols"], 1)
        for t in range(4):
            tile_out(POS_MVO + t, EV_MVO + t, mv[:, 0, 2 * t:2 * t + 2, 0:256])
            if t == 1:
                act.wait_ge(s["g_neg"], 1)
                link(act.activation(gw[0:16, 2, :], gw[0:16, 2, :], ACT.Exp))
                act.activation(gw[0:16, 2, :], gw[0:16, 2, :], ACT.Ln, bias=1.0).then_inc(s["g_ln"], 1)
        for t in range(4):
            tile_out(POS_MVO + 4 + t, EV_MVO + 4 + t, mo[:, 0, 512 * t:512 * t + 512])
        act.wait_ge(s["g_T"], 1)
        v = ps[:, 4, 0:64].rearrange("p (b w r) -> p b w r", b=2, w=2)
        act.activation(mcol[:, :, 0, :], v[:, :, 0, :], ACT.Copy)
        act.activation(mcol[:, :, 1, :], v[:, :, 1, :], ACT.Exp).then_inc(s["g_cols"], 1)
        act.wait_ge(s["ev_dve"], EV_MVO + 8)
        act.wait_ge(s["ev_act"], EV_MVO + 8)
        act.activation(mo[:, :, :], mo[:, :, :], ACT.Sigmoid).then_inc(s["o_sig"], 1)
        act.wait_ge(s["g_cols"], 2)

        def head_squares(h):
            act.wait_ge(s["ml_h"], 2 * h + 2)
            for b in range(TB):
                ins = act.activation(hid[:, 28 + 3 * b, :], mh[:, b, 256 * h:256 * h + 256], ACT.Square, accum_out=mstat[:, b, h:h + 1])
            link(ins)

        for i in range(2 * ML_H):
            h, d = i // 2, i % 2
            r, n0 = d * 8 + h, (L if d == 0 else P)
            act.wait_ge(s["ml_arg"], i + 1)
            if i >= 2:
                act.wait_ge(s["ml_M"], i - 1)
            act.activation(mE[:, i % 2, 0:n0], ps[:, i % 2, 0:n0], ACT.Exp, bias=mcol[:, 0, 0, r:r + 1])
            act.activation(mE[:, i % 2, n0:384], ps[:, i % 2, n0:384], ACT.Exp, bias=mcol[:, 1, 0, r:r + 1])\
                .then_inc(s["ml_exp"], 1)
            if i >= 5 and i % 2 == 1:
                head_squares((i - 5) // 2)
        head_squares(6)
        head_squares(7)
        rsqrt(mstat[:, :, :], mstat[:, :, :], 1.0 / ML_DV).then_inc(s["ml_rs"], 1)
        for g in range(0, 8, 2):
            act.wait_ge(s["ml_yT"], g + 1)
            act.activation(hid[:, 2 * g:2 * g + 2, :], ps[:, g, :], ACT.Copy).then_inc(s["ml_yT_act"], 1)
        gated_stats(POS_MOUT + 3)
        norm_stats(3)
        norm_out(3, coef[:, 1, 1, :], modT[:, 1, 24:32])
        for l in range(2):
            for name, (r, n) in PACK.items():
                v = a[name + "_2"][l]
                v = v.rearrange("t (r n) -> (t r) n", n=P) if name == "conv_w" else \
                    v.rearrange("(r u) n -> r (u n)", u=2) if name == "rwkv_r_k" else v.rearrange("(r n) -> r n", n=P)
                act.dma_start(packC[l][r:r + n], v).then_inc(s["c_packs"], 16)
            act.dma_start(packC[l][PACK_LB:PACK_N], a["hgrn_lb_logits_2"].rearrange("l (r n) -> (l r) n", n=P))\
                .then_inc(s["c_packs"], 16)

        def load_low_rank(l):
            act.dma_start(lowA[0:64], a["rwkv_w2_2"][l]).then_inc(s["c_lowrank"], 16)
            act.dma_start(lowA[64:128], a["rwkv_a2_2"][l]).then_inc(s["c_lowrank"], 16)
            act.dma_start(lowG, a["rwkv_g2_2"][l]).then_inc(s["c_lowrank"], 16)

        load_low_rank(0)
        mlp_out_act(1)
        gated_stats(POS_MLP[1] + 15)

        def gated_out_act(ev0, pos0):
            def body(j, i, t):
                pos, ev = pos0 + j, ev0 + j
                act.wait_ge(w_used[pos % R], pos // R + 1 + i)
                act.activation(relu[:, j % 4, :], ps[:, 2 * (ev % 2), :], ACT.Silu).then_inc(s["ev_act"], 1)
            rounds(act, FB // 2, body)

        def mixer_act(l, p0, e0):
            mark = marks["act"].done
            DV, PV = (lambda n: at["dve"](n, l)), (lambda n: at["pe"](n, l))
            act.wait_ge(s["dve_mix"], DV("lb_arg"))
            mark(act.activation(lbc[:, 1:3, :], lbc[:, 1:3, :], ACT.Exp), "lb_exp")
            for t in range(7):
                tile_out(p0 + O_MIX + t, e0 + E_MIX + t, flat(cpT[:, 4 * t:4 * t + 2, :]))
                if t == 3:
                    act.wait_ge(s["dve_mix"], DV("hg_in"))
                    act.activation(hgB, hgB, ACT.Exp)
                    act.activation(hgD, hgA, ACT.Exp, scale=-1.0)
                    link(act.activation(hgC, hgC, ACT.Exp))
                    mark(act.activation(hgC, hgC, ACT.Ln, bias=1.0), "hg_exp")
                    act.activation(hgK[0], cpT[:, 9:12, :], ACT.Sigmoid, scale=-1.0)
                    mark(act.activation(cpT[:, 6:9, :], cpT[:, 6:9, :], ACT.Silu), "hg_k")
                if t == 4:
                    act.wait_ge(s["ev_act"], e0 + E_MIX + 5)
                    act.wait_ge(s["ev_dve"], e0 + E_MIX + 4)
                    mark(act.activation(hgSG, cpT[:, 15:18, :], ACT.Silu), "hg_g")
                    act.wait_ge(s["dve_mix"], DV("hg_mix"))
                    mark(act.activation(hgB, hgB, ACT.Ln), "hg_ln")
            pos, ev = p0 + O_MIX + 7, e0 + E_MIX + 7
            act.wait_ge(w_used[pos % R], pos // R + 1)
            act.activation(cpT[:, 28, :], ps[:, 2 * (ev % 2), 0:L], ACT.Copy).then_inc(s["ev_act"], 1)
            act.wait_ge(s["pe_mix"], PV("tokens"))
            for b in range(TB):
                ins = act.activation(i_tok[:, b, :], ps[:, 6 + b, 0:384], ACT.Copy)
            mark(ins, "i_tok")
            for n, m in enumerate(LEVELS):
                act.wait_ge(s["dve_mix"], DV(f"diff{m}"))
                mark(act.activation((hgD, hgC)[n % 2], (hgD, hgC)[n % 2], ACT.Exp), f"exp{m}")
                if n == 1:
                    act.wait_ge(s["pe_mix"], PV(f"level{LEVELS[0]}"))
                    mark(act.activation(
                        hgAtt2.rearrange("p (h j) n -> p h (j n)", h=2),
                        ps[:, 0:4, :].rearrange("p (h b) n -> p h b n", b=2)[:, :, 0, 0:384], ACT.Copy), "att2")
                if n == 3:
                    act.wait_ge(s["dve_mix"], DV("shifted"))
                    act.activation(cpT[0:64, 27, :], cpT[0:64, 27, :], ACT.Tanh)
                    mark(act.activation(cpT[:, 28, :], cpT[:, 28, :], ACT.Sigmoid), "low_in")
            act.wait_ge(s["pe_mix"], PV("hg_o"))
            mark(act.activation(flat(hgC), psf[:, 3072:3840], ACT.Square), "hg_sq")
            act.wait_ge(s["pe_mix"], PV("hg_ss"))
            link(act.activation(flat(hgD), psf[:, 0:768], ACT.Ln, bias=eps_c[:, :], scale=1.0 / 64))
            mark(act.activation(flat(hgD), flat(hgD), ACT.Exp, scale=-0.5), "hg_rs")
            act.wait_ge(s["pe_mix"], PV("low_rank"))
            for j in range(HP):
                act.activation(rwSig[:, j, :], psf[:, 1024 + j * L:1024 + (j + 1) * L], ACT.Sigmoid,
                               bias=pc("rwkv_w0", j))
                ins = act.activation(rwA[:, j, :], psf[:, 2048 + j * L:2048 + (j + 1) * L], ACT.Sigmoid,
                                     bias=pc("rwkv_a0", j))
            mark(ins, "sig")
            act.wait_ge(s["dve_mix"], DV("y_hg"))
            act.activation(flat(rwG), psf[:, 2816:3584], ACT.Copy)
            if l == 0:
                load_low_rank(1)
            act.wait_ge(s["pe_mix"], PV("tokens2"))
            mark(act.activation(v_tok[:, 0, :], ps[:, 0, 0:384], ACT.Copy), "gate")
            mark(act.activation(v_tok[:, 1, :], ps[:, 1, 0:384], ACT.Copy), "v_tok")
            act.wait_ge(s["dve_mix"], DV("kk_raw"))
            mark(act.activation(rwT0, rwKK, ACT.Square), "kk_sq")
            act.wait_ge(s["dve_mix"], DV("centred"))
            act.activation(rwEN, rwSc, ACT.Exp, scale=RW_C)
            act.activation(rwScal[:, 0:3], rwS[:, :, 191], ACT.Exp, scale=-RW_C)
            act.activation(rwEX, rwEX, ACT.Exp, scale=-RW_C)
            mark(act.activation(rt_, rwSc, ACT.Exp, scale=-RW_C), "decays")
            act.wait_ge(s["dve_mix"], DV("kk_ss"))
            mark(act.activation(rwT0, rwT0, ACT.Sqrt), "kk_norm")
            act.wait_ge(s["pe_mix"], PV("bk_tok"))
            act.activation(bk_tok[:, 0, :], ps[:, 6, 0:384], ACT.Copy)
            mark(act.activation(bk_tok[:, 1, :], ps[:, 7, 0:384], ACT.Copy), "bk_tok")
            mats = lambda bank: ps[:, bank:bank + 4, 0:384]
            four = lambda v: v.rearrange("p (b u) n -> p b (u n)", b=4)
            act.wait_ge(s["pe_mix"], PV("LabT"))
            mark(act.activation(four(LabT), mats(0), ACT.Copy), "LabT")
            for p in range(3):
                act.wait_ge(s["pe_mix"], PV(f"NT{p}" if p < 2 else "N2"))
                mark(act.activation(four(iN), mats(0), ACT.Copy), f"N{p}")
            for p in range(3):
                act.wait_ge(s["pe_mix"], PV(f"W{p}"))
                mark(act.activation(four(iNT), mats(0), ACT.Copy), f"W{p}")
            for c in range(2):
                act.wait_ge(s["pe_mix"], PV(f"Z{c}"))
                mark(act.activation(rwZ[:, c, :].rearrange("p (j h n) -> p h j n", h=2, n=64),
                                    ps[:, 0:6, 0:192].rearrange("p (h b) (j n) -> p h b j n", b=3, n=64)[:, :, 0],
                                    ACT.Copy), f"Z{c}")
                act.wait_ge(s["pe_mix"], PV(f"P{c}"))
                mark(act.activation(rwP[:, c, :], ps[:, 1, 0:384], ACT.Copy), f"P{c}")
            act.wait_ge(s["pe_mix"], PV("y1"))
            mark(act.activation(flat(at_), psf[:, 3072:3840], ACT.Copy), "y")
            act.wait_ge(s["dve_mix"], DV("y_centred"))
            mark(act.activation(kh_, bh_, ACT.Square), "y_sq")
            act.wait_ge(s["pe_mix"], PV("var"))
            link(act.activation(flat(rt_), psf[:, 1024:1792], ACT.Ln, bias=gn_eps, scale=1.0 / 64))
            mark(act.activation(rt_, rt_, ACT.Exp, scale=-0.5), "y_rs")

        def attention_act(l, p0, e0):
            for b in range(2):
                act.wait_ge(s["mem_T"], 4 * l + b + 1)
                for u in range(2):
                    k = 2 * b + u
                    ins = act.activation(memT[:, k, :], ps[:, 4 + b, u * L:(u + 1) * L], ACT.Copy,
                                         scale=pc("mem_norm", k))
            ins.then_inc(s["memT_act"], 1)
            for t in range(2):
                tile_out(p0 + O_K + t, e0 + E_K + t, flat(xkT[:, 4 * t:4 * t + 2, :]))
            for t in range(2):
                tile_out(p0 + O_V + t, e0 + E_V + t, xv[:, 0, 512 * t:512 * t + 512])
            norm_stats(6 + 4 * l)
            norm_out(6 + 4 * l, pc("xattn_norm", 0, 8), None)
            for t in range(2):
                tile_out(p0 + O_Q + t, e0 + E_Q + t, flat(xqT[:, 4 * t:4 * t + 2, :]))
            for h in range(4):
                act.wait_ge(s["xa_max"], 4 * l + h + 1)
                for b in range(TB):
                    ins = act.activation(xP[:, h, b, :], ps[:, 4 + h, b * L:(b + 1) * L], ACT.Exp, scale=1.0 / 16,
                                         bias=xM[:, h, b:b + 1], accum_out=xM[:, h, 2 + b:3 + b])
                ins.then_inc(s["xa_exp"], 1)
            for h in (0, 2):
                act.wait_ge(s["xa_pT"], 4 * l + h + 1)
                act.activation(flat(xPT[:, h, :, :]), ps[:, h, :], ACT.Copy).then_inc(s["xa_pT_act"], 1)
            for h in (0, 2):
                act.wait_ge(s["xa_o"], 4 * l + h + 1)
                act.activation(flat(hid[:, 2 * h:2 * h + 2, :]), ps[:, 4 + h, :], ACT.Copy).then_inc(s["xa_y_act"], 1)

        act.wait_ge(s["x_ready"], 4)
        act.dma_start(memn[:, :, :], a["mem_2"][0].rearrange("(b p) n -> p b n", p=P)).then_inc(s["mem_in"], 16)
        for l in range(2):
            p0, e0 = POS_C + C_TILES * l, EV_C + C_EVS * l
            norm_stats(4 + 4 * l)
            if l == 0:
                act.wait_ge(s["mem_in"], 16)
                for b in range(TB):
                    ins = act.activation(flat(hid[:, 24 + 4 * b:28 + 4 * b, :]), memn[:, b, :], ACT.Square,
                                         accum_out=stat[:, 8 + b:9 + b])
                link(ins)
                rsqrt(stat[:, 10:12], stat[:, 8:10], 1.0 / D).then_inc(s["mem_ss"], 1)
            act.wait_ge(s["c_cols"], l + 1)
            norm_out(4 + 4 * l, pc("ffn1_norm", 0, 8), None)
            gated_out_act(e0 + E_F1, p0 + O_F1)
            norm_stats(5 + 4 * l)
            norm_out(5 + 4 * l, pc("mix_norm", 0, 8), None)
            mixer_act(l, p0, e0)
            attention_act(l, p0, e0)
            norm_stats(7 + 4 * l)
            norm_out(7 + 4 * l, pc("ffn2_norm", 0, 8), None)
            gated_out_act(e0 + E_F2, p0 + O_F2)
        act.wait_ge(s["memT_act"], 2)
        act.wait_ge(s["memT_dve"], 2)
        act.dma_start(gains[:, 0, :], a["final_norm_2"].unsqueeze(0).to_broadcast([P, D])).then_inc(s["final_in"], 16)
        norm_stats(12)

    @block.tensor
    def _(pe):
        def weights(pos, i=0):
            pe.wait_ge(w_loaded[pos % R], loaded(pos) + i * (loaded(pos) - loaded(pos - R)) if pos >= R else 16)

        def banks_free(ev, i=0, per=0):
            if ev >= 2 or not isinstance(i, int):
                pe.wait_ge(s["ev_act"], ev - 1 + i * R)
                pe.wait_ge(s["ev_dve"], ev - 1 + i * R)

        def channel_tile(pos, ev, i=0, src=hT):
            weights(pos, i)
            banks_free(ev, i)
            w = ring_k(pos % R, 512)
            for m in range(4):
                o = ps[:, 2 * (ev % 2) + m // 2, (m % 2) * L:(m % 2 + 1) * L]
                for k in range(DB):
                    last = pe.matmul(o, w[:, k, m * P:(m + 1) * P], src[:, k, :], start=(k == 0), stop=(k == DB - 1))
            last.then_inc(w_used[pos % R], 1)

        def token_tile(pos, ev, i=0, src=hT):
            weights(pos, i)
            banks_free(ev, i)
            w = ring_k(pos % R, 512)
            for b in range(TB):
                for k in range(DB):
                    last = pe.matmul(ps[:, 2 * (ev % 2) + b, :], src[:, k, b * P:(b + 1) * P], w[:, k, :],
                                     start=(k == 0), stop=(k == DB - 1))
            last.then_inc(w_used[pos % R], 1)

        def out_product(pos, n_k, src, ready):
            for t in range((n_k + 3) // 4):
                weights(pos + t)
                ready(t)
                w = ring_o((pos + t) % R, 4)
                for kb in range(min(4, n_k - 4 * t)):
                    k = 4 * t + kb
                    for b in range(TB):
                        for c in range(2):
                            last = pe.matmul(ps[:, 2 * b + c, :], src[:, k, b * P:(b + 1) * P],
                                             w[:, kb, c * 512:(c + 1) * 512], start=(k == 0), stop=(k == n_k - 1))
                last.then_inc(w_used[(pos + t) % R], 1)

        def norm_transposes(site):
            pe.wait_ge(s["xn_ready"], site + 1)
            for bank in range(4):
                for u in range(2):
                    k = 2 * bank + u
                    for b in range(TB):
                        last = pe.transpose(ps[:, 4 + bank, u * L + b * P:u * L + (b + 1) * P],
                                            xn[:, b, k * P:(k + 1) * P], ident[:, :])
                last.then_inc(s["xn_T"], 1)

        def hT_ready(site):
            pe.wait_ge(s["hT_act"], site + 1)
            pe.wait_ge(s["hT_dve"], site + 1)

        def ada_tile(l, t):
            pos, n = POS_ADA[l] + t, 12 * l + t
            weights(pos)
            if n >= 2:
                pe.wait_ge(s["ada_ev"], n - 1)
            w = ring_k(pos % R, 512)
            q = 32 * (t % 4)
            for k in range(DB):
                last = pe.matmul(ps[q:q + 1, 2 + n % 2, :], cT[:, k:k + 1], w[:, k, :], start=(k == 0), stop=(k == DB - 1))
            last.then_inc(w_used[pos % R], 1)

        def mod_columns(l):
            pe.wait_ge(s["mod_rows"], 16 * 12 * (l + 1))
            pe.transpose(ps[:, 4, 0:48], modpack[:, :], ident[0:48, 0:48]).then_inc(s["mod_T"], 1)

        def gate_rows(l):
            for i, t in enumerate((4, 5, 10, 11)):
                q, c = 32 * (t % 4), t // 4
                last = pe.matmul(ps[:, i, :], ones[q:q + 1, :], modrow[q:q + 1, c, :], start=True, stop=True)
            last.then_inc(s["gate_bc"], 1)

        def bias_group(g):
            if g >= 2:
                pe.wait_ge(s["bias_ev"], g - 1)
            for u in range(4):
                kc = 4 * g + u
                last = pe.matmul(ps[:, 6 + g % 2, 96 * u:96 * u + 96], band[:, 63 - kc:191 - kc], rpbT,
                                 start=True, stop=True)
            last.then_inc(s["bias_mm"], 1)

        pe.wait_ge(s["const"], 1)
        pe.wait_ge(s["packs"], 16 * (6 + 2 * NA_H))
        o = 0
        for pk in packs:
            n = pk.shape[0]
            pe.transpose(ps[:, 4, o:o + n], pk, ident[0:n, 0:n])
            o += n
        pe.transpose(ps[0:64, 5, 0:96], rpb_pack, ident[0:96, 0:96]).then_inc(s["cols_T"], 1)
        pe.wait_ge(s["cols"], 2)
        pe.wait_ge(s["cond"], 1)
        for g in range(4):
            bias_group(g)
        for t in range(ADA_T):
            ada_tile(0, t)
            bias_group(4 + t)
        mod_columns(0)
        pe.wait_ge(s["coef"], 1)
        gate_rows(0)
        norm_transposes(0)
        hT_ready(0)
        pe.wait_ge(s["gate_done"], 1)
        for t in range(5):
            channel_tile(POS_ZX + t, EV_ZX + t)
        weights(POS_DT)
        banks_free(EV_DT)
        w = ring_k(POS_DT % R, 32)
        for k in range(DB):
            last = pe.matmul(ps[0:32, 2 * (EV_DT % 2), 0:L], w[:, k, :], hT[:, k, :], start=(k == 0), stop=(k == DB - 1))
        last.then_inc(w_used[POS_DT % R], 1)
        for t in range(4):
            channel_tile(POS_QK + t, EV_QK + t)
        for t in range(2):
            token_tile(POS_V + t, EV_V + t)
        pe.wait_ge(s["conv_silu"], 3)
        for g in range(2):
            for b in range(TB):
                last = pe.matmul(ps[:, 6 + g, b * L:(b + 1) * L], cvT[:, 8 + g, b * P:(b + 1) * P], cvT[:, 10 + g, :],
                                 start=(b == 0), stop=(b == 1), skip_group_check=True)
        last.then_inc(s["CB"], 1)
        pe.wait_ge(s["ev_act"], EV_V + 2)
        pe.wait_ge(s["ev_dve"], EV_V + 2)
        for b in range(TB):
            for c in range(2):
                for u in range(4):
                    last = pe.transpose(ps[:, (2 + c) if b == 0 else c, u * P:(u + 1) * P],
                                        cvT[:, 4 * c + u, b * P:(b + 1) * P], ident[:, :])
                last.then_inc(s["X_T"], 1)
        pe.wait_ge(s["U_ready"], 2)
        for b in range(TB):
            pe.transpose(ps[:, 5, 64 * b:64 * b + 32], Urow[:, b * P:(b + 1) * P], ident[0:32, 0:32])
            last = pe.transpose(ps[:, 5, 64 * b + 32:64 * b + 64], dtw[:, 2, b * P:(b + 1) * P], ident[0:32, 0:32])
        last.then_inc(s["U_T"], 1)
        pe.wait_ge(s["X_ev"], 4)

        def decay_arg(i):
            h, d = i // 2, i % 2
            if i >= 2:
                pe.wait_ge(s["ss_exp"], i - 1)
            sel = ident[0:32, d * 16 + h:d * 16 + h + 1].to_broadcast([32, P])
            o = ps[:, i % 2, :]
            if d == 0:
                pe.matmul(o[:, 0:L], sel, Urow[:, :], start=True, stop=False, skip_group_check=True)
                pe.matmul(o[:, L:384], sel, Urow[:, P:L], start=False, stop=False, skip_group_check=True)
            else:
                pe.matmul(o[:, 0:P], sel, Urow[:, 0:P], start=True, stop=False, skip_group_check=True)
                pe.matmul(o[:, P:384], sel, Urow[:, :], start=False, stop=False, skip_group_check=True)
            pe.matmul(o[:, 0:P], ident[:, :], tri[:, d, :], start=False, stop=False, skip_group_check=True)
            pe.matmul(o[:, L:384], ident[:, :], tri[:, d, :], start=False, stop=True, skip_group_check=True)\
                .then_inc(s["ss_arg"], 1)

        def ssd_y(i):
            h, d = i // 2, i % 2
            pe.wait_ge(s["ss_M"], i + 1)
            if i % 4 == 0 and i >= 8:
                pe.wait_ge(s["y_gated"], i // 4 - 1)
            rows = slice(64 * (h % 2), 64 * (h % 2) + 64)
            o = ps[rows, 4 + (h // 2) % 2, :]
            xh = [X[:, b, 64 * h:64 * h + 64] for b in range(TB)]
            m = ssM[:, i % 2, :]
            if d == 0:
                pe.matmul(o[:, 0:L], xh[0], m[:, 0:L], start=True, stop=False, skip_group_check=True)
                last = pe.matmul(o[:, P:L], xh[1], m[:, L:384], start=False, stop=False, skip_group_check=True)
            else:
                pe.matmul(o[:, 0:P], xh[0], m[:, 0:P], start=False, stop=False, skip_group_check=True)
                last = pe.matmul(o[:, 0:L], xh[1], m[:, P:384], start=False, stop=True, skip_group_check=True)
            last.then_inc(s["ss_y"], 1)

        t1 = 0
        pe.wait_ge(s["U_cols"], 1)
        for i in range(2 * SSD_H + 1):
            if i < 2 * SSD_H:
                decay_arg(i)
            if i >= 1:
                ssd_y(i - 1)
            if i < 32 and i % 8 in (1, 4, 6):
                ada_tile(1, t1)
                t1 += 1
        pe.wait_ge(s["y_sq"], 1)
        for j in range(DB):
            last = pe.matmul(ps[:, 4, 0:L], ones[:, :], cvT[:, j, :], start=(j == 0), stop=(j == DB - 1))
        last.then_inc(s["y_sum"], 1)
        pe.wait_ge(s["y_rs"], 1)
        pe.wait_ge(s["ada_ev"], 24)

        def na_scores(h):
            if h >= 2:
                pe.wait_ge(s["na_max"], h - 1)
            rows = slice(64 * (h % 2), 64 * (h % 2) + 64)
            for b in range(TB):
                last = pe.matmul(ps[:, h % 2, b * L:(b + 1) * L], pT[rows, 20 + h // 2, b * P:(b + 1) * P],
                                 pT[rows, 28 + h // 2, :], start=(b == 0), stop=(b == 1), skip_group_check=True)
            last.then_inc(s["na_s"], 1)

        def na_transposes(h):
            pe.wait_ge(s["na_p"], h + 1)
            if h >= 2:
                pe.wait_ge(s["na_pT_ev"], h - 1)
            for c in range(2):
                for b in range(TB):
                    last = pe.transpose(ps[:, 2 + h % 2, c * L + b * P:c * L + (b + 1) * P],
                                        naS[:, h % 2, b * L + c * P:b * L + (c + 1) * P], ident[:, :])
            last.then_inc(s["na_pT"], 1)

        def na_out(h):
            pe.wait_ge(s["na_pT_ev"], h + 1)
            if h % 2 == 0 and h >= 4:
                pe.wait_ge(s["na_y"], h // 2 - 1)
            rows = slice(64 * (h % 2), 64 * (h % 2) + 64)
            for c in range(2):
                last = pe.matmul(ps[rows, 4 + (h // 2) % 2, 0:L], v_na[:, c, 64 * h:64 * h + 64], naPT[:, c, :],
                                 start=(c == 0), stop=(c == 1))
            last.then_inc(s["na_o"], 1)

        for h in range(NA_H + 2):
            if h < NA_H:
                na_scores(h)
            if h >= 2:
                na_out(h - 2)
            if 1 <= h <= NA_H:
                na_transposes(h - 1)
        pe.wait_ge(s["y_ssd"], 1)
        pe.wait_ge(s["na_y"], 8)
        mod_columns(1)
        out_product(POS_AOUT, 16, hid, lambda t: None)

        def mlp(l, site):
            norm_transposes(site)
            hT_ready(site)
            rounds(pe, 8, lambda j, i, t: channel_tile(POS_MLP[l] + j, EV_MLP[l] + j, i))
            pe.wait_ge(s["ev_act"], EV_MLP[l] + 8)
            pe.wait_ge(s["ev_dve"], EV_MLP[l] + 8)

            def ready(t):
                pe.wait_ge(s["hid"], 8 * l + t + 1)
            out_product(POS_MLP[l] + 8, 32, hid, ready)

        mlp(0, 1)

        pe.wait_ge(s["x_ready"], 2)
        gate_rows(1)
        norm_transposes(2)
        hT_ready(2)
        pe.wait_ge(s["gate_done"], 2)
        for t in range(4):
            channel_tile(POS_MQK + t, EV_MQK + t)
        weights(POS_MG)
        banks_free(EV_MG)
        w = ring_k(POS_MG % R, 32)
        for k in range(DB):
            last = pe.matmul(ps[0:32, 2 * (EV_MG % 2), 0:L], w[:, k, :], hT[:, k, :], start=(k == 0), stop=(k == DB - 1))
        last.then_inc(w_used[POS_MG % R], 1)
        token_tile(POS_MVO, EV_MVO)
        pe.wait_ge(s["perm"], 4)
        pe.wait_ge(s["ev_act"], EV_MG + 1)
        for w in range(2):
            last = pe.matmul(ps[0:16, 5, w * L:(w + 1) * L], perm[:, w, :], gw[:, 0, :], start=(w == 0), stop=(w == 1),
                             skip_group_check=True)
        last.then_inc(s["g_IF"], 1)
        for t in range(1, 8):
            token_tile(POS_MVO + t, EV_MVO + t)
        pe.wait_ge(s["g_rows2"], 1)
        for b in range(TB):
            pe.transpose(ps[:, 4, 32 * b:32 * b + 16], gw[0:16, 5, b * P:(b + 1) * P], ident[0:16, 0:16])
            last = pe.transpose(ps[:, 4, 32 * b + 16:32 * b + 32], gw[0:16, 3, b * P:(b + 1) * P], ident[0:16, 0:16])
        last.then_inc(s["g_T"], 1)
        pe.wait_ge(s["ev_act"], EV_MVO + 8)
        pe.wait_ge(s["ev_dve"], EV_MVO + 8)

        def ml_arg(i):
            h, d = i // 2, i % 2
            if i >= 2:
                pe.wait_ge(s["ml_exp"], i - 1)
            sel = ident[0:16, d * 8 + h:d * 8 + h + 1].to_broadcast([16, P])
            o = ps[:, i % 2, :]
            if d == 0:
                pe.matmul(o[:, 0:L], sel, nMrow[:, :], start=True, stop=False, skip_group_check=True)
                pe.matmul(o[:, L:384], sel, nMrow[:, P:L], start=False, stop=False, skip_group_check=True)
            else:
                pe.matmul(o[:, 0:P], sel, nMrow[:, 0:P], start=True, stop=False, skip_group_check=True)
                pe.matmul(o[:, P:384], sel, nMrow[:, :], start=False, stop=False, skip_group_check=True)
            pe.matmul(o[:, 0:P], ident[:, :], tri[:, d, :], start=False, stop=False, skip_group_check=True)
            pe.matmul(o[:, L:384], ident[:, :], tri[:, d, :], start=False, stop=True, skip_group_check=True)\
                .then_inc(s["ml_arg"], 1)

        def ml_scores(h):
            if h >= 2:
                pe.wait_ge(s["ml_M"], 2 * h - 2)
            for b in range(TB):
                last = pe.matmul(ps[:, 2 + h % 2, b * L:(b + 1) * L], mkT[:, h, b * P:(b + 1) * P], mqT[:, h, :],
                                 start=(b == 0), stop=(b == 1), skip_group_check=True)
            last.then_inc(s["ml_S"], 1)

        def ml_values(i):
            h, d = i // 2, i % 2
            pe.wait_ge(s["ml_M"], i + 1)
            if i >= 2:
                pe.wait_ge(s["ml_h"], i - 1)
            m = mM[:, i % 2, :]
            o = [ps[:, 4 + 2 * (i % 2) + b, 0:257] for b in range(TB)]
            v = [mv[:, b, h, :] for b in range(TB)]
            if d == 0:
                pe.matmul(o[0], m[:, 0:P], v[0], start=True, stop=True)
                pe.matmul(o[1], m[:, P:L], v[0], start=True, stop=False)
                last = pe.matmul(o[1], m[:, L:384], v[1], start=False, stop=True)
            else:
                pe.matmul(o[0], m[:, 0:P], v[0], start=True, stop=False)
                pe.matmul(o[0], m[:, P:L], v[1], start=False, stop=True)
                last = pe.matmul(o[1], m[:, L:384], v[1], start=True, stop=True)
            last.then_inc(s["ml_num"], 1)

        pe.wait_ge(s["g_cols"], 2)
        for i in range(2 * ML_H + 1):
            if i < 2 * ML_H:
                if i % 2 == 0:
                    ml_scores(i // 2)
                ml_arg(i)
            if i >= 1:
                ml_values(i - 1)
        pe.wait_ge(s["ml_h"], 16)
        for g in range(8):
            pe.wait_ge(s["ml_y"], g + 1)
            for u in range(2):
                for b in range(TB):
                    last = pe.transpose(ps[:, g, u * L + b * P:u * L + (b + 1) * P],
                                        mh[:, b, (2 * g + u) * P:(2 * g + u + 1) * P], ident[:, :])
            last.then_inc(s["ml_yT"], 1)
        pe.wait_ge(s["ml_yT_act"], 4)
        pe.wait_ge(s["ml_yT_dve"], 4)
        out_product(POS_MOUT, 16, hid, lambda t: None)
        mlp(1, 3)

        def gated_ffn(pos, ev):
            rounds(pe, FB // 2, lambda j, i, t: channel_tile(pos + j, ev + j, i))
            pe.wait_ge(s["ev_act"], ev + FB // 2)
            pe.wait_ge(s["ev_dve"], ev + FB // 2)
            out_product(pos + FB // 2, FB, hid, lambda t: None)

        def mats(bank, lhsT, rhs, name):
            for n in range(4 * HP):
                i = 6 * (n % 2) + n // 2
                o = ps[:, bank + i // 3, (i % 3) * P:(i % 3 + 1) * P]
                last = pe.matmul(o, lhsT(i), rhs(i), start=True, stop=True)
            marks["pe"].done(last, name)

        def head(v):
            return lambda i: v[64 * (i // 6):64 * (i // 6) + 64, i % 6 // 2, (i % 2) * P:(i % 2 + 1) * P]

        def head_sums(col, src, name):
            for j in range(HP):
                last = pe.matmul(psf[:, col + j * L:col + (j + 1) * L], blk, src[:, j, :], start=True, stop=True)
            marks["pe"].done(last, name)

        def mixer_pe(l, p0, e0):
            mark = marks["pe"].done
            AV, DV = (lambda n: at["act"](n, l)), (lambda n: at["dve"](n, l))
            for t in range(7):
                channel_tile(p0 + O_MIX + t, e0 + E_MIX + t)
            pos, ev = p0 + O_MIX + 7, e0 + E_MIX + 7
            weights(pos)
            banks_free(ev)
            w = ring_k(pos % R, P)
            for k in range(DB):
                last = pe.matmul(ps[:, 2 * (ev % 2), 0:L], w[:, k, :], hT[:, k, :], start=(k == 0), stop=(k == DB - 1))
            last.then_inc(w_used[pos % R], 1)
            for b in range(TB):
                for j in range(HP):
                    last = pe.transpose(ps[:, 6 + b, j * P:(j + 1) * P], cpT[:, 12 + j, b * P:(b + 1) * P], ident[:, :])
            mark(last, "tokens")
            pe.wait_ge(s["ev_act"], e0 + E_MIX + 8)
            pe.wait_ge(s["ev_dve"], e0 + E_MIX + 8)
            for n, m in enumerate(LEVELS):
                pe.wait_ge(s["dve_mix"], DV(f"qk{m}"))
                q, k = head(hgQ[n % 2]), head(hgK[n % 2])
                if n == 0:
                    for n6 in range(2 * HP):
                        h, j = n6 % 2, n6 // 2
                        last = pe.matmul(ps[:, 2 * h, j * P:(j + 1) * P], k(6 * h + 2 * j), q(6 * h + 2 * j + 1),
                                         start=True, stop=True)
                    mark(last, f"level{m}")
                else:
                    if n == 2:
                        pe.wait_ge(s["act_mix"], AV("att2"))
                    elif n >= 3:
                        pe.wait_ge(s["dve_mix"], DV(f"att{LEVELS[n - 2]}"))
                    mats(4 * (n % 2), k, q, f"level{m}")
            pe.wait_ge(s["dve_mix"], DV(f"att{LEVELS[-2]}"))
            mats(0, head(cpT[:, 9:12, :]), head(cpT[:, 6:9, :]), "level0")
            pe.wait_ge(s["dve_mix"], DV("att0"))
            pe.wait_ge(s["act_mix"], AV("i_tok"))
            for j in range(HP):
                for h in range(2):
                    o = ps[64 * h:64 * h + 64, 6 + j // 2, (j % 2) * L:(j % 2 + 1) * L]
                    v = [i_tok[:, b, P * j + 64 * h:P * j + 64 * h + 64] for b in range(TB)]
                    u = 6 * h + 2 * j
                    pe.matmul(o[:, 0:P], v[0], hgAtt[:, u, :], start=(j % 2 == 0), stop=False, skip_group_check=True)
                    pe.matmul(o[:, P:L], v[0], hgAtt2[:, 3 * h + j, :], start=False, stop=False, skip_group_check=True)
                    last = pe.matmul(o[:, P:L], v[1], hgAtt[:, u + 1, :], start=False, stop=True,
                                     skip_group_check=True)
            mark(last, "hg_o")
            pe.wait_ge(s["act_mix"], AV("low_in"))
            pe.wait_ge(s["c_lowrank"], 48 * (l + 1))
            for j in range(HP):
                c = slice(j * P, (j + 1) * P)
                pe.matmul(psf[:, 1024 + j * L:1024 + (j + 1) * L], lowA[0:64, c], cpT[0:64, 27, :], start=True, stop=True)
                pe.matmul(psf[:, 2048 + j * L:2048 + (j + 1) * L], lowA[64:128, c], cpT[64:128, 27, :], start=True,
                          stop=True)
            pe.wait_ge(s["act_mix"], AV("hg_sq"))
            head_sums(0, hgC, "hg_ss")
            pe.wait_ge(s["dve_mix"], DV("o_norm"))
            for j in range(HP):
                last = pe.matmul(psf[:, 2816 + j * L:2816 + (j + 1) * L], lowG[:, j * P:(j + 1) * P], cpT[:, 28, :],
                                 start=True, stop=True)
            mark(last, "low_rank")
            pe.wait_ge(s["act_mix"], AV("hg_rs"))
            for b in range(TB):
                for j in range(HP):
                    last = pe.transpose(ps[:, b, j * P:(j + 1) * P], cpT[:, 24 + j, b * P:(b + 1) * P], ident[:, :])
            mark(last, "tokens2")
            pe.wait_ge(s["act_mix"], AV("kk_sq"))
            head_sums(0, rwT0, "kk_ss")
            pe.wait_ge(s["dve_mix"], DV("rk"))
            head_sums(1024, rwT1, "bonus")
            pe.wait_ge(s["dve_mix"], DV("operands"))
            for i, v in enumerate((bh_, kh_)):
                for j in range(HP):
                    last = pe.transpose(ps[:, 6 + i, j * P:(j + 1) * P], v[:, j, 0:P], ident[:, :])
            mark(last, "bk_tok")
            mats(0, head(bh_), head(at_), "LabT")
            pe.wait_ge(s["act_mix"], AV("bk_tok"))
            mats(4, head(at_), head(bh_), "Lab")
            pe.wait_ge(s["act_mix"], AV("LabT"))
            mats(0, head(kh_), head(at_), "LakT")
            pe.wait_ge(s["dve_mix"], DV("Lab"))
            mats(4, head(bh_), head(rt_), "LrbT")
            pe.wait_ge(s["dve_mix"], DV("LakT"))
            mats(0, head(kh_), head(rt_), "LrkT")
            e = lambda v: (lambda i: v[:, i, :])
            X, XT, N, NT = e(iX), e(iXT), e(iN), e(iNT)
            pe.wait_ge(s["dve_mix"], DV("base"))
            for p in range(3):
                mats(0, NT, N, f"N{p}")
                if p < 2:
                    mats(4, N, NT, f"NT{p}")
                pe.wait_ge(s["act_mix"], AV(f"N{p}"))
                mats(0, XT, N, f"dX{p}")
                if p < 2:
                    pe.wait_ge(s["dve_mix"], DV(f"NT{p}"))
                mats(4, N, XT, f"dXT{p}")
                pe.wait_ge(s["dve_mix"], DV(f"XT{p}"))
            for p in range(3):
                pe.wait_ge(s["dve_mix"], DV(f"B{p}"))
                mats(0, N, X, f"W{p}")
                pe.wait_ge(s["act_mix"], AV(f"W{p}"))
                if p < 2:
                    mats(0, XT, NT, f"mX{p}")
                mats(4, NT, XT, f"mXT{p}")
                pe.wait_ge(s["dve_mix"], DV(f"mXT{p}"))
            for c in range(2):
                heads = [(2 * j + h, j, 6 * h + 2 * j + c, slice(64 * h, 64 * h + 64), slice(128 * j + 64 * h, 128 * j + 64 * h + 64))
                         for j in range(HP) for h in range(2)]
                for u, j, i, rows, cu in heads:
                    o = ps[:, 3 * (u % 2), 64 * j:64 * j + 64]
                    last = pe.matmul(o, LakT[:, i, :], v_tok[:, c, cu], start=True, stop=(c == 0))
                    if c == 1:
                        last = pe.matmul(o, at_[rows, j, P:L], rwState[rows, j, :], start=False, stop=True)
                mark(last, f"Z{c}")
                pe.wait_ge(s["act_mix"], AV(f"Z{c}"))
                for u, j, i, rows, cu in heads:
                    last = pe.matmul(ps[:, 1, cu], iXT[:, i, :], rwZ[:, c, cu], start=True, stop=True)
                mark(last, f"P{c}")
                pe.wait_ge(s["act_mix"], AV(f"P{c}"))
                if c == 0:
                    for u, j, i, rows, cu in heads:
                        o = ps[rows, 2, 64 * j:64 * j + 64]
                        pe.matmul(o, bk_tok[:, 0, cu], rwP[:, 0, cu], start=True, stop=False)
                        last = pe.matmul(o, bk_tok[:, 1, cu], v_tok[:, 0, cu], start=False, stop=True)
                    mark(last, "state")
                for u, j, i, rows, cu in heads:
                    o = ps[rows, 6 + j // 2, (j % 2) * L + c * P:(j % 2) * L + (c + 1) * P]
                    pe.matmul(o, rwP[:, c, cu], LrbT[:, i, :], start=True, stop=False)
                    last = pe.matmul(o, v_tok[:, c, cu], LrkT[:, i, :], start=False, stop=(c == 0))
                    if c == 1:
                        last = pe.matmul(o, rwState[rows, j, :], rt_[rows, j, P:L], start=False, stop=True)
                mark(last, f"y{c}")
                if c == 0:
                    pe.wait_ge(s["dve_mix"], DV("state"))
            pe.wait_ge(s["act_mix"], AV("y"))
            head_sums(0, at_, "mean")
            pe.wait_ge(s["act_mix"], AV("y_sq"))
            head_sums(1024, kh_, "var")
            pe.wait_ge(s["dve_mix"], DV("y_rw"))
            out_product(p0 + O_MO, DB, hid, lambda t: None)

        def attention_pe(l, p0, e0):
            if l == 0:
                pe.wait_ge(s["mem_xn"], 1)
            for bank in range(4):
                for u in range(2):
                    k = 2 * bank + u
                    for b in range(TB):
                        last = pe.transpose(ps[:, 4 + bank, u * L + b * P:u * L + (b + 1) * P],
                                            memn[:, b, k * P:(k + 1) * P], ident[:, :])
                last.then_inc(s["mem_T"], 1)
            pe.wait_ge(s["memT_act"], l + 1)
            pe.wait_ge(s["memT_dve"], l + 1)
            pe.wait_ge(s["x_ready"], 6 + 4 * l)
            for t in range(2):
                channel_tile(p0 + O_K + t, e0 + E_K + t, src=memT)
            for t in range(2):
                token_tile(p0 + O_V + t, e0 + E_V + t, src=memT)
            norm_transposes(6 + 4 * l)
            hT_ready(6 + 4 * l)
            for t in range(2):
                channel_tile(p0 + O_Q + t, e0 + E_Q + t)
            pe.wait_ge(s["ev_act"], e0 + E_Q + 2)
            pe.wait_ge(s["ev_dve"], e0 + E_Q + 2)
            for h in range(4):
                for b in range(TB):
                    for k in range(2):
                        last = pe.matmul(ps[:, 4 + h, b * L:(b + 1) * L], xqT[:, 2 * h + k, b * P:(b + 1) * P],
                                         xkT[:, 2 * h + k, :], start=(k == 0), stop=(k == 1))
                last.then_inc(s["xa_s"], 1)
            for h in range(4):
                pe.wait_ge(s["xa_p"], 4 * l + h + 1)
                for c in range(2):
                    for b in range(TB):
                        last = pe.transpose(ps[:, h, c * L + b * P:c * L + (b + 1) * P], xP[:, h, b, c * P:(c + 1) * P],
                                            ident[:, :])
                last.then_inc(s["xa_pT"], 1)
            for h in range(4):
                pe.wait_ge(s["xa_pT_dve" if h % 2 else "xa_pT_act"], 2 * l + h // 2 + 1)
                for u in range(2):
                    for c in range(2):
                        last = pe.matmul(ps[:, 4 + h, u * L:(u + 1) * L], xv[:, c, (2 * h + u) * P:(2 * h + u + 1) * P],
                                         xPT[:, h, c, :], start=(c == 0), stop=(c == 1))
                last.then_inc(s["xa_o"], 1)
            pe.wait_ge(s["xa_y_act"], 2 * l + 2)
            pe.wait_ge(s["xa_y_dve"], 2 * l + 2)
            out_product(p0 + O_WO, DB, hid, lambda t: None)

        pe.wait_ge(s["c_packs"], 2 * 16 * (len(PACK) + 1))
        pe.wait_ge(s["masks"], 1)
        for l in range(2):
            p0, e0 = POS_C + C_TILES * l, EV_C + C_EVS * l
            pe.wait_ge(s["x_ready"], 4 + 4 * l)
            pe.transpose(ps[:, 0, 0:PACK_N], packC[l], ident[0:PACK_N, 0:PACK_N]).then_inc(s["c_cols_T"], 1)
            norm_transposes(4 + 4 * l)
            hT_ready(4 + 4 * l)
            pe.wait_ge(s["c_cols"], l + 1)
            gated_ffn(p0 + O_F1, e0 + E_F1)
            norm_transposes(5 + 4 * l)
            hT_ready(5 + 4 * l)
            mixer_pe(l, p0, e0)
            attention_pe(l, p0, e0)
            norm_transposes(7 + 4 * l)
            hT_ready(7 + 4 * l)
            gated_ffn(p0 + O_F2, e0 + E_F2)

    @block.vector
    def _(dve):
        chain = [0]

        def link(ins):
            chain[0] += 1
            ins.then_inc(s["dve_chain"], 1)
            dve.wait_ge(s["dve_chain"], chain[0])

        def tile_out(pos, ev, dst):
            dve.wait_ge(w_used[pos % R], pos // R + 1)
            dve.tensor_copy(dst, ps[:, 2 * (ev % 2) + 1, 0:512]).then_inc(s["ev_dve"], 1)

        def chan(t0, t):
            return pT[:, t0 + 4 * t + 2:t0 + 4 * t + 4, :].rearrange("p b n -> p (b n)")

        def ada_out(l, t):
            pos, n = POS_ADA[l] + t, 12 * l + t
            q = 32 * (t % 4)
            dve.wait_ge(w_used[pos % R], pos // R + 1)
            if t == 0:
                dve.wait_ge(s["mod_in"], 64 * (l + 1))
            r = modrow[q:q + 1, t // 4, :]
            dve.tensor_tensor(r, ps[q:q + 1, 2 + n % 2, :], r, ALU.add).then_inc(s["ada_ev"], 1)

        def bias_out(g):
            dve.wait_ge(s["bias_mm"], g + 1)
            dve.tensor_tensor(biasf[:, :, :].rearrange("p h (x c) -> p (h x) c", x=6)[:, :, 4 * g:4 * g + 4],
                              ps[:, 6 + g % 2, 0:384].rearrange("p (c y) -> p y c", c=4),
                              wmask[:, 4 * g:4 * g + 4].unsqueeze(1).to_broadcast([P, 96, 4]),
                              ALU.add).then_inc(s["bias_ev"], 1)

        def mod_coefs(l):
            dve.wait_ge(s["mod_T"], l + 1)
            link(dve.tensor_copy(modT[:, l, :], ps[:, 4, 0:48]))
            for n in range(2):
                g = cols[:, C_NG + 32 * l + 16 * n:C_NG + 32 * l + 16 * n + 8]
                ins = dve.scalar_tensor_tensor(coef[:, l, n, :], modT[:, l, 24 * n + 8:24 * n + 16], 1.0, g,
                                               ALU.add, ALU.mult)
            ins.then_inc(s["coef"], 1)

        def gate_gains(l):
            dve.wait_ge(s["gate_bc"], l + 1)
            dve.wait_ge(s["gain_in"], 32 * (l + 1))
            for i in range(4):
                g = gains[:, i // 2, (i % 2) * 512:(i % 2) * 512 + 512]
                ins = dve.tensor_tensor(g, ps[:, i, :], g, ALU.mult)
            ins.then_inc(s["gate_done"], 1)

        def normalise(site, ssq):
            dve.wait_ge(s["ssq"], ssq)
            for b in range(TB):
                ins = dve.tensor_scalar(xn[:, b, :], x[:, b, :], stat[:, 2 + b:3 + b], None, ALU.mult)
            ins.then_inc(s["xn_ready"], 1)

        def norm_out(site, A, B):
            for b in range(2, 4):
                dve.wait_ge(s["xn_T"], 4 * site + b + 1)
                for u in range(2):
                    k = 2 * b + u
                    o, i = hT[:, k, :], ps[:, 4 + b, u * L:(u + 1) * L]
                    if B is None:
                        ins = dve.tensor_scalar(o, i, A[:, k:k + 1], None, ALU.mult)
                    else:
                        ins = dve.tensor_scalar(o, i, A[:, k:k + 1], B[:, k:k + 1], ALU.mult, ALU.add)
            ins.then_inc(s["hT_dve"], 1)

        dve.wait_ge(s["cols_T"], 1)
        dve.tensor_copy(cols[:, 0:248], ps[:, 4, 0:248]).then_inc(s["cols"], 1)
        dve.tensor_copy(rpbT, ps[0:64, 5, 0:96]).then_inc(s["cols"], 1)
        for g in range(4):
            bias_out(g)
        for t in range(ADA_T):
            ada_out(0, t)
            bias_out(4 + t)
        normalise(0, 1)
        mod_coefs(0)
        gate_gains(0)
        norm_out(0, coef[:, 0, 0, :], modT[:, 0, 0:8])
        for t in range(5):
            tile_out(POS_ZX + t, EV_ZX + t, chan(0, t))
        dve.wait_ge(s["alog_e"], 1)
        dve.tensor_scalar(small[0:32, 2:3], small[0:32, 2:3], -1.0, None, ALU.mult)
        dve.wait_ge(s["ev_act"], EV_DT + 1)
        dve.scalar_tensor_tensor(dtw[:, 1, :], dtw[:, 0, :], -1.0, dtw[:, 0, :], ALU.mult, ALU.min)\
            .then_inc(s["ev_dve"], 1)

        def conv_block(j):
            u, o = pT[:, 8 + j, :], cvT[:, j, :]
            tap = lambda d: cols[:, C_CW + 12 * d + j:C_CW + 12 * d + j + 1]
            link(dve.tensor_scalar(o, u, tap(2), cols[:, C_CB + j:C_CB + j + 1], ALU.mult, ALU.add))
            for d in (0, 1, 3, 4):
                k = d - 2
                lo, hi = max(0, -k), L - max(0, k)
                ins = dve.scalar_tensor_tensor(o[:, lo:hi], u[:, lo + k:hi + k], tap(d), o[:, lo:hi], ALU.mult, ALU.add)
                if d < 4:
                    link(ins)
            return ins

        for t in range(4):
            tile_out(POS_QK + t, EV_QK + t, chan(20, t))
            if t == 0:
                dve.wait_ge(s["ev_act"], EV_ZX + 5)
            for j in range(4 * t, min(4 * t + 4, CONV_B)):
                ins = conv_block(j)
            if t < 3:
                ins.then_inc(s["conv"], 1)
        dve.wait_ge(s["dt_ln"], 1)
        link(dve.scalar_tensor_tensor(dtw[:, 2, :], dtw[:, 0, :], 0.0, dtw[:, 1, :], ALU.max, ALU.add))
        link(dve.tensor_scalar(dtw[:, 3, :], dtw[:, 2, :], small[0:32, 2:3], None, ALU.mult))
        link(dve.tensor_tensor_scan(dtw[:, 0, :], ones[0:32, 0:1].to_broadcast([32, L]), dtw[:, 3, :], 0.0,
                                    ALU.mult, ALU.add))
        link(dve.tensor_scalar(dtw[:, 3, :], dtw[:, 3, :], dirs[:, 1:2], None, ALU.mult))
        dve.scalar_tensor_tensor(Urow[:, :], dtw[:, 0, :], dirs[:, 0:1], dtw[:, 3, :], ALU.mult, ALU.add)\
            .then_inc(s["U_ready"], 2)
        for t in range(2):
            tile_out(POS_V + t, EV_V + t, v_na[:, 1, 512 * t:512 * t + 512])
        for b in range(2):
            dve.wait_ge(s["X_T"], 3 + b)
            dve.tensor_copy(X[:, 1, 512 * b:512 * b + 512], ps[:, b, :]).then_inc(s["X_ev"], 1)
        dve.wait_ge(s["U_T"], 1)
        v = ps[:, 5, 0:128].rearrange("p (b w r) -> p b w r", b=2, w=2)
        dve.tensor_scalar(Ucol[:, :, 0, :], v[:, :, 0, :], -1.0, None, ALU.mult)
        dve.tensor_copy(Ucol[:, :, 1, :], v[:, :, 1, :]).then_inc(s["U_cols"], 1)
        dve.wait_ge(s["U_cols"], 1)
        dve.wait_ge(s["CB"], 1)
        dve.wait_ge(s["z_silu"], 1)
        t1 = 0
        for i in range(2 * SSD_H):
            h, d = i // 2, i % 2
            g, r, n0 = h // 8, d * 16 + h, (L if d == 0 else P)
            t0 = 0 if d == 1 else P
            dve.wait_ge(s["ss_exp"], i + 1)
            if i >= 2:
                dve.wait_ge(s["ss_y"], i - 1)
            e, m = ssE[:, i % 2, :], ssM[:, i % 2, :]
            dve.scalar_tensor_tensor(m[:, 0:n0], e[:, 0:n0], Ucol[:, 0, 1, r:r + 1], ps[:, 6 + g, 0:n0],
                                     ALU.mult, ALU.mult)
            dve.scalar_tensor_tensor(m[:, n0:384], e[:, n0:384], Ucol[:, 1, 1, r:r + 1],
                                     ps[:, 6 + g, L + t0:2 * L], ALU.mult, ALU.mult).then_inc(s["ss_M"], 1)
            if i % 8 in (1, 4, 6):
                ada_out(1, t1)
                t1 += 1
            if i % 4 == 3:
                j = i // 4
                dve.wait_ge(s["ss_y"], i + 1)
                link(dve.scalar_tensor_tensor(cvT[:, j, :], cvT[:, j, :], small[:, 4 + j:5 + j],
                                              ps[:, 4 + j % 2, 0:L], ALU.mult, ALU.add))
                dve.tensor_tensor(pT[:, j, :], pT[:, j, :], cvT[:, j, :], ALU.mult).then_inc(s["y_gated"], 1)
        dve.wait_ge(s["y_rs"], 1)
        for j in range(DB):
            ins = dve.scalar_tensor_tensor(hid[:, j, :], pT[:, j, :], cols[:, C_SN + j:C_SN + j + 1], cvT[:, 8, :],
                                           ALU.mult, ALU.mult)
        ins.then_inc(s["y_ssd"], 1)

        def na_bias(h):
            dve.wait_ge(s["na_s"], h + 1)
            if h >= 2:
                dve.wait_ge(s["na_pT"], h - 1)
            for b in range(TB):
                x0 = 64 * (2 - 2 * b)
                ins = dve.scalar_tensor_tensor(naS[:, h % 2, b * L:(b + 1) * L], ps[:, h % 2, b * L:(b + 1) * L],
                                               NA_D ** -0.5, biasf[:, h, x0:x0 + L], ALU.mult, ALU.add)
            link(ins)
            dve.tensor_reduce(naM[:, h % 2, 0:2], naS[:, h % 2, :].rearrange("p (b n) -> p b n", b=2), AX.X, ALU.max,
                              negate=True).then_inc(s["na_max"], 1)

        def na_normalise(h):
            dve.wait_ge(s["na_exp"], h + 1)
            link(dve.reciprocal(naM[:, h % 2, 2:4], naM[:, h % 2, 2:4]))
            for b in range(TB):
                v = naS[:, h % 2, b * L:(b + 1) * L]
                ins = dve.tensor_scalar(v, v, naM[:, h % 2, 2 + b:3 + b], None, ALU.mult)
            ins.then_inc(s["na_p"], 1)

        def na_pair(j):
            dve.wait_ge(s["na_o"], 2 * j + 2)
            dve.tensor_copy(hid[:, 8 + j, :], ps[:, 4 + j % 2, 0:L]).then_inc(s["na_y"], 1)

        for h in range(NA_H + 3):
            if h < NA_H:
                na_bias(h)
            if 1 <= h <= NA_H:
                na_normalise(h - 1)
            if h >= 4 and h % 2 == 0:
                na_pair(h // 2 - 2)
        mod_coefs(1)

        def gated_residual(pos, ssq, g):
            dve.wait_ge(w_used[pos % R], pos // R + 1)
            dve.wait_ge(s["ssq"], ssq)
            for b in range(TB):
                ins = dve.scalar_tensor_tensor(xn[:, b, :], ps[:, 2 * b:2 * b + 2, :].rearrange("p c n -> p (c n)"),
                                               stat[:, 6 + b:7 + b], gains[:, g, :], ALU.mult, ALU.mult)
            link(ins)
            for b in range(TB):
                ins = dve.tensor_tensor(x[:, b, :], x[:, b, :], xn[:, b, :], ALU.add)
            ins.then_inc(s["x_ready"], 1)

        def mlp_out_dve(l):
            def body(j, i, t):
                pos, ev = POS_MLP[l] + j, EV_MLP[l] + j
                dve.wait_ge(w_used[pos % R], pos // R + 1 + i)
                half = [hid[:, bass.ds(t * 4 + 2 * u, 2), :].rearrange("p b n -> p (b n)") for u in range(2)]
                dve.tensor_scalar(half[1], ps[:, 2 * (ev % 2) + 1, :], 0.0, None, ALU.max).then_inc(s["ev_dve"], 1)
                dve.wait_ge(s["ev_act"], EV_MLP[l] + 1 + t)
                dve.tensor_tensor(half[0], relu[:, j, :], relu[:, j, :], ALU.mult)
                dve.wait_ge(s["ev_dve"], EV_MLP[l] + 1 + t)
                dve.tensor_tensor(half[1], half[1], half[1], ALU.mult).then_inc(s["hid"], 1)
            rounds(dve, 8, body)

        gated_residual(POS_AOUT + 3, 2, 0)
        normalise(1, 3)
        norm_out(1, coef[:, 0, 1, :], modT[:, 0, 24:32])
        mlp_out_dve(0)
        gated_residual(POS_MLP[0] + 15, 4, 1)

        gate_gains(1)
        normalise(2, 5)
        norm_out(2, coef[:, 1, 0, :], modT[:, 1, 0:8])
        for t in range(4):
            tile_out(POS_MQK + t, EV_MQK + t, arena[:, 4 * t + 2:4 * t + 4, :].rearrange("p b n -> p (b n)"))
        for w in range(2):
            for d in range(2):
                c = 16 * d + 8 * w
                dve.tensor_copy(perm[:, w, 8 * d:8 * d + 8], ident[0:32, c:c + 8]).then_inc(s["perm"], 1)
        dve.wait_ge(s["ev_act"], EV_MG + 1)
        dve.wait_ge(s["ev_dve"], EV_MG)
        dve.sem_inc(s["ev_dve"], 1)
        dve.wait_ge(s["g_cols"], 1)
        tile_out(POS_MVO, EV_MVO, mv[:, 1, 0:2, 0:256])
        f = lambda k: gw[0:16, k, :]
        sgn, flag = dirsB[:, 0:1], dirsB[:, 1:2]
        dve.wait_ge(s["g_IF"], 1)
        link(dve.tensor_copy(f(1), ps[0:16, 5, L:2 * L]))
        dve.scalar_tensor_tensor(f(2), f(1), -1.0, f(1), ALU.mult, ALU.min).then_inc(s["g_neg"], 1)
        tile_out(POS_MVO + 1, EV_MVO + 1, mv[:, 1, 2:4, 0:256])
        tile_out(POS_MVO + 2, EV_MVO + 2, mv[:, 1, 4:6, 0:256])
        dve.wait_ge(s["g_ln"], 1)
        link(dve.scalar_tensor_tensor(f(1), f(1), 0.0, f(2), ALU.min, ALU.subtract))
        link(dve.tensor_tensor_scan(f(2), ones[0:16, 0:1].to_broadcast([16, L]), f(1), 0.0, ALU.mult, ALU.add))
        link(dve.tensor_scalar(mtot[:, :], f(2)[:, L - 1:L], flag, None, ALU.mult))
        link(dve.tensor_scalar(f(3), f(1), flag, mtot[:, :], ALU.mult, ALU.add))
        link(dve.scalar_tensor_tensor(f(4), f(2), sgn, f(3), ALU.mult, ALU.add))
        link(dve.tensor_tensor(f(5), ps[0:16, 5, 0:L], f(4), ALU.subtract))
        tile_out(POS_MVO + 3, EV_MVO + 3, mv[:, 1, 6:8, 0:256])
        dve.tensor_tensor_scan(f(1), f(5), f(5), 0.0, ALU.max, ALU.max)
        link(dve.tensor_tensor_scan(f(2)[:, ::-1], f(5)[:, ::-1], f(5)[:, ::-1], 0.0, ALU.max, ALU.max))
        link(dve.tensor_tensor(f(2), f(2), f(1), ALU.subtract))
        link(dve.scalar_tensor_tensor(f(2), f(2), flag, f(1), ALU.mult, ALU.add))
        link(dve.tensor_scalar(nMrow[:, :], f(2), -1.0, None, ALU.mult))
        dve.tensor_tensor(f(3), nMrow[:, :], f(4), ALU.subtract).then_inc(s["g_rows2"], 1)
        for t in range(4):
            tile_out(POS_MVO + 4 + t, EV_MVO + 4 + t, mo[:, 1, 512 * t:512 * t + 512])
        dve.wait_ge(s["g_cols"], 2)

        def ml_weights(i):
            h, d = i // 2, i % 2
            n0, t0 = (L, P) if d == 0 else (P, 0)
            dve.wait_ge(s["ml_exp"], i + 1)
            if d == 0:
                dve.wait_ge(s["ml_S"], h + 1)
            if i >= 2:
                dve.wait_ge(s["ml_num"], i - 1)
            e, m, sc = mE[:, i % 2, :], mM[:, i % 2, :], ps[:, 2 + h % 2, :]
            dve.scalar_tensor_tensor(m[:, 0:n0], sc[:, 0:n0], P ** -0.5, e[:, 0:n0], ALU.mult, ALU.mult)
            dve.scalar_tensor_tensor(m[:, n0:384], sc[:, L + t0:2 * L], P ** -0.5, e[:, n0:384], ALU.mult, ALU.mult)\
                .then_inc(s["ml_M"], 1)

        def ml_head(i):
            h, d = i // 2, i % 2
            r = d * 8 + h
            dve.wait_ge(s["ml_num"], i + 1)
            bank = 4 + 2 * (i % 2)
            link(dve.tensor_copy(mden[:, 0, :], ps[:, bank:bank + 2, 256]))
            link(dve.scalar_tensor_tensor(mden[:, 1, :], mden[:, 0, :], -1.0, mden[:, 0, :], ALU.mult, ALU.max))
            link(dve.tensor_tensor(mden[:, 1, :], mden[:, 1, :], mcol[:, :, 1, r], ALU.max))
            link(dve.reciprocal(mden[:, 1, :], mden[:, 1, :]))
            for b in range(TB):
                o = mh[:, b, 256 * h:256 * h + 256]
                if d == 0:
                    ins = dve.tensor_scalar(o, ps[:, bank + b, 0:256], mden[:, 1, b:b + 1], None, ALU.mult)
                else:
                    ins = dve.scalar_tensor_tensor(o, ps[:, bank + b, 0:256], mden[:, 1, b:b + 1], o, ALU.mult, ALU.add)
            ins.then_inc(s["ml_h"], 1)
            if d == 0:
                dve.wait_ge(s["ml_h"], i + 1)

        for i in range(2 * ML_H + 1):
            if i < 2 * ML_H:
                ml_weights(i)
            if i >= 1:
                ml_head(i - 1)
        dve.wait_ge(s["ml_rs"], 1)
        dve.wait_ge(s["o_gain"], 1)
        for h in range(ML_H):
            for b in range(TB):
                v = slice(256 * h, 256 * h + 256)
                ins = dve.scalar_tensor_tensor(mh[:, b, v], mh[:, b, v], mstat[:, b, h:h + 1], mo[:, b, v],
                                               ALU.mult, ALU.mult)
            ins.then_inc(s["ml_y"], 1)
        for g in range(1, 8, 2):
            dve.wait_ge(s["ml_yT"], g + 1)
            dve.tensor_copy(hid[:, 2 * g:2 * g + 2, :].rearrange("p b n -> p (b n)"), ps[:, g, :])\
                .then_inc(s["ml_yT_dve"], 1)
        gated_residual(POS_MOUT + 3, 6, 0)
        normalise(3, 7)
        norm_out(3, coef[:, 1, 1, :], modT[:, 1, 24:32])
        mlp_out_dve(1)
        gated_residual(POS_MLP[1] + 15, 8, 1)

        def gated_out_dve(ev0):
            def body(j, i, t):
                ev = ev0 + j
                dve.wait_ge(s["ev_act"], ev + 1 + i * R)
                dve.tensor_tensor(hid[:, bass.ds(t * 2, 2), :].rearrange("p b n -> p (b n)"), relu[:, j % 4, :],
                                  ps[:, 2 * (ev % 2) + 1, :], ALU.mult).then_inc(s["ev_dve"], 1)
            rounds(dve, FB // 2, body)

        def residual(pos, factor=None):
            dve.wait_ge(w_used[pos % R], pos // R + 1)
            for b in range(TB):
                y = ps[:, 2 * b:2 * b + 2, :].rearrange("p c n -> p (c n)")
                if factor is None:
                    ins = dve.tensor_tensor(x[:, b, :], y, x[:, b, :], ALU.add)
                else:
                    ins = dve.scalar_tensor_tensor(x[:, b, :], y, factor, x[:, b, :], ALU.mult, ALU.add)
            ins.then_inc(s["x_ready"], 1)

        def mixer_dve(l, p0, e0):
            mark = marks["dve"].done
            AV, PV, own = (lambda n: at["act"](n, l)), (lambda n: at["pe"](n, l)), (lambda n: at["dve"](n, l))
            lin = lambda v: v.rearrange("p b n -> p (b n)")
            mats = lambda bank: ps[:, bank:bank + 4, 0:384].rearrange("p b (u n) -> p b u n", n=P)
            four = lambda v: v.rearrange("p (b u) n -> p b u n", b=4)
            every = lambda m: m.unsqueeze(1).unsqueeze(1).to_broadcast([P, 4, HP, P])
            lg = [cols[:, PACK_LB + 3 * i:PACK_LB + 3 * i + 3] for i in range(2)]
            link(dve.tensor_tensor(lbc[:, 0, :], lg[0], lg[1], ALU.max))
            dve.tensor_tensor(lbc[:, 1, :], lg[0], lbc[:, 0, :], ALU.subtract)
            mark(dve.tensor_tensor(lbc[:, 2, :], lg[1], lbc[:, 0, :], ALU.subtract), "lb_arg")
            tile_out(p0 + O_MIX, e0 + E_MIX, lin(cpT[:, 2:4, :]))
            tile_out(p0 + O_MIX + 1, e0 + E_MIX + 1, lin(cpT[:, 6:8, :]))
            dve.wait_ge(s["act_mix"], AV("lb_exp"))
            link(dve.tensor_tensor(lbc[:, 3, :], lbc[:, 1, :], lbc[:, 2, :], ALU.add))
            link(dve.reciprocal(lbc[:, 3, :], lbc[:, 3, :]))
            dve.tensor_tensor(lbc[:, 4, :], lbc[:, 1, :], lbc[:, 3, :], ALU.mult)
            link(dve.tensor_tensor(lbc[:, 5, :], lbc[:, 2, :], lbc[:, 3, :], ALU.mult))
            run = lbc[:, 4, :]
            if l == 1:
                link(dve.tensor_tensor(lbc[:, 6, :], lbc[:, 4, :], lbc[:, 5, :], ALU.add))
                run = lbc[:, 6, :]
            link(dve.tensor_tensor(lbc[:, 6, :], run, lbc[:, 4, :], ALU.subtract))
            link(dve.tensor_scalar(lbc[:, 6, :], lbc[:, 6, :], 0.0, None, ALU.max))
            dve.tensor_scalar(lbc[:, 7, :], lbc[:, 6, :], -1.0, 1.0, ALU.mult, ALU.add)
            dve.wait_ge(s["ev_act"], e0 + E_MIX + 2)
            dve.wait_ge(s["ev_dve"], e0 + E_MIX + 2)
            z, zc = aa(53, 2), aa(55, 2)
            link(dve.tensor_tensor(z, cpT[:, 2:4, :], cpT[:, 4:6, :], ALU.mult))
            for j in range(2):
                ins = dve.tensor_scalar(zc[:, j, :], z[:, j, :], pc("conv_w", 4 + j), pc("conv_b", j), ALU.mult, ALU.add)
            link(ins)
            for k in (1, 2):
                for j in range(2):
                    ins = dve.scalar_tensor_tensor(zc[:, j, k:L], z[:, j, 0:L - k], pc("conv_w", 2 * (2 - k) + j),
                                                   zc[:, j, k:L], ALU.mult, ALU.add)
                link(ins)
            dve.tensor_tensor(hid[:, 0:2, :], cpT[:, 0:2, :], zc, ALU.mult)
            dve.memset(flat(hh(8, 6)), 0.0)
            tile_out(p0 + O_MIX + 2, e0 + E_MIX + 2, lin(cpT[:, 10:12, :]))
            dve.wait_ge(s["ev_act"], e0 + E_MIX + 3)
            dve.wait_ge(s["ev_dve"], e0 + E_MIX + 3)
            fT, kT, qT = cpT[:, 9:12, :], cpT[:, 9:12, :], cpT[:, 6:9, :]
            link(dve.tensor_scalar(hgA, fT, -1.0, 80.0, ALU.mult, ALU.min))
            link(dve.tensor_scalar(hgB, hgA, 40.0, None, ALU.min))
            link(dve.tensor_scalar(hgA, hgA, 40.0, 0.0, ALU.subtract, ALU.max))
            mark(dve.scalar_tensor_tensor(lin(hgC), lin(fT), -1.0, lin(fT), ALU.mult, ALU.min), "hg_in")
            for t in (3, 4):
                tile_out(p0 + O_MIX + t, e0 + E_MIX + t, lin(cpT[:, 4 * t + 2:4 * t + 4, :]))
            dve.wait_ge(s["act_mix"], AV("hg_exp"))
            for j in range(HP):
                ins = dve.scalar_tensor_tensor(hgB[:, j, :], hgB[:, j, :], lbc[:, 6, j:j + 1], hgD[:, j, :],
                                               ALU.mult, ALU.add)
            mark(ins, "hg_mix")
            link(dve.scalar_tensor_tensor(lin(hgC), lin(fT), 0.0, lin(hgC), ALU.min, ALU.subtract))
            link(dve.tensor_tensor(hgA, hgA, hgC, ALU.add))
            dve.wait_ge(s["act_mix"], AV("hg_k"))
            for j in range(HP):
                ins = dve.tensor_scalar(kT[:, j, :], hgK[0][:, j, :], lbc[:, 7, j:j + 1], None, ALU.mult)
            for t in (5, 6):
                tile_out(p0 + O_MIX + t, e0 + E_MIX + t, lin(cpT[:, 4 * t + 2:4 * t + 4, :]))
            dve.wait_ge(s["ev_dve"], e0 + E_MIX + 7)
            dve.sem_inc(s["ev_dve"], 1)
            dve.wait_ge(s["act_mix"], AV("hg_ln"))
            link(dve.tensor_tensor(hgA, hgA, hgB, ALU.add))
            for j in range(HP):
                ins = dve.tensor_tensor_scan(hgB[:, j, :], ones[:, 0:1].to_broadcast([P, L]), hgA[:, j, :], 0.0,
                                             ALU.mult, ALU.add)
            link(ins)
            E = (hgD, hgC)
            halves = lambda v, m: lin(v).rearrange("p (i u r) -> p i u r", u=2, r=m)

            def diff(n):
                m = LEVELS[n]
                b, o = halves(hgB, m), halves(E[n % 2], m)
                if n >= 2:
                    dve.wait_ge(s["dve_mix"], own(f"qk{LEVELS[n - 2]}"))
                mid = b[:, :, 0, m - 1:m].to_broadcast([P, HP * L // (2 * m), m])
                dve.tensor_tensor(o[:, :, 1, :], b[:, :, 1, :], mid, ALU.subtract)
                mark(dve.tensor_tensor(o[:, :, 0, :], mid, b[:, :, 0, :], ALU.subtract), f"diff{m}")

            def att(m, bank):
                dve.wait_ge(s["pe_mix"], PV(f"level{m}"))
                if m < 64:
                    dve.wait_ge(s["dve_mix"], own(f"att{2 * m or 1}"))
                mask = LV_MASK[m] if m else ident[:, :]
                mark(dve.copy_predicated(four(hgAtt), every(i32(mask)), mats(bank)), f"att{m}")

            diff(0)
            for n, m in enumerate(LEVELS):
                if n + 1 < len(LEVELS):
                    diff(n + 1)
                if n == 2:
                    dve.wait_ge(s["pe_mix"], PV(f"level{LEVELS[0]}"))
                dve.wait_ge(s["act_mix"], AV(f"exp{m}"))
                e = halves(E[n % 2], m)
                dve.tensor_tensor(halves(hgQ[n % 2], m)[:, :, 1, :], halves(qT, m)[:, :, 1, :], e[:, :, 1, :], ALU.mult)
                mark(dve.tensor_tensor(halves(hgK[n % 2], m)[:, :, 0, :], halves(kT, m)[:, :, 0, :], e[:, :, 0, :],
                                       ALU.mult), f"qk{m}")
                if n == 2:
                    dve.wait_ge(s["ev_act"], e0 + E_MIX + 8)
                    pr = cpT[:, 18:29, :]
                    t8 = xnf.rearrange("p (b n) -> p b n", n=L)
                    for d, v in ((t8, pr[:, 0:8, :]), (hT[:, 0:3, :], pr[:, 8:11, :])):
                        dve.tensor_scalar(d[:, :, 0], v[:, :, 0], -1.0, None, ALU.mult)
                        ins = dve.tensor_tensor(d[:, :, 1:L], v[:, :, 0:L - 1], v[:, :, 1:L], ALU.subtract)
                    link(ins)
                    for j in range(11):
                        d = t8[:, j, :] if j < 8 else hT[:, j - 8, :]
                        ins = dve.scalar_tensor_tensor(pr[:, j, :], d, pc("rwkv_mu", j), pr[:, j, :], ALU.mult, ALU.add)
                    mark(ins, "shifted")
                if n >= 2:
                    att(LEVELS[n - 1], 4 * ((n - 1) % 2))
            att(1, 4)
            att(0, 0)
            rT, kr, vT = cpT[:, 18:21, :], cpT[:, 21:24, :], cpT[:, 24:27, :]
            dve.wait_ge(s["dve_mix"], own("shifted"))
            for j in range(HP):
                ins = dve.tensor_scalar(rwKK[:, j, :], kr[:, j, :], pc("rwkv_k_k", j), None, ALU.mult)
            mark(ins, "kk_raw")
            dve.wait_ge(s["act_mix"], AV("hg_rs"))
            mark(dve.tensor_tensor(lin(hgA), psf[:, 3072:3840], lin(hgD), ALU.mult), "o_norm")
            dve.wait_ge(s["dve_mix"], own("o_norm"))
            for j in range(HP):
                ins = dve.scalar_tensor_tensor(hid[:, 2 + j, :], hgA[:, j, :], pc("hgrn_norm", j), hgSG[:, j, :],
                                               ALU.mult, ALU.mult)
            mark(ins, "y_hg")
            dve.wait_ge(s["act_mix"], AV("sig"))
            for j in range(HP):
                for c in range(2):
                    t = slice(c * P, (c + 1) * P)
                    ins = dve.tensor_tensor_scan(rwS[:, j, t], ones[:, 0:1].to_broadcast([P, P]), rwSig[:, j, t], 0.0,
                                                 ALU.mult, ALU.add)
            link(ins)
            S4 = lin(rwS).rearrange("p (u n) -> p u n", n=P)
            link(dve.tensor_tensor(lin(rwSc).rearrange("p (u n) -> p u n", n=P), S4,
                                   S4[:, :, 63:64].to_broadcast([P, 2 * HP, P]), ALU.subtract))
            mark(dve.tensor_tensor(lin(rwEX), lin(rwSc), lin(rwSig), ALU.subtract), "centred")
            for j in range(HP):
                ins = dve.tensor_scalar(rwT1[:, j, :], rwA[:, j, :], 1.0, pc("rwkv_k_a", j), ALU.subtract, ALU.mult)
            link(ins)
            link(dve.scalar_tensor_tensor(lin(kr), lin(rwT1), 1.0, lin(kr), ALU.add, ALU.mult))
            for j in range(HP):
                ins = dve.scalar_tensor_tensor(rwT1[:, j, :], kr[:, j, :], pc("rwkv_r_k", j), rT[:, j, :],
                                               ALU.mult, ALU.mult)
            mark(ins, "rk")
            dve.wait_ge(s["pe_mix"], PV("kk_ss"))
            mark(dve.tensor_scalar(lin(rwT0), psf[:, 0:768], 1e-24, None, ALU.max), "kk_ss")
            dve.wait_ge(s["act_mix"], AV("decays"))
            dve.tensor_tensor(rwScal[:, 3:6], rwScal[:, 0:3], rt_[:, :, P - 1], ALU.mult)
            link(dve.tensor_tensor(kh_, kr, rwEN, ALU.mult))
            dve.tensor_tensor(rt_, rt_, rT, ALU.mult)
            dve.wait_ge(s["act_mix"], AV("kk_norm"))
            link(dve.reciprocal(lin(rwT0), lin(rwT0)))
            link(dve.tensor_tensor(rwKK, rwKK, rwT0, ALU.mult))
            link(dve.tensor_tensor(bh_, rwKK, rwA, ALU.mult))
            dve.tensor_tensor(bh_, bh_, rwEN, ALU.mult)
            dve.wait_ge(s["pe_mix"], PV("bonus"))
            dve.tensor_tensor(lin(rwBonus), psf[:, 1024:1792], lin(vT), ALU.mult)
            mark(dve.scalar_tensor_tensor(lin(at_), lin(rwKK), -1.0, lin(rwEX), ALU.mult, ALU.mult), "operands")
            dve.wait_ge(s["pe_mix"], PV("Lab"))
            mark(dve.tensor_tensor(four(iN), mats(4), every(m_bdT), ALU.mult), "Lab")
            dve.wait_ge(s["pool_mix"], l + 1)
            dve.wait_ge(s["pe_mix"], PV("LakT"))
            mark(dve.copy_predicated(four(LakT), every(i32(m_su)), mats(0)), "LakT")
            dve.wait_ge(s["act_mix"], AV("LabT"))
            link(dve.tensor_tensor(four(iNT), four(LabT), every(m_bd), ALU.mult))
            dve.wait_ge(s["pe_mix"], PV("LrbT"))
            dve.copy_predicated(four(LrbT), every(i32(m_iu)), mats(4))
            dve.tensor_tensor(four(iX), four(iN), every(ident[:, :]), ALU.add)
            dve.tensor_tensor(four(iXT), four(iNT), every(ident[:, :]), ALU.add)
            dve.wait_ge(s["pe_mix"], PV("LrkT"))
            mark(dve.copy_predicated(four(LrkT), every(i32(m_iu)), mats(0)), "base")
            dve.wait_ge(s["dve_mix"], own("base"))
            for p in range(3):
                if p < 2:
                    dve.wait_ge(s["pe_mix"], PV(f"NT{p}"))
                    mark(dve.tensor_copy(four(iNT), mats(4)), f"NT{p}")
                dve.wait_ge(s["pe_mix"], PV(f"dX{p}"))
                dve.tensor_tensor(four(iX), four(iX), mats(0), ALU.add)
                dve.wait_ge(s["pe_mix"], PV(f"dXT{p}"))
                mark(dve.tensor_tensor(four(iXT), four(iXT), mats(4), ALU.add), f"XT{p}")
                dve.wait_ge(s["dve_mix"], own(f"XT{p}"))
            mark(dve.tensor_tensor(four(iN), four(LabT), every(LV_MASK[16]), ALU.mult), "B0")
            for p in range(3):
                dve.wait_ge(s["pe_mix"], PV(f"W{p}"))
                if p < 2:
                    mark(dve.tensor_tensor(four(iN), four(LabT), every(LV_MASK[32 << p]), ALU.mult), f"B{p + 1}")
                    dve.wait_ge(s["pe_mix"], PV(f"mX{p}"))
                    dve.tensor_tensor(four(iX), four(iX), mats(0), ALU.add)
                dve.wait_ge(s["pe_mix"], PV(f"mXT{p}"))
                mark(dve.tensor_tensor(four(iXT), four(iXT), mats(4), ALU.add), f"mXT{p}")
                dve.wait_ge(s["dve_mix"], own(f"mXT{p}"))
            dve.wait_ge(s["pe_mix"], PV("state"))
            mark(dve.tensor_tensor(rwState, ps[:, 2, 0:192].rearrange("p (j n) -> p j n", n=64),
                                   rwScal[:, 3:6].unsqueeze(2).to_broadcast([P, HP, 64]), ALU.mult), "state")
            dve.wait_ge(s["pe_mix"], PV("mean"))
            mark(dve.scalar_tensor_tensor(lin(bh_), psf[:, 0:768], -1.0 / 64, lin(at_), ALU.mult, ALU.add), "y_centred")
            dve.wait_ge(s["act_mix"], AV("y_rs"))
            y = hid[:, 5:8, :]
            for j in range(HP):
                ins = dve.scalar_tensor_tensor(y[:, j, :], bh_[:, j, :], pc("rwkv_ln_w", j), rt_[:, j, :],
                                               ALU.mult, ALU.mult)
            link(ins)
            for j in range(HP):
                ins = dve.scalar_tensor_tensor(y[:, j, :], y[:, j, :], pc("rwkv_ln_b", j), rwBonus[:, j, :],
                                               ALU.add, ALU.add)
            link(ins)
            mark(dve.tensor_tensor(y, y, rwG, ALU.mult), "y_rw")

        def attention_dve(l, p0, e0):
            for b in range(2, 4):
                dve.wait_ge(s["mem_T"], 4 * l + b + 1)
                for u in range(2):
                    k = 2 * b + u
                    ins = dve.tensor_scalar(memT[:, k, :], ps[:, 4 + b, u * L:(u + 1) * L], pc("mem_norm", k), None,
                                            ALU.mult)
            ins.then_inc(s["memT_dve"], 1)
            for t in range(2):
                tile_out(p0 + O_K + t, e0 + E_K + t, flat(xkT[:, 4 * t + 2:4 * t + 4, :]))
            for t in range(2):
                tile_out(p0 + O_V + t, e0 + E_V + t, xv[:, 1, 512 * t:512 * t + 512])
            normalise(6 + 4 * l, 11 + 4 * l)
            norm_out(6 + 4 * l, pc("xattn_norm", 0, 8), None)
            for t in range(2):
                tile_out(p0 + O_Q + t, e0 + E_Q + t, flat(xqT[:, 4 * t + 2:4 * t + 4, :]))
            for h in range(4):
                dve.wait_ge(s["xa_s"], 4 * l + h + 1)
                link(dve.tensor_reduce(xM[:, h, 0:2], ps[:, 4 + h, :].rearrange("p (b n) -> p b n", b=2), AX.X, ALU.max,
                                       negate=True))
                dve.tensor_scalar(xM[:, h, 0:2], xM[:, h, 0:2], 1.0 / 16, None, ALU.mult).then_inc(s["xa_max"], 1)
            for h in range(4):
                dve.wait_ge(s["xa_exp"], 4 * l + h + 1)
                link(dve.reciprocal(xM[:, h, 2:4], xM[:, h, 2:4]))
                for b in range(TB):
                    ins = dve.tensor_scalar(xP[:, h, b, :], xP[:, h, b, :], xM[:, h, 2 + b:3 + b], None, ALU.mult)
                ins.then_inc(s["xa_p"], 1)
            for h in (1, 3):
                dve.wait_ge(s["xa_pT"], 4 * l + h + 1)
                dve.tensor_copy(flat(xPT[:, h, :, :]), ps[:, h, :]).then_inc(s["xa_pT_dve"], 1)
            for h in (1, 3):
                dve.wait_ge(s["xa_o"], 4 * l + h + 1)
                dve.tensor_copy(flat(hid[:, 2 * h:2 * h + 2, :]), ps[:, 4 + h, :]).then_inc(s["xa_y_dve"], 1)

        for l in range(2):
            p0, e0 = POS_C + C_TILES * l, EV_C + C_EVS * l
            dve.wait_ge(s["c_cols_T"], l + 1)
            dve.tensor_copy(cols[:, 0:PACK_N], ps[:, 0, 0:PACK_N]).then_inc(s["c_cols"], 1)
            normalise(4 + 4 * l, 9 + 4 * l)
            dve.wait_ge(s["c_cols"], l + 1)
            norm_out(4 + 4 * l, pc("ffn1_norm", 0, 8), None)
            gated_out_dve(e0 + E_F1)
            if l == 0:
                dve.wait_ge(s["mem_ss"], 1)
                for b in range(TB):
                    ins = dve.tensor_scalar(memn[:, b, :], memn[:, b, :], stat[:, 10 + b:11 + b], None, ALU.mult)
                ins.then_inc(s["mem_xn"], 1)
            residual(p0 + O_F1O + 5, 0.5)
            normalise(5 + 4 * l, 10 + 4 * l)
            norm_out(5 + 4 * l, pc("mix_norm", 0, 8), None)
            mixer_dve(l, p0, e0)
            residual(p0 + O_MO + 1)
            attention_dve(l, p0, e0)
            residual(p0 + O_WO + 1)
            normalise(7 + 4 * l, 12 + 4 * l)
            norm_out(7 + 4 * l, pc("ffn2_norm", 0, 8), None)
            gated_out_dve(e0 + E_F2)
            residual(p0 + O_F2O + 5, 0.5)
        dve.wait_ge(s["ssq"], 17)
        dve.wait_ge(s["final_in"], 16)
        for b in range(TB):
            ins = dve.scalar_tensor_tensor(xn[:, b, :], x[:, b, :], stat[:, 2 + b:3 + b], gains[:, 0, :],
                                           ALU.mult, ALU.mult)
        ins.then_inc(s["out_ready"], 1)


def kernel(**inputs):
    import numpy as np
    from contextlib import ExitStack
    from concourse import bacc
    from concourse.bass_utils import run_bass_kernel_spmd

    nc = bacc.Bacc("TRN2", target_bir_lowering=False, num_devices=1)
    arrays, aps = {}, {}
    for name in inputs:
        v = np.ascontiguousarray(inputs[name])
        arrays["in_" + name] = v
        aps[name] = nc.dram_tensor("in_" + name, v.shape, mybir.dt.from_np(v.dtype), kind="ExternalInput").ap()
    out = nc.dram_tensor("out_x", (1, L, D), F32, kind="ExternalOutput").ap()
    with ExitStack() as ctx:
        build(nc, ctx, aps, out[0])
    r = run_bass_kernel_spmd(nc, [arrays], core_ids=[0])
    return r.results[0]["out_x"]
```

```python
import concourse.bass as bass
from concourse import mybir

F32 = mybir.dt.float32
I32 = mybir.dt.int32
ALU = mybir.AluOpType
ACT = mybir.ActivationFunctionType
AX = mybir.AxisListType

P = 128
L = 256
TB = L // P
D = 1024
DB = D // P
FF = 4 * D
NEG = -1.0e30
EPS = 1e-6
R = 4
SLOT = 4096

SSD_H = 16
CONV_B = 12
NA_H, NA_D = 16, 64
ML_H, ML_DV = 8, 256

ADA_T = 6 * D // 512
ADA_0 = 4
POS_ZX = [4, 6, 8, 10, 12]
POS_DT = 14
POS_QK = [16, 18, 20, 21]
POS_V = [22, 23]
POS_AOUT = 36
POS_MLP = [40, 73]
POS_MQK = 56
POS_MG = POS_MQK + 4
POS_MVO = POS_MG + 1
POS_MOUT = POS_MVO + 8
POS_C = 89
C_TILES = 52

EV_ZX, EV_DT, EV_QK, EV_V = 0, 5, 6, 10
EV_MLP = [12, 33]
EV_MQK = 20
EV_MG = 24
EV_MVO = 25
EV_C = 41

O_F1, O_F1O, O_MIX, O_K, O_MO, O_V, O_Q, O_WO, O_F2, O_F2O = 0, 11, 17, 25, 27, 29, 31, 33, 35, 46
E_F1, E_MIX, E_K, E_V, E_Q, E_F2, C_EVS = 0, 11, 19, 21, 23, 25, 36
FB = 22
PACK = {}
for _name, _n in (("ffn1_norm", 8), ("mix_norm", 8), ("xattn_norm", 8), ("mem_norm", 8), ("ffn2_norm", 8),
                  ("conv_w", 6), ("conv_b", 2), ("hgrn_norm", 3), ("rwkv_mu", 11), ("rwkv_w0", 3), ("rwkv_a0", 3),
                  ("rwkv_k_k", 3), ("rwkv_k_a", 3), ("rwkv_r_k", 3), ("rwkv_ln_w", 3), ("rwkv_ln_b", 3)):
    PACK[_name] = (sum(n for _, n in PACK.values()), _n)
PACK_LB = 83
PACK_N = 89
LEVELS = (128, 64, 32, 16, 8, 4, 2, 1)
RW_C = 0.606531
HP = 3

PE_MARKS = [f"level{m}" for m in LEVELS[:-2]] + ["tokens"] + [f"level{m}" for m in LEVELS[-2:]] + \
    ["level0", "hg_o", "hg_ss", "low_rank", "tokens2", "kk_ss", "bonus", "bk_tok", "LabT", "Lab", "LakT", "LrbT", "LrkT"] + \
    [f"{k}{p}_{h}" for p in range(3) for ks in ((("N", "NT") if p < 2 else ("N",)), ("dX", "dXT")) for h in range(2)
     for k in ks] + \
    [f"{k}{p}_{h}" for p in range(3) for ks in (("W",), (("mX", "mXT") if p < 2 else ("mXT",))) for h in range(2)
     for k in ks] + \
    ["Z0", "P0", "state", "y0", "Z1", "P1", "y1", "mean", "var"]
ACT_MARKS = ["lb_exp", "hg_exp", "hg_k", "hg_ln", "exp128", "exp64", "exp32", "hg_g", "att2_evac", "exp16", "exp8",
             "exp4", "exp2", "exp1", "i_tok", "low_in", "hg_sq", "hg_rms", "sig", "gate", "v_tok", "kk_sq", "decays",
             "kk_norm", "bk_tok", "LabT"] + [f"{k}{p}_{h}" for k in ("N", "W") for p in range(3) for h in range(2)] + \
    ["Z0", "P0", "Z1", "P1", "y", "y_sq", "y_rms"]
DVE_MARKS = ["lb_arg", "hg_in", "hg_mix", "diff128", "diff64", "qk128", "diff32", "qk64", "diff16", "qk32",
             "att64", "diff8", "qk16", "att32", "diff4", "qk8", "att16", "diff2", "qk4", "att8", "diff1", "qk2",
             "att4", "qk1", "shifted", "att2", "att1", "att0", "kk_raw", "o_norm", "y_hg", "centred", "rk", "kk_ss",
             "operands", "Lab", "LakT", "base"] + \
    [n for p in range(3) for n in ([f"NT{p}_0", f"NT{p}_1"] if p < 2 else []) + [f"XT{p}_0", f"XT{p}_1"]] + ["B0"] + \
    [n for p in range(3) for n in ([f"B{p + 1}"] if p < 2 else []) + [f"mXT{p}_0", f"mXT{p}_1"]] + \
    ["state", "y_centred", "y_rw"]


def loaded(pos):
    gated = lambda q: q >= POS_C and ((q - POS_C) % C_TILES < O_F1O or O_F2 <= (q - POS_C) % C_TILES < O_F2O)
    return 16 * sum(2 if gated(q) else 1 for q in range(pos % R, pos + 1, R))


def pos_ada(l, t):
    return 24 + t if l == 1 else t if t < ADA_0 else 2 * t - 3


def ada_on_vector(l, t):
    return t >= ADA_0 if l == 0 else t % 2 == 0


class Marks:

    def __init__(self, sem, names):
        self.sem, self.names, self.k = sem, list(names), 0

    def at(self, name, l):
        return l * len(self.names) + self.names.index(name) + 1

    def done(self, ins, name):
        assert self.names[self.k % len(self.names)] == name, (self.names[self.k % len(self.names)], name)
        self.k += 1
        ins.then_inc(self.sem, 1)


def build(nc, ctx, a, out):

    def sb(name, shape, dt=F32):
        return nc.alloc_sbuf_tensor(name, shape, dt)

    s = {}

    def sem(*names):
        for n in names:
            s[n] = nc.alloc_semaphore(n)

    sem("const", "packs", "pack_zero", "small", "x_in", "cols_T", "cols", "cond",
        "dve_chain", "act_chain", "pool_chain", "mod_in",
        "ada_ev", "ada_sum", "mod_rows", "mod_first", "mod_T", "coef", "gain_in", "gate_bc", "gate_done",
        "x_ready", "ssq", "y_ssq", "y_half", "xn_ready", "xn_T", "hT_act", "hT_dve",
        "ev_act", "ev_dve", "hid",
        "bias_mm", "bias_ev",
        "dt_ln", "U_ready", "U_T", "U_cols", "alog_e",
        "conv", "conv_silu", "z_silu", "X_T", "X_ev", "CB", "ss_arg", "ss_exp", "ss_M", "ss_y", "y_gated",
        "y_sq", "y_sum", "y_rs", "y_ssd",
        "na_s", "na_max", "na_exp", "na_p", "na_pT", "na_pT_ev", "na_o", "na_y",
        "gate_small", "perm", "g_IF", "g_neg", "g_ln", "g_rows2", "g_T", "g_cols", "head_gain",
        "o_sig", "o_gain", "ml_arg", "ml_S", "ml_exp", "ml_M", "ml_num", "ml_h", "ml_rs", "ml_y", "ml_yT",
        "ml_yT_act", "ml_yT_dve",
        "stored")
    sem("masks", "c_packs", "c_lowrank", "c_cols_T", "c_cols", "mem_in", "mem_ss", "mem_xn", "mem_T", "memT_act",
        "memT_dve", "final_in", "pe_mix", "act_mix", "dve_mix", "pool_mix", "xa_s", "xa_max", "xa_exp", "xa_p", "xa_pT",
        "xa_pT_act", "xa_pT_dve", "xa_o", "xa_y_act", "xa_y_dve", "out_ready")
    w_loaded = [nc.alloc_semaphore(f"w_loaded{i}") for i in range(R)]
    w_used = [nc.alloc_semaphore(f"w_used{i}") for i in range(R)]

    ring = sb("ring", [P, R, SLOT])
    x = sb("x", [P, TB, D])
    hT = sb("hT", [P, DB, L])
    xn = sb("xn", [P, TB, D])
    hid = sb("hid", [P, FF // P, L])
    gains = sb("gains", [P, 2, D])
    modrow = sb("modrow", [P, 3, 512])
    modpack = sb("modpack", [48, P])
    modT = sb("modT", [P, 2, 48])
    coef = sb("coef", [P, 2, 2, DB])
    cols = sb("cols", [P, 248])
    stat = sb("stat", [P, 16])
    ident = sb("ident", [P, P])
    ones = sb("ones", [P, P])
    tri = sb("tri", [P, 2, P])
    eps_c = sb("eps_c", [P, 1])
    dirs = sb("dirs", [32, 2])
    small = sb("small", [P, 16])
    Urow = sb("Urow", [P, L])
    Ucol = sb("Ucol", [P, TB, 2, 32])
    arena = sb("arena", [P, 68, L])
    ps = nc.alloc_psum_tensor("ps", [P, 8, 512], F32)

    def ring_k(slot, n):
        return ring[:, slot, 0:8 * n].rearrange("p (k n) -> p k n", n=n)

    def ring_o(slot, kb):
        return ring[:, slot, 0:kb * D].rearrange("p (k n) -> p k n", n=D)

    pT = arena[:, 0:36, :]
    v_na = arena[:, 36:44, :].rearrange("p b n -> p (b n)").rearrange("p (t n) -> p t n", t=TB)
    biasf = arena[:, 44:68, :].rearrange("p b n -> p (b n)").rearrange("p (h n) -> p h n", h=NA_H)
    cvT = hid[:, 16:28, :]
    ada_acc = [hid[:, 8 + 2 * i:10 + 2 * i, :].rearrange("p b n -> p (b n)") for i in range(2)]
    ADA_BANK = [4, 2]
    relu = xn[:, :, :].rearrange("p b (u n) -> p (b u) n", u=2)
    X = xn[:, :, :]
    ssE = arena[:, 8:11, :].rearrange("p b n -> p (b n)").rearrange("p (u n) -> p u n", u=2)
    ssM = arena[:, 11:14, :].rearrange("p b n -> p (b n)").rearrange("p (u n) -> p u n", u=2)
    naS = arena[:, 14:18, :].rearrange("p b n -> p (b n)").rearrange("p (u n) -> p u n", u=2)
    naPT = arena[:, 18:20, :].rearrange("p b n -> p (b n)").rearrange("p (c t) -> p c t", c=2)
    dtw = hid[0:32, 28:32, :]
    naM = sb("naM", [P, 2, 4])
    packs = [hid[0:96, 0, 0:P], hid[0:124, 1, 0:P], hid[0:28, 2, 0:P]]
    rpb_pack = hid[0:96, 3, 0:64]
    rpbT = hid[0:64, 4, 0:96]
    band = hid[0:64, 5, 0:191]
    wmask = hid[:, 6, 0:64]

    C_NG, C_CW, C_CB, C_SN, C_C = 96, 160, 220, 232, 240
    cT = cols[:, C_C:C_C + 8]

    aa = lambda lo, n: arena[:, lo:lo + n, :]
    flat = lambda v: v.rearrange("p b n -> p (b n)")
    hh = lambda lo, n: hid[:, lo:lo + n, :]
    mk = aa(60, 8).rearrange("p b (u n) -> p (b u) n", u=2)
    LV_MASK = {m: mk[:, i, :] for i, m in enumerate((1, 2, 4, 8, 16, 32, 64))}
    m_bd, m_bdT, m_su, m_iu, blk = (mk[:, 7 + i, :] for i in range(5))
    gn_eps = mk[:, 12, 0:1]
    i32 = lambda v: v.bitcast(I32)
    cpT = aa(0, 29)
    hgA, hgB, hgC, hgD = aa(41, 3), aa(44, 3), aa(47, 3), aa(50, 3)
    hgQ = [aa(29, 3), aa(32, 3)]
    hgK = [aa(35, 3), aa(38, 3)]
    hgS = aa(56, 3)
    hgAtt = hh(8, 6).rearrange("p b (u n) -> p (b u) n", u=2)
    hgAtt2 = hh(14, 3).rearrange("p b (u n) -> p (b u) n", u=2)
    i_tok = flat(hh(17, 3)).rearrange("p (b n) -> p b n", b=TB)
    hgSG = hh(20, 3)
    lbc = hh(23, 1)[:, 0, 0:24].rearrange("p (u n) -> p u n", n=3)
    rwS = aa(29, 3)
    rwSig, rwA = hh(24, 3), hh(27, 3)
    rwEN, rwKK = hT[:, 0:3, :], hT[:, 3:6, :]
    rwT0, rwT1 = aa(41, 3), aa(44, 3)
    v_tok = flat(aa(53, 3)).rearrange("p (b n) -> p b n", b=TB)
    bk_tok = flat(aa(56, 3)).rearrange("p (b n) -> p b n", b=2)
    rwG, rwBonus = aa(47, 3), aa(50, 3)
    six = lambda v: v.rearrange("p b (u n) -> p (b u) n", u=2)
    LakT, LrbT, LrkT = six(aa(0, 6)), six(aa(6, 6)), six(aa(12, 6))
    at_, bh_, kh_, rt_ = aa(29, 3), aa(32, 3), aa(35, 3), aa(38, 3)
    iX, iXT, iN, iNT, LabT = six(hh(8, 6)), six(hh(14, 6)), six(hh(20, 6)), six(hh(26, 6)), six(aa(41, 6))
    xnf = flat(xn[:, :, :])
    rwP = xnf[:, 0:768].rearrange("p (c n) -> p c n", c=2)
    rwZ = xnf[:, 768:1536].rearrange("p (c n) -> p c n", c=2)
    rwState = xnf[:, 1536:1728].rearrange("p (j n) -> p j n", j=HP)
    rwScal = xnf[:, 1728:1740]
    rwSc, rwEX = (xnf[:, 768 * i:768 * i + 768].rearrange("p (b n) -> p b n", n=L) for i in range(2))
    psf = ps[:, :, :].rearrange("p b n -> p (b n)")
    memT, xkT, xqT = aa(0, 8), aa(8, 8), aa(24, 8)
    xv = flat(aa(16, 8)).rearrange("p (b n) -> p b n", b=TB)
    xP = aa(32, 8).rearrange("p (h b) n -> p h b n", b=TB)
    xPT = aa(40, 8).rearrange("p (h c) n -> p h c n", c=2)
    xM = aa(48, 1)[:, 0, 0:16].rearrange("p (h n) -> p h n", h=4)
    memn = gains
    packC = [modrow[0:PACK_N, i, 0:P] for i in range(2)]
    lowA, lowG = modrow[:, 0, P:512], modrow[:, 1, P:512]
    pc = lambda name, k=0, n=None: cols[:, PACK[name][0] + k:PACK[name][0] + k + (n or 1)]

    marks = {"pe": Marks(s["pe_mix"], PE_MARKS), "act": Marks(s["act_mix"], ACT_MARKS), "dve": Marks(s["dve_mix"], DVE_MARKS)}
    at = {e: m.at for e, m in marks.items()}
    kpn = lambda v: v.rearrange("(k p) n -> p k n", p=P)

    w_in = a["ab_w_in"][0].rearrange("(k p) n -> p k n", p=P)
    ada_w = [a["ada_w"][i].rearrange("(k p) n -> p k n", p=P) for i in range(2)]
    w1 = [a["mlp_w1"][i].rearrange("(k p) n -> p k n", p=P) for i in range(2)]
    w2 = [a["mlp_w2"][i].rearrange("(k p) n -> p k n", p=P) for i in range(2)]
    w_outA = a["ab_w_out"][0].rearrange("(k p) n -> p k n", p=P)
    QKV0 = 2592
    w_ml = a["ml_w_in"][0].rearrange("(k p) n -> p k n", p=P)
    w_outB = a["ml_w_out"][0].rearrange("(k p) n -> p k n", p=P)

    mqT, mkT = arena[:, 0:8, :], arena[:, 8:16, :]
    af = arena[:, :, :].rearrange("p b n -> p (b n)")
    mv = af[:, 4096:4096 + TB * ML_H * 257].rearrange("p (b h n) -> p b h n", b=TB, h=ML_H)
    mo = af[:, 8212:8212 + 4096].rearrange("p (b n) -> p b n", b=TB)
    mh = af[:, 12310:12310 + 4096].rearrange("p (b n) -> p b n", b=TB)
    gw = hid[0:32, 16:22, :]
    hf = hid[:, 22:28, :].rearrange("p b n -> p (b n)")
    mE = hf[:, 0:768].rearrange("p (u n) -> p u n", u=2)
    mM = hf[:, 768:1536].rearrange("p (u n) -> p u n", u=2)
    gate_bias = sb("gate_bias", [32, 1])
    dirsB = sb("dirsB", [16, 2])
    perm = hid[0:32, 29, 0:32].rearrange("p (w n) -> p w n", w=2)
    mtot = sb("mtot", [16, 1])
    nMrow = Urow[0:16, :]
    mcol = hid[:, 30, 0:64].rearrange("p (b w n) -> p b w n", b=TB, w=2)
    mden = hid[:, 30, 80:84].rearrange("p (w n) -> p w n", w=2)
    mstat = hid[:, 30, 64:80].rearrange("p (b n) -> p b n", b=TB)

    def rounds(eng, n, body):
        full = n // R
        if full > 1:
            with eng.Fori(0, full) as i:
                for j in range(R):
                    body(j, i, i * R + j)
        rest = range(full * R if full > 1 else 0, n)
        for t in rest:
            body(t, 0, t)

    ctx.enter_context(nc.allow_non_contiguous_dma(reason="a few hundred parameters of one head or row each"))
    block = ctx.enter_context(nc.Block())

    @block.sync
    def _(sp):
        def load(pos, i, dst, src, skip_wait=False):
            if pos >= R or not isinstance(i, int):
                sp.wait_ge(w_used[pos % R], pos // R + i)
            sp.dma_start(dst, src).then_inc(w_loaded[pos % R], 16)

        def cols_tiles(pos, n, w, c0=0):
            rounds(sp, n, lambda j, i, t: load(pos + j, i, ring_k((pos + j) % R, 512),
                                               w[:, :, bass.ds(t * 512 + c0, 512)]))

        def out_tiles(pos, n, w):
            rounds(sp, n, lambda j, i, t: load(pos + j, i, ring_o((pos + j) % R, 4),
                                               w[:, bass.ds(t * 4, 4), :]))

        for t in range(R):
            load(t, 0, ring_k(t, 512), ada_w[0][:, :, t * 512:t * 512 + 512])
        def one_tile(pos, w, c0, n=512):
            load(pos, 0, ring_k(pos % R, n), w[:, :, c0:c0 + n])

        first = [(pos, w_in, 512 * t) for t, pos in enumerate(POS_ZX)] + [(POS_DT, w_in, 2560, 32)] + \
            [(pos, w_in, QKV0 + 512 * t) for t, pos in enumerate(POS_QK)] + \
            [(pos, w_in, QKV0 + 2048 + 512 * t) for t, pos in enumerate(POS_V)] + \
            [(pos_ada(0, t), ada_w[0], 512 * t) for t in range(ADA_0, ADA_T)]
        for tile in sorted(first, key=lambda f: f[0]):
            one_tile(*tile)
        cols_tiles(pos_ada(1, 0), ADA_T, ada_w[1])
        out_tiles(POS_AOUT, 4, w_outA)
        cols_tiles(POS_MLP[0], 8, w1[0])
        out_tiles(POS_MLP[0] + 8, 8, w2[0])
        cols_tiles(POS_MQK, 4, w_ml)
        load(POS_MG, 0, ring_k(POS_MG % R, 32), w_ml[:, :, 6144:6176])
        cols_tiles(POS_MVO, 8, w_ml, 2048)
        out_tiles(POS_MOUT, 4, w_outB)
        cols_tiles(POS_MLP[1], 8, w1[1])
        out_tiles(POS_MLP[1] + 8, 8, w2[1])
        def gated_tiles(pos, w):
            v = w.rearrange("(k p) (g n) -> p k g n", p=P, g=2)

            def one(j, i, t):
                sp.wait_ge(w_used[(pos + j) % R], (pos + j) // R + i)
                for g in range(2):
                    sp.dma_start(ring_k((pos + j) % R, 512)[:, :, 256 * g:256 * g + 256],
                                 v[:, :, g, bass.ds(t * 256, 256)]).then_inc(w_loaded[(pos + j) % R], 16)
            rounds(sp, FB // 2, one)

        def down_tiles(pos, w):
            out_tiles(pos, 5, w)
            load(pos + 5, 0, ring_o((pos + 5) % R, 2), w[:, 20:22, :])

        for l in range(2):
            p0 = POS_C + C_TILES * l
            gated_tiles(p0 + O_F1, a["ffn1_w_in_2"][l])
            down_tiles(p0 + O_F1O, kpn(a["ffn1_w_out_2"][l]))
            cols_tiles(p0 + O_MIX, 7, kpn(a["w_mix_in_2"][l]))
            load(p0 + O_MIX + 7, 0, ring_k((p0 + O_MIX + 7) % R, P), kpn(a["w_mix_in_2"][l])[:, :, 3584:3712])
            cols_tiles(p0 + O_K, 2, kpn(a["xattn_wkv_2"][l]))
            out_tiles(p0 + O_MO, 2, kpn(a["w_mix_out_2"][l]))
            cols_tiles(p0 + O_V, 2, kpn(a["xattn_wkv_2"][l]), D)
            cols_tiles(p0 + O_Q, 2, kpn(a["xattn_wq_2"][l]))
            out_tiles(p0 + O_WO, 2, kpn(a["xattn_wo_2"][l]))
            gated_tiles(p0 + O_F2, a["ffn2_w_in_2"][l])
            down_tiles(p0 + O_F2O, kpn(a["ffn2_w_out_2"][l]))
        for b in range(TB):
            sp.wait_ge(s["out_ready"], b + 1)
            sp.dma_start(out[b * P:(b + 1) * P, :], xn[:, b, :]).then_inc(s["stored"], 16)
        sp.wait_ge(s["stored"], 32)

    @block.gpsimd
    def _(pool):
        chain = [0]

        def link(ins):
            chain[0] += 1
            ins.then_inc(s["pool_chain"], 1)
            pool.wait_ge(s["pool_chain"], chain[0])

        def keep(t, pattern, base, mult, fill, cmp=ALU.is_ge):
            link(pool.affine_select(out=t, in_=t, compare_op=cmp, fill=fill, base=base, pattern=pattern,
                                    channel_multiplier=mult))

        pool.memset(rpb_pack, 0.0).then_inc(s["pack_zero"], 1)
        pool.wait_ge(s["pack_zero"], 1)
        link(pool.memset(ident[:, :], 0.0))
        link(pool.memset(ones[:, :], 1.0))
        link(pool.memset(Urow[:, :], 0.0))
        link(pool.memset(tri[:, :, :], 0.0))
        link(pool.memset(eps_c[:, :], EPS))
        link(pool.memset(dirs[:, 0:1], -1.0))
        link(pool.memset(dirs[:, 1:2], 1.0))
        link(pool.memset(band, 0.0))
        link(pool.memset(wmask, 0.0))
        keep(ident[:, :], [[-1, P]], 0, 1, 1.0, ALU.not_equal)
        keep(tri[:, 0, :], [[1, P]], 0, -1, NEG)
        keep(tri[:, 1, :], [[-1, P]], 0, 1, NEG)
        keep(dirs[:, 0:1], [[0, 1]], -16, 1, 1.0)
        keep(dirs[:, 1:2], [[0, 1]], -16, 1, 0.0)
        link(pool.memset(dirsB[:, 0:1], -1.0))
        link(pool.memset(dirsB[:, 1:2], 1.0))
        keep(dirsB[:, 0:1], [[0, 1]], -8, 1, 1.0)
        keep(dirsB[:, 1:2], [[0, 1]], -8, 1, 0.0)
        for half in range(2):
            keep(band[32 * half:32 * half + 31, :], [[1, 191]], -78 - 64 * half, 1, 1.0, ALU.not_equal)
        for half in range(2):
            v = wmask[64 * half:64 * half + 64, :]
            keep(v[:, 0:48], [[1, 48]], 8, -1, NEG)
            keep(v[:, 16:64], [[-1, 48]], 7 - 16, 1, NEG)
        pool.sem_inc(s["const"], 1)
        for l in range(2):
            pool.wait_ge(s["ada_ev"], ADA_T * (l + 1))
            for c in range(1 - l, 3):
                for q in range(4):
                    pool.dma_start(modpack[16 * c + 4 * q:16 * c + 4 * q + 4, :],
                                   modrow[32 * q:32 * q + 1, c, :].rearrange("o (r n) -> o r n", n=P))\
                        .then_inc(s["mod_rows"], 16)
        pool.wait_ge(s["x_ready"], 4)
        pool.memset(mv[:, :, :, 256:257], 1.0).then_inc(s["g_cols"], 1)
        pool.wait_ge(s["o_sig"], 1)
        pool.wait_ge(s["head_gain"], 16)
        for b in range(TB):
            ins = pool.tensor_tensor(mo[:, b, :], mo[:, b, :], xn[:, :, :].rearrange("p b n -> p (b n)"), ALU.mult)
        ins.then_inc(s["o_gain"], 1)
        pool.wait_ge(s["x_ready"], 6)
        for m, t in LV_MASK.items():
            v = t.rearrange("p (i u r) -> p i u r", u=2, r=m)
            link(pool.memset(t, 0.0))
            link(pool.memset(v[:, :, 1, :], 1.0))
            keep(v[:, :, 1, :], [[-2 * m, 64 // m], [0, m]], 0, 1, 0.0)
            keep(v[:, :, 1, :], [[2 * m, 64 // m], [0, m]], m - 1, -1, 0.0)
        for t in (m_bd, m_bdT, m_su, m_iu, blk):
            link(pool.memset(t, 1.0))
        keep(m_bd, [[1, P]], -1, -1, 0.0)
        keep(m_bd, [[-16, 8], [0, 16]], 0, 1, 0.0)
        keep(m_bdT, [[-1, P]], -1, 1, 0.0)
        keep(m_bdT, [[16, 8], [0, 16]], 15, -1, 0.0)
        keep(m_su, [[1, P]], -1, -1, 0.0)
        keep(m_iu, [[1, P]], 0, -1, 0.0)
        keep(blk[:, 0:64], [[0, 64]], 63, -1, 0.0)
        keep(blk[:, 64:128], [[0, 64]], -64, 1, 0.0)
        link(pool.memset(gn_eps, 64e-5))
        pool.sem_inc(s["masks"], 1)
        for l in range(2):
            pool.wait_ge(s["dve_mix"], at["dve"]("y_hg", l))
            pool.memset(flat(aa(0, 18)), 0.0).then_inc(s["pool_mix"], 1)

    @block.scalar
    def _(act):
        chain = [0]

        def link(ins):
            chain[0] += 1
            ins.then_inc(s["act_chain"], 1)
            act.wait_ge(s["act_chain"], chain[0])

        def rsqrt(dst, src, scale):
            link(act.activation(dst, src, ACT.Ln, bias=eps_c[0:dst.shape[0], :], scale=scale))
            return act.activation(dst, dst, ACT.Exp, scale=-0.5)

        def load_mod_bias(l):
            v = a["ada_b"][l].rearrange("(c q n) -> q c n", c=3, q=4)
            for q in range(4):
                act.dma_start(modrow[32 * q:32 * q + 1, :, :], v[q:q + 1]).then_inc(s["mod_in"], 16)

        act.dma_start(packs[0], a["ada_b"].rearrange("l (r n) -> (l r) n", n=P)).then_inc(s["packs"], 16)
        act.dma_start(packs[1][0:64], a["norm_g"].rearrange("l s (r n) -> (l s r) n", n=P)).then_inc(s["packs"], 16)
        act.dma_start(packs[1][64:124], a["ab_conv_w"][0].rearrange("t (r n) -> (t r) n", n=P)).then_inc(s["packs"], 16)
        act.dma_start(packs[2][0:12], a["ab_conv_b"][0].rearrange("(r n) -> r n", n=P)).then_inc(s["packs"], 16)
        act.dma_start(packs[2][12:20], a["ab_ssd_norm"][0].rearrange("(r n) -> r n", n=P)).then_inc(s["packs"], 16)
        act.dma_start(packs[2][20:28], a["c"][0].rearrange("(r n) -> r n", n=P)).then_inc(s["packs"], 16)
        act.wait_ge(s["pack_zero"], 1)
        rpb = a["ab_rpb"][0]
        for h in range(NA_H):
            act.dma_start(rpb_pack[6 * h:6 * h + 6, 0:31], rpb[h, 5:11, :]).then_inc(s["packs"], 16)
            act.dma_start(rpb_pack[6 * h:6 * h + 6, 32:63], rpb[h, 4:10, :]).then_inc(s["packs"], 16)
        load_mod_bias(0)
        act.dma_start(x[:, :, :], a["x"][0].rearrange("(b p) n -> p b n", p=P)).then_inc(s["x_in"], 16)
        act.dma_start(small[0:32, 0:1], a["ab_dt_bias"].rearrange("o d h -> (d h) o")).then_inc(s["small"], 16)
        act.dma_start(small[0:32, 1:2], a["ab_a_log"].rearrange("o d h -> (d h) o")).then_inc(s["small"], 16)
        for u in range(2):
            act.dma_start(small[64 * u:64 * u + 64, 4:12],
                          a["ab_d_skip"].rearrange("o (j u) -> u o j", u=2)[u].to_broadcast([64, 8]))\
                .then_inc(s["small"], 16)
        for i in range(2):
            act.dma_start(gains[:, i, :], a["norm_g"][0, 1 + 2 * i:2 + 2 * i, :].to_broadcast([P, D]))\
                .then_inc(s["gain_in"], 16)
        act.wait_ge(s["cols"], 1)
        act.activation(cT, cT, ACT.Silu).then_inc(s["cond"], 1)

        def table():
            link(act.activation(stat[:, 12:13], eps_c[:, :], ACT.Sqrt))

        def norm_stats(site, gated=None):
            table()
            for b in range(TB):
                if gated is not None:
                    if b == 0:
                        act.wait_ge(s["y_half"], site)
                    else:
                        act.wait_ge(w_used[gated % R], gated // R + 1)
                    link(act.activation(xn[:, b, :], ps[:, 2 * b:2 * b + 2, :], ACT.Square, accum_out=stat[:, 4 + b:5 + b]))
                    act.activation(stat[:, 6 + b:7 + b], stat[:, 4 + b:5 + b], ACT.Sqrt, bias=eps_c[:, :], scale=1.0 / D)\
                        .then_inc(s["y_ssq"], 1)
                if site == 0:
                    act.wait_ge(s["x_in"], 16)
                else:
                    act.wait_ge(s["x_ready"], 2 * site - 1 + b)
                link(act.activation(xn[:, b, :], x[:, b, :], ACT.Square, accum_out=stat[:, b:b + 1]))
                act.activation(stat[:, 2 + b:3 + b], stat[:, b:b + 1], ACT.Sqrt, bias=eps_c[:, :], scale=1.0 / D)\
                    .then_inc(s["ssq"], 1)

        def norm_out(site, A, B):
            for b in range(2):
                act.wait_ge(s["xn_T"], 4 * site + 2 * b + 1)
                for u in range(2):
                    k = 2 * b + u
                    ins = act.activation(hT[:, k, :], ps[:, 4 + b, u * L:(u + 1) * L], ACT.Identity,
                                         scale=A[:, k:k + 1], bias=B[:, k:k + 1] if B is not None else 0.0)
            ins.then_inc(s["hT_act"], 1)

        def tile_out(pos, ev, dst):
            act.wait_ge(w_used[pos % R], pos // R + 1)
            act.activation(dst, ps[:, 2 * (ev % 2), 0:512], ACT.Copy).then_inc(s["ev_act"], 1)

        def chan(t0, t):
            return pT[:, t0 + 4 * t:t0 + 4 * t + 2, :].rearrange("p b n -> p (b n)")

        norm_stats(0)
        act.wait_ge(s["ada_ev"], ADA_0)
        for q in range(4):
            act.dma_start(modpack[4 * q:4 * q + 4, :], modrow[32 * q:32 * q + 1, 0, :].rearrange("o (r n) -> o r n", n=P))\
                .then_inc(s["mod_first"], 16)
        act.wait_ge(s["coef"], 1)
        norm_out(0, coef[:, 0, 0, :], modT[:, 0, 0:8])
        for t in range(5):
            tile_out(POS_ZX[t], EV_ZX + t, chan(0, t))
        act.wait_ge(s["small"], 64)
        act.activation(small[0:32, 2:3], small[0:32, 1:2], ACT.Exp).then_inc(s["alog_e"], 1)
        act.wait_ge(w_used[POS_DT % R], POS_DT // R + 1)
        act.activation(dtw[:, 0, :], ps[0:32, 2 * (EV_DT % 2), 0:L], ACT.Identity, bias=small[0:32, 0:1])\
            .then_inc(s["ev_act"], 1)
        act.wait_ge(s["ev_dve"], EV_DT + 1)
        link(act.activation(dtw[:, 1, :], dtw[:, 1, :], ACT.Exp))
        act.activation(dtw[:, 1, :], dtw[:, 1, :], ACT.Ln, bias=1.0).then_inc(s["dt_ln"], 1)
        for t in range(4):
            tile_out(POS_QK[t], EV_QK + t, chan(20, t))
            if t > 0:
                act.wait_ge(s["conv"], t)
                act.activation(cvT[:, 4 * t - 4:4 * t, :], cvT[:, 4 * t - 4:4 * t, :], ACT.Silu)\
                    .then_inc(s["conv_silu"], 1)
        for t in range(2):
            tile_out(POS_V[t], EV_V + t, v_na[:, 0, 512 * t:512 * t + 512])
        act.wait_ge(s["ev_dve"], EV_ZX + 5)
        act.activation(pT[:, 0:8, :], pT[:, 0:8, :], ACT.Silu).then_inc(s["z_silu"], 1)
        for b in range(2):
            act.wait_ge(s["X_T"], b + 1)
            act.activation(X[:, 0, 512 * b:512 * b + 512], ps[:, 2 + b, :], ACT.Copy).then_inc(s["X_ev"], 1)
        act.wait_ge(s["mod_first"], 64)
        act.wait_ge(s["mod_rows"], 128)
        act.wait_ge(s["gate_done"], 1)
        load_mod_bias(1)
        act.wait_ge(s["U_cols"], 1)
        for i in range(2 * SSD_H):
            h, d = i // 2, i % 2
            r = d * 16 + h
            n0 = L if d == 0 else P
            act.wait_ge(s["ss_arg"], i + 1)
            if i >= 2:
                act.wait_ge(s["ss_M"], i - 1)
            act.activation(ssE[:, i % 2, 0:n0], ps[:, i % 2, 0:n0], ACT.Exp, bias=Ucol[:, 0, 0, r:r + 1])
            act.activation(ssE[:, i % 2, n0:384], ps[:, i % 2, n0:384], ACT.Exp, bias=Ucol[:, 1, 0, r:r + 1])\
                .then_inc(s["ss_exp"], 1)
        act.wait_ge(s["y_gated"], 8)
        act.activation(cvT[:, 0:8, :], pT[:, 0:8, :], ACT.Square).then_inc(s["y_sq"], 1)
        act.wait_ge(s["y_sum"], 1)
        rsqrt(cvT[:, 8, :], ps[:, 4, 0:L], 1.0 / D).then_inc(s["y_rs"], 1)

        def na_probs(h):
            act.wait_ge(s["na_max"], h + 1)
            for b in range(TB):
                ins = act.activation(naS[:, h % 2, b * L:(b + 1) * L], naS[:, h % 2, b * L:(b + 1) * L], ACT.Exp,
                                     bias=naM[:, h % 2, b:b + 1], accum_out=naM[:, h % 2, 2 + b:3 + b])
            ins.then_inc(s["na_exp"], 1)

        def na_transposed(h):
            act.wait_ge(s["na_pT"], h + 1)
            if h >= 1:
                act.wait_ge(s["na_o"], h)
            act.activation(naPT[:, :, :], ps[:, 2 + h % 2, :], ACT.Copy).then_inc(s["na_pT_ev"], 1)

        for h in range(NA_H + 1):
            if h < NA_H:
                na_probs(h)
            if h >= 1:
                na_transposed(h - 1)

        def mlp_out_act(l):
            def body(j, i, t):
                pos, ev = POS_MLP[l] + j, EV_MLP[l] + j
                act.wait_ge(w_used[pos % R], pos // R + 1 + i)
                act.activation(relu[:, j, :], ps[:, 2 * (ev % 2), :], ACT.Relu).then_inc(s["ev_act"], 1)
            rounds(act, 8, body)

        norm_stats(1, POS_AOUT + 3)
        act.wait_ge(s["coef"], 2)
        norm_out(1, coef[:, 0, 1, :], modT[:, 0, 24:32])
        mlp_out_act(0)
        norm_stats(2, POS_MLP[0] + 15)

        act.wait_ge(s["x_ready"], 4)
        for i in range(2):
            act.dma_start(gains[:, i, :], a["norm_g"][1, 1 + 2 * i:2 + 2 * i, :].to_broadcast([P, D]))\
                .then_inc(s["gain_in"], 16)
        act.dma_start(gate_bias[:, :], a["ml_gate_b"].rearrange("o g h -> (g h) o")).then_inc(s["gate_small"], 16)
        norm_out(2, coef[:, 1, 0, :], modT[:, 1, 0:8])
        act.wait_ge(s["hT_dve"], 3)
        act.dma_start(xn[:, :, :].rearrange("p b n -> p (b n)"), a["ml_head_norm"].to_broadcast([P, 2 * D]))\
            .then_inc(s["head_gain"], 16)
        for t in range(4):
            tile_out(POS_MQK + t, EV_MQK + t, arena[:, 4 * t:4 * t + 2, :].rearrange("p b n -> p (b n)"))
        act.wait_ge(s["gate_small"], 16)
        act.wait_ge(w_used[POS_MG % R], POS_MG // R + 1)
        act.activation(gw[:, 0, :], ps[0:32, 2 * (EV_MG % 2), 0:L], ACT.Identity, bias=gate_bias[:, :])\
            .then_inc(s["ev_act"], 1)
        act.wait_ge(s["g_cols"], 1)
        for t in range(4):
            tile_out(POS_MVO + t, EV_MVO + t, mv[:, 0, 2 * t:2 * t + 2, 0:256])
            if t == 1:
                act.wait_ge(s["g_neg"], 1)
                link(act.activation(gw[0:16, 2, :], gw[0:16, 2, :], ACT.Exp))
                act.activation(gw[0:16, 2, :], gw[0:16, 2, :], ACT.Ln, bias=1.0).then_inc(s["g_ln"], 1)
        for t in range(4):
            tile_out(POS_MVO + 4 + t, EV_MVO + 4 + t, mo[:, 0, 512 * t:512 * t + 512])
        act.wait_ge(s["g_T"], 1)
        v = ps[:, 4, 0:64].rearrange("p (b w r) -> p b w r", b=2, w=2)
        act.activation(mcol[:, :, 0, :], v[:, :, 0, :], ACT.Copy)
        act.activation(mcol[:, :, 1, :], v[:, :, 1, :], ACT.Exp).then_inc(s["g_cols"], 1)
        act.wait_ge(s["ev_dve"], EV_MVO + 8)
        act.wait_ge(s["ev_act"], EV_MVO + 8)
        act.activation(mo[:, :, :], mo[:, :, :], ACT.Sigmoid).then_inc(s["o_sig"], 1)
        act.wait_ge(s["g_cols"], 2)

        def head_squares(h):
            act.wait_ge(s["ml_h"], 2 * h + 2)
            for b in range(TB):
                ins = act.activation(hid[:, 28 + 3 * b, :], mh[:, b, 256 * h:256 * h + 256], ACT.Square, accum_out=mstat[:, b, h:h + 1])
            link(ins)

        for i in range(2 * ML_H):
            h, d = i // 2, i % 2
            r, n0 = d * 8 + h, (L if d == 0 else P)
            act.wait_ge(s["ml_arg"], i + 1)
            if i >= 2:
                act.wait_ge(s["ml_M"], i - 1)
            act.activation(mE[:, i % 2, 0:n0], ps[:, i % 2, 0:n0], ACT.Exp, bias=mcol[:, 0, 0, r:r + 1])
            act.activation(mE[:, i % 2, n0:384], ps[:, i % 2, n0:384], ACT.Exp, bias=mcol[:, 1, 0, r:r + 1])\
                .then_inc(s["ml_exp"], 1)
            if i >= 5 and i % 2 == 1:
                head_squares((i - 5) // 2)
        head_squares(6)
        head_squares(7)
        rsqrt(mstat[:, :, :], mstat[:, :, :], 1.0 / ML_DV).then_inc(s["ml_rs"], 1)
        for g in range(0, 8, 2):
            act.wait_ge(s["ml_yT"], g + 1)
            act.activation(hid[:, 2 * g:2 * g + 2, :], ps[:, g, :], ACT.Copy).then_inc(s["ml_yT_act"], 1)
        norm_stats(3, POS_MOUT + 3)
        norm_out(3, coef[:, 1, 1, :], modT[:, 1, 24:32])
        for l in range(2):
            for name, (r, n) in PACK.items():
                v = a[name + "_2"][l]
                v = v.rearrange("t (r n) -> (t r) n", n=P) if name == "conv_w" else \
                    v.rearrange("(r u) n -> r (u n)", u=2) if name == "rwkv_r_k" else v.rearrange("(r n) -> r n", n=P)
                act.dma_start(packC[l][r:r + n], v).then_inc(s["c_packs"], 16)
            act.dma_start(packC[l][PACK_LB:PACK_N], a["hgrn_lb_logits_2"].rearrange("l (r n) -> (l r) n", n=P))\
                .then_inc(s["c_packs"], 16)

        def load_low_rank(l):
            act.dma_start(lowA[0:64], a["rwkv_w2_2"][l]).then_inc(s["c_lowrank"], 16)
            act.dma_start(lowA[64:128], a["rwkv_a2_2"][l]).then_inc(s["c_lowrank"], 16)
            act.dma_start(lowG, a["rwkv_g2_2"][l]).then_inc(s["c_lowrank"], 16)

        load_low_rank(0)
        mlp_out_act(1)

        def gated_out_act(ev0, pos0):
            def body(j, i, t):
                pos, ev = pos0 + j, ev0 + j
                act.wait_ge(w_used[pos % R], pos // R + 1 + i)
                act.activation(relu[:, j % 4, :], ps[:, 2 * (ev % 2), :], ACT.Silu).then_inc(s["ev_act"], 1)
            rounds(act, FB // 2, body)

        def mixer_act(l, p0, e0):
            mark = marks["act"].done
            DV, PV = (lambda n: at["dve"](n, l)), (lambda n: at["pe"](n, l))
            act.wait_ge(s["dve_mix"], DV("lb_arg"))
            mark(act.activation(lbc[:, 1:3, :], lbc[:, 1:3, :], ACT.Exp), "lb_exp")
            def proj_out(t):
                tile_out(p0 + O_MIX + t, e0 + E_MIX + t, flat(cpT[:, 4 * t:4 * t + 2, :]))

            def decay(n):
                m, v = LEVELS[n], (hgD, hgC)[n % 2]
                act.wait_ge(s["dve_mix"], DV(f"diff{m}"))
                mark(act.activation(v, v, ACT.Exp), f"exp{m}")

            for t in range(4):
                proj_out(t)
            act.wait_ge(s["dve_mix"], DV("hg_in"))
            act.activation(hgB, hgB, ACT.Exp)
            act.activation(hgD, hgA, ACT.Exp, scale=-1.0)
            link(act.activation(hgC, hgC, ACT.Exp))
            mark(act.activation(hgC, hgC, ACT.Ln, bias=1.0), "hg_exp")
            act.activation(hgS, cpT[:, 9:12, :], ACT.Sigmoid, scale=-1.0)
            mark(act.activation(cpT[:, 6:9, :], cpT[:, 6:9, :], ACT.Silu), "hg_k")
            act.wait_ge(s["dve_mix"], DV("hg_mix"))
            mark(act.activation(hgB, hgB, ACT.Ln), "hg_ln")
            for n in range(3):
                decay(n)
            proj_out(4)
            act.wait_ge(s["ev_act"], e0 + E_MIX + 5)
            act.wait_ge(s["ev_dve"], e0 + E_MIX + 4)
            mark(act.activation(hgSG, cpT[:, 15:18, :], ACT.Silu), "hg_g")
            act.wait_ge(s["pe_mix"], PV(f"level{LEVELS[0]}"))
            mark(act.activation(hgAtt2.rearrange("p (h j) n -> p h (j n)", h=2),
                                ps[:, 4:8, :].rearrange("p (h b) n -> p h b n", b=2)[:, :, 0, 0:384], ACT.Copy), "att2_evac")
            decay(3)
            decay(4)
            proj_out(5)
            decay(5)
            proj_out(6)
            decay(6)
            pos, ev = p0 + O_MIX + 7, e0 + E_MIX + 7
            act.wait_ge(w_used[pos % R], pos // R + 1)
            act.activation(cpT[:, 28, :], ps[:, 2 * (ev % 2), 0:L], ACT.Copy).then_inc(s["ev_act"], 1)
            decay(7)
            act.wait_ge(s["pe_mix"], PV("tokens"))
            for b in range(TB):
                ins = act.activation(i_tok[:, b, :], ps[:, b, 0:384], ACT.Copy)
            mark(ins, "i_tok")
            act.wait_ge(s["dve_mix"], DV("shifted"))
            act.activation(cpT[0:64, 27, :], cpT[0:64, 27, :], ACT.Tanh)
            mark(act.activation(cpT[:, 28, :], cpT[:, 28, :], ACT.Sigmoid), "low_in")
            act.wait_ge(s["pe_mix"], PV("hg_o"))
            mark(act.activation(flat(hgC), psf[:, 3072:3840], ACT.Square), "hg_sq")
            table()
            act.wait_ge(s["pe_mix"], PV("hg_ss"))
            mark(act.activation(flat(hgD), psf[:, 0:768], ACT.Sqrt, bias=eps_c[:, :], scale=1.0 / 64), "hg_rms")
            act.wait_ge(s["pe_mix"], PV("low_rank"))
            for j in range(HP):
                act.activation(rwSig[:, j, :], psf[:, 1024 + j * L:1024 + (j + 1) * L], ACT.Sigmoid,
                               bias=pc("rwkv_w0", j))
                ins = act.activation(rwA[:, j, :], psf[:, 2048 + j * L:2048 + (j + 1) * L], ACT.Sigmoid,
                                     bias=pc("rwkv_a0", j))
            mark(ins, "sig")
            act.wait_ge(s["dve_mix"], DV("y_hg"))
            act.activation(flat(rwG), psf[:, 2816:3584], ACT.Copy)
            if l == 0:
                load_low_rank(1)
            act.wait_ge(s["pe_mix"], PV("tokens2"))
            mark(act.activation(v_tok[:, 0, :], ps[:, 0, 0:384], ACT.Copy), "gate")
            mark(act.activation(v_tok[:, 1, :], ps[:, 1, 0:384], ACT.Copy), "v_tok")
            act.wait_ge(s["dve_mix"], DV("kk_raw"))
            mark(act.activation(rwT0, rwKK, ACT.Square), "kk_sq")
            act.wait_ge(s["dve_mix"], DV("centred"))
            act.activation(rwEN, rwSc, ACT.Exp, scale=RW_C)
            act.activation(rwScal[:, 0:3], rwS[:, :, 191], ACT.Exp, scale=-RW_C)
            act.activation(rwEX, rwEX, ACT.Exp, scale=-RW_C)
            mark(act.activation(rt_, rwSc, ACT.Exp, scale=-RW_C), "decays")
            act.wait_ge(s["dve_mix"], DV("kk_ss"))
            mark(act.activation(rwT0, rwT0, ACT.Sqrt), "kk_norm")
            act.wait_ge(s["pe_mix"], PV("bk_tok"))
            act.activation(bk_tok[:, 0, :], ps[:, 6, 0:384], ACT.Copy)
            mark(act.activation(bk_tok[:, 1, :], ps[:, 7, 0:384], ACT.Copy), "bk_tok")
            mats = lambda bank: ps[:, bank:bank + 4, 0:384]
            four = lambda v: v.rearrange("p (b u) n -> p b (u n)", b=4)
            half_mats = lambda bank, h: ps[:, bank + 2 * h:bank + 2 * h + 2, 0:384]
            half = lambda v, h: v[:, 6 * h:6 * h + 6, :].rearrange("p (b u) n -> p b (u n)", b=2)
            act.wait_ge(s["pe_mix"], PV("LabT"))
            mark(act.activation(four(LabT), mats(0), ACT.Copy), "LabT")
            for p in range(3):
                for h in range(2):
                    act.wait_ge(s["pe_mix"], PV(f"NT{p}_{h}" if p < 2 else f"N2_{h}"))
                    mark(act.activation(half(iN, h), half_mats(0, h), ACT.Copy), f"N{p}_{h}")
            for p in range(3):
                for h in range(2):
                    act.wait_ge(s["pe_mix"], PV(f"W{p}_{h}"))
                    mark(act.activation(half(iNT, h), half_mats(0, h), ACT.Copy), f"W{p}_{h}")
            for c in range(2):
                act.wait_ge(s["pe_mix"], PV(f"Z{c}"))
                mark(act.activation(rwZ[:, c, :].rearrange("p (j h n) -> p h j n", h=2, n=64),
                                    ps[:, 0:6, 0:192].rearrange("p (h b) (j n) -> p h b j n", b=3, n=64)[:, :, 0],
                                    ACT.Copy), f"Z{c}")
                act.wait_ge(s["pe_mix"], PV(f"P{c}"))
                mark(act.activation(rwP[:, c, :], ps[:, 1, 0:384], ACT.Copy), f"P{c}")
            act.wait_ge(s["pe_mix"], PV("y1"))
            mark(act.activation(flat(at_), psf[:, 3072:3840], ACT.Copy), "y")
            table()
            act.wait_ge(s["dve_mix"], DV("y_centred"))
            mark(act.activation(kh_, bh_, ACT.Square), "y_sq")
            for b in range(2):
                act.wait_ge(s["mem_T"], 4 * l + b + 3)
                for u in range(2):
                    k = 4 + 2 * b + u
                    ins = act.activation(memT[:, k, :], ps[:, b, u * L:(u + 1) * L], ACT.Copy, scale=pc("mem_norm", k))
            ins.then_inc(s["memT_act"], 1)
            act.wait_ge(s["pe_mix"], PV("var"))
            mark(act.activation(flat(rt_), psf[:, 3072:3840], ACT.Sqrt, bias=gn_eps, scale=1.0 / 64), "y_rms")
            for t in range(2):
                tile_out(p0 + O_K + t, e0 + E_K + t, flat(xkT[:, 4 * t:4 * t + 2, :]))

        def attention_act(l, p0, e0):
            norm_stats(6 + 4 * l)
            for t in range(2):
                pos = p0 + O_V + t
                act.wait_ge(w_used[pos % R], pos // R + 1)
                act.activation(xv[:, 0, 512 * t:512 * t + 512], ps[:, 4 + 2 * t, :], ACT.Copy).then_inc(s["ev_act"], 1)
            norm_out(6 + 4 * l, pc("xattn_norm", 0, 8), None)
            for t in range(2):
                tile_out(p0 + O_Q + t, e0 + E_Q + t, flat(xqT[:, 4 * t:4 * t + 2, :]))
            for h in range(4):
                act.wait_ge(s["xa_max"], 4 * l + h + 1)
                for b in range(TB):
                    ins = act.activation(xP[:, h, b, :], ps[:, 4 + h, b * L:(b + 1) * L], ACT.Exp, scale=1.0 / 16,
                                         bias=xM[:, h, b:b + 1], accum_out=xM[:, h, 2 + b:3 + b])
                ins.then_inc(s["xa_exp"], 1)
            for h in (0, 2):
                act.wait_ge(s["xa_pT"], 4 * l + h + 1)
                act.activation(flat(xPT[:, h, :, :]), ps[:, h, :], ACT.Copy).then_inc(s["xa_pT_act"], 1)
            for h in (0, 2):
                act.wait_ge(s["xa_o"], 4 * l + h + 1)
                act.activation(flat(hid[:, 2 * h:2 * h + 2, :]), ps[:, 4 + h, :], ACT.Copy).then_inc(s["xa_y_act"], 1)

        for l in range(2):
            p0, e0 = POS_C + C_TILES * l, EV_C + C_EVS * l
            norm_stats(4 + 4 * l, POS_MLP[1] + 15 if l == 0 else None)
            if l == 0:
                act.wait_ge(s["x_ready"], 8)
                act.dma_start(memn[:, :, :], a["mem_2"][0].rearrange("(b p) n -> p b n", p=P)).then_inc(s["mem_in"], 16)
            act.wait_ge(s["c_cols"], l + 1)
            norm_out(4 + 4 * l, pc("ffn1_norm", 0, 8), None)
            gated_out_act(e0 + E_F1, p0 + O_F1)
            if l == 0:
                act.wait_ge(s["mem_in"], 16)
                for b in range(TB):
                    ins = act.activation(flat(hid[:, 24 + 4 * b:28 + 4 * b, :]), memn[:, b, :], ACT.Square,
                                         accum_out=stat[:, 8 + b:9 + b])
                link(ins)
                act.activation(stat[:, 10:12], stat[:, 8:10], ACT.Sqrt, bias=eps_c[:, :], scale=1.0 / D)\
                    .then_inc(s["mem_ss"], 1)
            norm_stats(5 + 4 * l)
            norm_out(5 + 4 * l, pc("mix_norm", 0, 8), None)
            mixer_act(l, p0, e0)
            attention_act(l, p0, e0)
            norm_stats(7 + 4 * l)
            norm_out(7 + 4 * l, pc("ffn2_norm", 0, 8), None)
            gated_out_act(e0 + E_F2, p0 + O_F2)
        act.wait_ge(s["memT_act"], 2)
        act.wait_ge(s["memT_dve"], 2)
        act.dma_start(gains[:, 0, :], a["final_norm_2"].unsqueeze(0).to_broadcast([P, D])).then_inc(s["final_in"], 16)
        norm_stats(12)

    @block.tensor
    def _(pe):
        def weights(pos, i=0):
            pe.wait_ge(w_loaded[pos % R], loaded(pos) + i * (loaded(pos) - loaded(pos - R)) if pos >= R else 16)

        def banks_free(ev, i=0):
            if ev >= 2 or not isinstance(i, int):
                pe.wait_ge(s["ev_act"], ev - 1 + i * R)
                pe.wait_ge(s["ev_dve"], ev - 1 + i * R)

        def channel_tile(pos, ev, i=0, src=hT, between=None):
            weights(pos, i)
            banks_free(ev, i)
            w = ring_k(pos % R, 512)
            for m in range(4):
                o = ps[:, 2 * (ev % 2) + m // 2, (m % 2) * L:(m % 2 + 1) * L]
                for k in range(DB):
                    last = pe.matmul(o, w[:, k, m * P:(m + 1) * P], src[:, k, :], start=(k == 0), stop=(k == DB - 1))
                if m == 1 and between is not None:
                    between()
            last.then_inc(w_used[pos % R], 1)

        def token_tile(pos, ev, i=0, src=hT, bank=None):
            weights(pos, i)
            if bank is None:
                banks_free(ev, i)
                bank = 2 * (ev % 2)
            w = ring_k(pos % R, 512)
            for b in range(TB):
                for k in range(DB):
                    last = pe.matmul(ps[:, bank + b, :], src[:, k, b * P:(b + 1) * P], w[:, k, :],
                                     start=(k == 0), stop=(k == DB - 1))
            last.then_inc(w_used[pos % R], 1)

        def out_product(pos, n_k, src, ready):
            tiles = (n_k + 3) // 4
            for t in range(tiles):
                weights(pos + t)
                ready(t)
                w = ring_o((pos + t) % R, 4)
                for b in range(TB):
                    for kb in range(min(4, n_k - 4 * t)):
                        k = 4 * t + kb
                        for c in range(2):
                            last = pe.matmul(ps[:, 2 * b + c, :], src[:, k, b * P:(b + 1) * P],
                                             w[:, kb, c * 512:(c + 1) * 512], start=(k == 0), stop=(k == n_k - 1))
                    if t == tiles - 1 and b == 0:
                        last.then_inc(s["y_half"], 1)
                last.then_inc(w_used[(pos + t) % R], 1)

        def norm_transposes(site, first=None):
            for b in range(TB):
                pe.wait_ge(s["xn_ready"], 2 * site + b + 1)
                for bank in (0, 2, 1, 3):
                    if first is not None and b == 0:
                        first(bank)
                    for u in range(2):
                        k = 2 * bank + u
                        last = pe.transpose(ps[:, 4 + bank, u * L + b * P:u * L + (b + 1) * P],
                                            xn[:, b, k * P:(k + 1) * P], ident[:, :])
                    if b == 1:
                        last.then_inc(s["xn_T"], 1)

        def hT_ready(site):
            pe.wait_ge(s["hT_act"], site + 1)
            pe.wait_ge(s["hT_dve"], site + 1)

        def ada_tile(l, t):
            pos, n = pos_ada(l, t), 12 * l + t
            if n >= 2:
                pe.wait_ge(s["ada_ev"], n - 1)
            q = 32 * (t % 4)
            o = ps[q:q + 1, ADA_BANK[l] + n % 2, :]
            if ada_on_vector(l, t):
                pe.wait_ge(w_used[pos % R], pos // R + 1)
                pe.matmul(o, ones[:, 0:1], ada_acc[n % 4 // 2 if l else n % 2], start=True, stop=True)\
                    .then_inc(s["ada_sum"], 1)
            else:
                weights(pos)
                w = ring_k(pos % R, 512)
                for k in range(DB):
                    last = pe.matmul(o, cT[:, k:k + 1], w[:, k, :], start=(k == 0), stop=(k == DB - 1))
                last.then_inc(w_used[pos % R], 1)

        def mod_columns(l, n=48, bank=4):
            if n == 16:
                pe.wait_ge(s["mod_first"], 64)
            else:
                pe.wait_ge(s["mod_rows"], 16 * (12 * l + 8))
            pe.transpose(ps[:, bank, 0:n], modpack[0:n, :], ident[0:n, 0:n]).then_inc(s["mod_T"], 1)

        def gate_rows(l):
            for i, t in enumerate((4, 5, 10, 11)):
                q, c = 32 * (t % 4), t // 4
                last = pe.matmul(ps[:, i, :], ones[q:q + 1, :], modrow[q:q + 1, c, :], start=True, stop=True)
            last.then_inc(s["gate_bc"], 1)

        def bias_group(g):
            if g >= 2:
                pe.wait_ge(s["bias_ev"], g - 1)
            for u in range(4):
                kc = 4 * g + u
                last = pe.matmul(ps[:, 6 + g % 2, 96 * u:96 * u + 96], band[:, 63 - kc:191 - kc], rpbT,
                                 start=True, stop=True)
            last.then_inc(s["bias_mm"], 1)

        pe.wait_ge(s["const"], 1)
        pe.wait_ge(s["packs"], 16 * (6 + 2 * NA_H))
        o = 0
        for pk in packs:
            n = pk.shape[0]
            pe.transpose(ps[:, 4, o:o + n], pk, ident[0:n, 0:n])
            o += n
        pe.transpose(ps[0:64, 5, 0:96], rpb_pack, ident[0:96, 0:96]).then_inc(s["cols_T"], 1)
        pe.wait_ge(s["cols"], 2)
        pe.wait_ge(s["cond"], 1)
        for g in range(4):
            bias_group(g)
        for t in range(ADA_0):
            ada_tile(0, t)
            bias_group(4 + t)
        norm_transposes(0)
        mod_columns(0, 16, 0)
        hT_ready(0)
        for t in range(5):
            channel_tile(POS_ZX[t], EV_ZX + t)
            if t >= 1:
                ada_tile(0, 3 + t)
            if t < 4:
                bias_group(8 + 2 * t)
                bias_group(9 + 2 * t)
        weights(POS_DT)
        banks_free(EV_DT)
        w = ring_k(POS_DT % R, 32)
        for k in range(DB):
            last = pe.matmul(ps[0:32, 2 * (EV_DT % 2), 0:L], w[:, k, :], hT[:, k, :], start=(k == 0), stop=(k == DB - 1))
        last.then_inc(w_used[POS_DT % R], 1)
        ada_tile(0, 8)
        for t in range(4):
            channel_tile(POS_QK[t], EV_QK + t)
            if t < 3:
                ada_tile(0, 9 + t)
        for t in range(2):
            token_tile(POS_V[t], EV_V + t)
        pe.wait_ge(s["ev_act"], EV_V + 2)
        pe.wait_ge(s["ev_dve"], EV_V + 2)
        pe.wait_ge(s["ada_ev"], ADA_T)
        gate_rows(0)
        pe.wait_ge(s["conv_silu"], 3)
        pe.wait_ge(s["bias_ev"], 16)
        for g in range(2):
            for b in range(TB):
                last = pe.matmul(ps[:, 6 + g, b * L:(b + 1) * L], cvT[:, 8 + g, b * P:(b + 1) * P], cvT[:, 10 + g, :],
                                 start=(b == 0), stop=(b == 1), skip_group_check=True)
        last.then_inc(s["CB"], 1)
        pe.wait_ge(s["gate_done"], 1)
        for b in range(TB):
            for c in range(2):
                for u in range(4):
                    last = pe.transpose(ps[:, (2 + c) if b == 0 else c, u * P:(u + 1) * P],
                                        cvT[:, 4 * c + u, b * P:(b + 1) * P], ident[:, :])
                last.then_inc(s["X_T"], 1)
        pe.wait_ge(s["U_ready"], 2)
        for b in range(TB):
            pe.transpose(ps[:, 5, 64 * b:64 * b + 32], Urow[0:32, b * P:(b + 1) * P], ident[0:32, 0:32])
            last = pe.transpose(ps[:, 5, 64 * b + 32:64 * b + 64], dtw[:, 2, b * P:(b + 1) * P], ident[0:32, 0:32])
        last.then_inc(s["U_T"], 1)
        pe.wait_ge(s["X_ev"], 4)
        mod_columns(0)
        pe.wait_ge(s["coef"], 2)

        def decay_arg(i):
            h, d = i // 2, i % 2
            if i >= 2:
                pe.wait_ge(s["ss_exp"], i - 1)
            sel = ident[:, d * 16 + h:d * 16 + h + 1].to_broadcast([P, P])
            o = ps[:, i % 2, :]
            if d == 0:
                pe.matmul(o[:, 0:L], sel, Urow[:, :], start=True, stop=False, skip_group_check=True)
                pe.matmul(o[:, L:384], sel, Urow[:, P:L], start=False, stop=False, skip_group_check=True)
            else:
                pe.matmul(o[:, 0:P], sel, Urow[:, 0:P], start=True, stop=False, skip_group_check=True)
                pe.matmul(o[:, P:384], sel, Urow[:, :], start=False, stop=False, skip_group_check=True)
            pe.matmul(o[:, 0:P], ident[:, :], tri[:, d, :], start=False, stop=False, skip_group_check=True)
            pe.matmul(o[:, L:384], ident[:, :], tri[:, d, :], start=False, stop=True, skip_group_check=True)\
                .then_inc(s["ss_arg"], 1)

        def ssd_y(i):
            h, d = i // 2, i % 2
            pe.wait_ge(s["ss_M"], i + 1)
            if i % 4 == 0 and i >= 8:
                pe.wait_ge(s["y_gated"], i // 4 - 1)
            rows = slice(64 * (h % 2), 64 * (h % 2) + 64)
            o = ps[rows, 4 + (h // 2) % 2, :]
            xh = [X[:, b, 64 * h:64 * h + 64] for b in range(TB)]
            m = ssM[:, i % 2, :]
            if d == 0:
                pe.matmul(o[:, 0:L], xh[0], m[:, 0:L], start=True, stop=False, skip_group_check=True)
                last = pe.matmul(o[:, P:L], xh[1], m[:, L:384], start=False, stop=False, skip_group_check=True)
            else:
                pe.matmul(o[:, 0:P], xh[0], m[:, 0:P], start=False, stop=False, skip_group_check=True)
                last = pe.matmul(o[:, 0:L], xh[1], m[:, P:384], start=False, stop=True, skip_group_check=True)
            last.then_inc(s["ss_y"], 1)

        t1 = 0
        pe.wait_ge(s["U_cols"], 1)
        for i in range(2 * SSD_H + 1):
            if i < 2 * SSD_H:
                decay_arg(i)
            if i >= 1:
                ssd_y(i - 1)
            if i < 32 and i % 8 in (1, 4, 6):
                ada_tile(1, t1)
                t1 += 1
        pe.wait_ge(s["y_sq"], 1)
        for j in range(DB):
            last = pe.matmul(ps[:, 4, 0:L], ones[:, :], cvT[:, j, :], start=(j == 0), stop=(j == DB - 1))
        last.then_inc(s["y_sum"], 1)
        pe.wait_ge(s["y_rs"], 1)
        pe.wait_ge(s["ada_ev"], 24)

        def na_scores(h):
            if h >= 2:
                pe.wait_ge(s["na_max"], h - 1)
            rows = slice(64 * (h % 2), 64 * (h % 2) + 64)
            for b in range(TB):
                last = pe.matmul(ps[:, h % 2, b * L:(b + 1) * L], pT[rows, 20 + h // 2, b * P:(b + 1) * P],
                                 pT[rows, 28 + h // 2, :], start=(b == 0), stop=(b == 1), skip_group_check=True)
            last.then_inc(s["na_s"], 1)

        def na_transposes(h):
            pe.wait_ge(s["na_p"], h + 1)
            if h >= 2:
                pe.wait_ge(s["na_pT_ev"], h - 1)
            for c in range(2):
                for b in range(TB):
                    last = pe.transpose(ps[:, 2 + h % 2, c * L + b * P:c * L + (b + 1) * P],
                                        naS[:, h % 2, b * L + c * P:b * L + (c + 1) * P], ident[:, :])
            last.then_inc(s["na_pT"], 1)

        def na_out(h):
            pe.wait_ge(s["na_pT_ev"], h + 1)
            if h % 2 == 0 and h >= 4:
                pe.wait_ge(s["na_y"], h // 2 - 1)
            rows = slice(64 * (h % 2), 64 * (h % 2) + 64)
            for c in range(2):
                last = pe.matmul(ps[rows, 4 + (h // 2) % 2, 0:L], v_na[:, c, 64 * h:64 * h + 64], naPT[:, c, :],
                                 start=(c == 0), stop=(c == 1))
            last.then_inc(s["na_o"], 1)

        for h in range(NA_H + 2):
            if h < NA_H:
                na_scores(h)
            if h >= 2:
                na_out(h - 2)
            if 1 <= h <= NA_H:
                na_transposes(h - 1)
        pe.wait_ge(s["y_ssd"], 1)
        pe.wait_ge(s["na_y"], 8)
        mod_columns(1)
        out_product(POS_AOUT, 16, hid, lambda t: None)

        def mlp(l, site):
            norm_transposes(site)
            hT_ready(site)
            rounds(pe, 8, lambda j, i, t: channel_tile(POS_MLP[l] + j, EV_MLP[l] + j, i))
            pe.wait_ge(s["ev_act"], EV_MLP[l] + 8)
            pe.wait_ge(s["ev_dve"], EV_MLP[l] + 8)

            def ready(t):
                pe.wait_ge(s["hid"], 8 * l + t + 1)
            out_product(POS_MLP[l] + 8, 32, hid, ready)

        mlp(0, 1)

        pe.wait_ge(s["x_ready"], 4)
        gate_rows(1)
        norm_transposes(2)
        hT_ready(2)
        pe.wait_ge(s["gate_done"], 2)
        for t in range(4):
            channel_tile(POS_MQK + t, EV_MQK + t)
        weights(POS_MG)
        banks_free(EV_MG)
        w = ring_k(POS_MG % R, 32)
        for k in range(DB):
            last = pe.matmul(ps[0:32, 2 * (EV_MG % 2), 0:L], w[:, k, :], hT[:, k, :], start=(k == 0), stop=(k == DB - 1))
        last.then_inc(w_used[POS_MG % R], 1)
        token_tile(POS_MVO, EV_MVO)
        pe.wait_ge(s["perm"], 4)
        pe.wait_ge(s["ev_act"], EV_MG + 1)
        for w in range(2):
            last = pe.matmul(ps[0:16, 5, w * L:(w + 1) * L], perm[:, w, :], gw[:, 0, :], start=(w == 0), stop=(w == 1),
                             skip_group_check=True)
        last.then_inc(s["g_IF"], 1)
        for t in range(1, 8):
            token_tile(POS_MVO + t, EV_MVO + t)
        pe.wait_ge(s["g_rows2"], 1)
        for b in range(TB):
            pe.transpose(ps[:, 4, 32 * b:32 * b + 16], gw[0:16, 5, b * P:(b + 1) * P], ident[0:16, 0:16])
            last = pe.transpose(ps[:, 4, 32 * b + 16:32 * b + 32], gw[0:16, 3, b * P:(b + 1) * P], ident[0:16, 0:16])
        last.then_inc(s["g_T"], 1)
        pe.wait_ge(s["ev_act"], EV_MVO + 8)
        pe.wait_ge(s["ev_dve"], EV_MVO + 8)

        def ml_arg(i):
            h, d = i // 2, i % 2
            if i >= 2:
                pe.wait_ge(s["ml_exp"], i - 1)
            sel = ident[:, d * 8 + h:d * 8 + h + 1].to_broadcast([P, P])
            o = ps[:, i % 2, :]
            if d == 0:
                pe.matmul(o[:, 0:L], sel, Urow[:, :], start=True, stop=False, skip_group_check=True)
                pe.matmul(o[:, L:384], sel, Urow[:, P:L], start=False, stop=False, skip_group_check=True)
            else:
                pe.matmul(o[:, 0:P], sel, Urow[:, 0:P], start=True, stop=False, skip_group_check=True)
                pe.matmul(o[:, P:384], sel, Urow[:, :], start=False, stop=False, skip_group_check=True)
            pe.matmul(o[:, 0:P], ident[:, :], tri[:, d, :], start=False, stop=False, skip_group_check=True)
            pe.matmul(o[:, L:384], ident[:, :], tri[:, d, :], start=False, stop=True, skip_group_check=True)\
                .then_inc(s["ml_arg"], 1)

        def ml_scores(h):
            if h >= 2:
                pe.wait_ge(s["ml_M"], 2 * h - 2)
            for b in range(TB):
                last = pe.matmul(ps[:, 2 + h % 2, b * L:(b + 1) * L], mkT[:, h, b * P:(b + 1) * P], mqT[:, h, :],
                                 start=(b == 0), stop=(b == 1), skip_group_check=True)
            last.then_inc(s["ml_S"], 1)

        def ml_values(i):
            h, d = i // 2, i % 2
            pe.wait_ge(s["ml_M"], i + 1)
            if i >= 2:
                pe.wait_ge(s["ml_h"], i - 1)
            m = mM[:, i % 2, :]
            o = [ps[:, 4 + 2 * (i % 2) + b, 0:257] for b in range(TB)]
            v = [mv[:, b, h, :] for b in range(TB)]
            if d == 0:
                pe.matmul(o[0], m[:, 0:P], v[0], start=True, stop=True)
                pe.matmul(o[1], m[:, P:L], v[0], start=True, stop=False)
                last = pe.matmul(o[1], m[:, L:384], v[1], start=False, stop=True)
            else:
                pe.matmul(o[0], m[:, 0:P], v[0], start=True, stop=False)
                pe.matmul(o[0], m[:, P:L], v[1], start=False, stop=True)
                last = pe.matmul(o[1], m[:, L:384], v[1], start=True, stop=True)
            last.then_inc(s["ml_num"], 1)

        pe.wait_ge(s["g_cols"], 2)
        for i in range(2 * ML_H + 1):
            if i < 2 * ML_H:
                if i % 2 == 0:
                    ml_scores(i // 2)
                ml_arg(i)
            if i >= 1:
                ml_values(i - 1)
        pe.wait_ge(s["ml_h"], 16)
        for g in range(8):
            pe.wait_ge(s["ml_y"], g + 1)
            for u in range(2):
                for b in range(TB):
                    last = pe.transpose(ps[:, g, u * L + b * P:u * L + (b + 1) * P],
                                        mh[:, b, (2 * g + u) * P:(2 * g + u + 1) * P], ident[:, :])
            last.then_inc(s["ml_yT"], 1)
        pe.wait_ge(s["ml_yT_act"], 4)
        pe.wait_ge(s["ml_yT_dve"], 4)
        out_product(POS_MOUT, 16, hid, lambda t: None)
        mlp(1, 3)

        def gated_ffn(pos, ev):
            rounds(pe, FB // 2, lambda j, i, t: channel_tile(pos + j, ev + j, i))
            pe.wait_ge(s["ev_act"], ev + FB // 2)
            pe.wait_ge(s["ev_dve"], ev + FB // 2)
            out_product(pos + FB // 2, FB, hid, lambda t: None)

        def mats(bank, lhsT, rhs, name):
            for n in range(4 * HP):
                i = 6 * (n % 2) + n // 2
                o = ps[:, bank + i // 3, (i % 3) * P:(i % 3 + 1) * P]
                last = pe.matmul(o, lhsT(i), rhs(i), start=True, stop=True)
            marks["pe"].done(last, name)

        def half_mats(bank, h, lhsT, rhs, name):
            for i in range(6 * h, 6 * h + 6):
                o = ps[:, bank + i // 3, (i % 3) * P:(i % 3 + 1) * P]
                last = pe.matmul(o, lhsT(i), rhs(i), start=True, stop=True)
            marks["pe"].done(last, name)

        def head(v):
            return lambda i: v[64 * (i // 6):64 * (i // 6) + 64, i % 6 // 2, (i % 2) * P:(i % 2 + 1) * P]

        def head_sums(col, src, name):
            for j in range(HP):
                last = pe.matmul(psf[:, col + j * L:col + (j + 1) * L], blk, src[:, j, :], start=True, stop=True)
            marks["pe"].done(last, name)

        def memory_transposes(l, first, bank):
            if l == 0:
                pe.wait_ge(s["mem_xn"], 1)
            for i in range(2):
                for u in range(2):
                    k = 2 * (first + i) + u
                    for b in range(TB):
                        last = pe.transpose(ps[:, bank + i, u * L + b * P:u * L + (b + 1) * P],
                                            memn[:, b, k * P:(k + 1) * P], ident[:, :])
                last.then_inc(s["mem_T"], 1)

        def mixer_pe(l, p0, e0):
            mark = marks["pe"].done
            AV, DV = (lambda n: at["act"](n, l)), (lambda n: at["dve"](n, l))
            def level(n):
                m = LEVELS[n]
                pe.wait_ge(s["dve_mix"], DV(f"qk{m}"))
                q, k = head(hgQ[n % 2]), head(hgK[n % 2])
                if n == 0:
                    for n6 in range(2 * HP):
                        h, j = n6 % 2, n6 // 2
                        last = pe.matmul(ps[:, 4 + 2 * h, j * P:(j + 1) * P], k(6 * h + 2 * j), q(6 * h + 2 * j + 1),
                                         start=True, stop=True)
                    mark(last, f"level{m}")
                else:
                    if n == 1:
                        pe.wait_ge(s["act_mix"], AV("att2_evac"))
                    elif n == 7:
                        pe.wait_ge(s["act_mix"], AV("i_tok"))
                    else:
                        pe.wait_ge(s["dve_mix"], DV(f"att{LEVELS[n - 1]}"))
                    mats(0 if n == 7 else 4, k, q, f"level{m}")

            for t in range(4):
                channel_tile(p0 + O_MIX + t, e0 + E_MIX + t)
            channel_tile(p0 + O_MIX + 4, e0 + E_MIX + 4)
            level(0)
            channel_tile(p0 + O_MIX + 5, e0 + E_MIX + 5, between=lambda: level(1))
            level(2)
            channel_tile(p0 + O_MIX + 6, e0 + E_MIX + 6, between=lambda: level(3))
            level(4)
            pos, ev = p0 + O_MIX + 7, e0 + E_MIX + 7
            weights(pos)
            banks_free(ev)
            w = ring_k(pos % R, P)
            for k in range(DB):
                last = pe.matmul(ps[:, 2 * (ev % 2), 0:L], w[:, k, :], hT[:, k, :], start=(k == 0), stop=(k == DB - 1))
            last.then_inc(w_used[pos % R], 1)
            level(5)
            pe.wait_ge(s["ev_act"], e0 + E_MIX + 8)
            pe.wait_ge(s["ev_dve"], e0 + E_MIX + 8)
            for b in range(TB):
                for j in range(HP):
                    last = pe.transpose(ps[:, b, j * P:(j + 1) * P], cpT[:, 12 + j, b * P:(b + 1) * P], ident[:, :])
            mark(last, "tokens")
            level(6)
            level(7)
            pe.wait_ge(s["dve_mix"], DV(f"att{LEVELS[6]}"))
            mats(4, head(cpT[:, 9:12, :]), head(cpT[:, 6:9, :]), "level0")
            pe.wait_ge(s["dve_mix"], DV("att0"))
            pe.wait_ge(s["act_mix"], AV("i_tok"))
            for j in range(HP):
                for h in range(2):
                    o = ps[64 * h:64 * h + 64, 6 + j // 2, (j % 2) * L:(j % 2 + 1) * L]
                    v = [i_tok[:, b, P * j + 64 * h:P * j + 64 * h + 64] for b in range(TB)]
                    u = 6 * h + 2 * j
                    pe.matmul(o[:, 0:P], v[0], hgAtt[:, u, :], start=(j % 2 == 0), stop=False, skip_group_check=True)
                    pe.matmul(o[:, P:L], v[0], hgAtt2[:, 3 * h + j, :], start=False, stop=False, skip_group_check=True)
                    last = pe.matmul(o[:, P:L], v[1], hgAtt[:, u + 1, :], start=False, stop=True,
                                     skip_group_check=True)
            mark(last, "hg_o")
            pe.wait_ge(s["act_mix"], AV("low_in"))
            pe.wait_ge(s["c_lowrank"], 48 * (l + 1))
            for j in range(HP):
                c = slice(j * P, (j + 1) * P)
                pe.matmul(psf[:, 1024 + j * L:1024 + (j + 1) * L], lowA[0:64, c], cpT[0:64, 27, :], start=True, stop=True)
                pe.matmul(psf[:, 2048 + j * L:2048 + (j + 1) * L], lowA[64:128, c], cpT[64:128, 27, :], start=True,
                          stop=True)
            pe.wait_ge(s["act_mix"], AV("hg_sq"))
            head_sums(0, hgC, "hg_ss")
            pe.wait_ge(s["dve_mix"], DV("o_norm"))
            for j in range(HP):
                last = pe.matmul(psf[:, 2816 + j * L:2816 + (j + 1) * L], lowG[:, j * P:(j + 1) * P], cpT[:, 28, :],
                                 start=True, stop=True)
            mark(last, "low_rank")
            pe.wait_ge(s["act_mix"], AV("hg_rms"))
            for b in range(TB):
                for j in range(HP):
                    last = pe.transpose(ps[:, b, j * P:(j + 1) * P], cpT[:, 24 + j, b * P:(b + 1) * P], ident[:, :])
            mark(last, "tokens2")
            pe.wait_ge(s["act_mix"], AV("kk_sq"))
            head_sums(0, rwT0, "kk_ss")
            pe.wait_ge(s["dve_mix"], DV("rk"))
            head_sums(1024, rwT1, "bonus")
            pe.wait_ge(s["dve_mix"], DV("operands"))
            for i, v in enumerate((bh_, kh_)):
                for j in range(HP):
                    last = pe.transpose(ps[:, 6 + i, j * P:(j + 1) * P], v[:, j, 0:P], ident[:, :])
            mark(last, "bk_tok")
            mats(0, head(bh_), head(at_), "LabT")
            pe.wait_ge(s["act_mix"], AV("bk_tok"))
            mats(4, head(at_), head(bh_), "Lab")
            pe.wait_ge(s["act_mix"], AV("LabT"))
            mats(0, head(kh_), head(at_), "LakT")
            pe.wait_ge(s["dve_mix"], DV("Lab"))
            mats(4, head(bh_), head(rt_), "LrbT")
            pe.wait_ge(s["dve_mix"], DV("LakT"))
            mats(0, head(kh_), head(rt_), "LrkT")
            e = lambda v: (lambda i: v[:, i, :])
            X, XT, N, NT = e(iX), e(iXT), e(iN), e(iNT)
            pe.wait_ge(s["dve_mix"], DV("base"))
            for p in range(3):
                for h in range(2):
                    if p > 0:
                        pe.wait_ge(s["dve_mix"], DV(f"XT{p - 1}_{h}"))
                    half_mats(0, h, NT, N, f"N{p}_{h}")
                    if p < 2:
                        half_mats(4, h, N, NT, f"NT{p}_{h}")
                for h in range(2):
                    pe.wait_ge(s["act_mix"], AV(f"N{p}_{h}"))
                    half_mats(0, h, XT, N, f"dX{p}_{h}")
                    if p < 2:
                        pe.wait_ge(s["dve_mix"], DV(f"NT{p}_{h}"))
                    half_mats(4, h, N, XT, f"dXT{p}_{h}")
            for p in range(3):
                pe.wait_ge(s["dve_mix"], DV(f"B{p}"))
                for h in range(2):
                    if p > 0:
                        pe.wait_ge(s["dve_mix"], DV(f"mXT{p - 1}_{h}"))
                    half_mats(0, h, N, X, f"W{p}_{h}")
                for h in range(2):
                    pe.wait_ge(s["act_mix"], AV(f"W{p}_{h}"))
                    if p < 2:
                        half_mats(0, h, XT, NT, f"mX{p}_{h}")
                    half_mats(4, h, NT, XT, f"mXT{p}_{h}")
            pe.wait_ge(s["dve_mix"], DV("mXT2_1"))
            for c in range(2):
                heads = [(2 * j + h, j, 6 * h + 2 * j + c, slice(64 * h, 64 * h + 64), slice(128 * j + 64 * h, 128 * j + 64 * h + 64))
                         for j in range(HP) for h in range(2)]
                for u, j, i, rows, cu in heads:
                    o = ps[:, 3 * (u % 2), 64 * j:64 * j + 64]
                    last = pe.matmul(o, LakT[:, i, :], v_tok[:, c, cu], start=True, stop=(c == 0))
                    if c == 1:
                        last = pe.matmul(o, at_[rows, j, P:L], rwState[rows, j, :], start=False, stop=True)
                mark(last, f"Z{c}")
                pe.wait_ge(s["act_mix"], AV(f"Z{c}"))
                for u, j, i, rows, cu in heads:
                    last = pe.matmul(ps[:, 1, cu], iXT[:, i, :], rwZ[:, c, cu], start=True, stop=True)
                mark(last, f"P{c}")
                pe.wait_ge(s["act_mix"], AV(f"P{c}"))
                if c == 0:
                    for u, j, i, rows, cu in heads:
                        o = ps[rows, 2, 64 * j:64 * j + 64]
                        pe.matmul(o, bk_tok[:, 0, cu], rwP[:, 0, cu], start=True, stop=False)
                        last = pe.matmul(o, bk_tok[:, 1, cu], v_tok[:, 0, cu], start=False, stop=True)
                    mark(last, "state")
                for u, j, i, rows, cu in heads:
                    o = ps[rows, 6 + j // 2, (j % 2) * L + c * P:(j % 2) * L + (c + 1) * P]
                    pe.matmul(o, rwP[:, c, cu], LrbT[:, i, :], start=True, stop=False)
                    last = pe.matmul(o, v_tok[:, c, cu], LrkT[:, i, :], start=False, stop=(c == 0))
                    if c == 1:
                        last = pe.matmul(o, rwState[rows, j, :], rt_[rows, j, P:L], start=False, stop=True)
                mark(last, f"y{c}")
                if c == 0:
                    pe.wait_ge(s["dve_mix"], DV("state"))
            memory_transposes(l, 0, 4)
            pe.wait_ge(s["act_mix"], AV("y"))
            head_sums(3072, at_, "mean")
            memory_transposes(l, 2, 0)
            pe.wait_ge(s["act_mix"], AV("y_sq"))
            head_sums(3072, kh_, "var")
            pe.wait_ge(s["memT_act"], l + 1)
            pe.wait_ge(s["memT_dve"], l + 1)
            for t in range(2):
                channel_tile(p0 + O_K + t, e0 + E_K + t, src=memT)
            pe.wait_ge(s["dve_mix"], DV("y_rw"))
            pe.wait_ge(s["ev_act"], e0 + E_K + 2)
            pe.wait_ge(s["ev_dve"], e0 + E_K + 2)
            out_product(p0 + O_MO, DB, hid, lambda t: None)

        def attention_pe(l, p0, e0):
            for t in range(2):
                token_tile(p0 + O_V + t, e0 + E_V + t, src=memT, bank=4 + 2 * t)

            def bank_free(bank):
                pe.wait_ge(s["ev_act"], e0 + E_V + 1 + bank // 2)
                pe.wait_ge(s["ev_dve"], e0 + E_V + 1 + bank // 2)
            norm_transposes(6 + 4 * l, bank_free)
            hT_ready(6 + 4 * l)
            for t in range(2):
                channel_tile(p0 + O_Q + t, e0 + E_Q + t)
            pe.wait_ge(s["ev_act"], e0 + E_Q + 2)
            pe.wait_ge(s["ev_dve"], e0 + E_Q + 2)
            for h in range(4):
                for b in range(TB):
                    for k in range(2):
                        last = pe.matmul(ps[:, 4 + h, b * L:(b + 1) * L], xqT[:, 2 * h + k, b * P:(b + 1) * P],
                                         xkT[:, 2 * h + k, :], start=(k == 0), stop=(k == 1))
                last.then_inc(s["xa_s"], 1)
            for h in range(4):
                pe.wait_ge(s["xa_p"], 4 * l + h + 1)
                for c in range(2):
                    for b in range(TB):
                        last = pe.transpose(ps[:, h, c * L + b * P:c * L + (b + 1) * P], xP[:, h, b, c * P:(c + 1) * P],
                                            ident[:, :])
                last.then_inc(s["xa_pT"], 1)
            for h in range(4):
                pe.wait_ge(s["xa_pT_dve" if h % 2 else "xa_pT_act"], 2 * l + h // 2 + 1)
                for u in range(2):
                    for c in range(2):
                        last = pe.matmul(ps[:, 4 + h, u * L:(u + 1) * L], xv[:, c, (2 * h + u) * P:(2 * h + u + 1) * P],
                                         xPT[:, h, c, :], start=(c == 0), stop=(c == 1))
                last.then_inc(s["xa_o"], 1)
            pe.wait_ge(s["xa_y_act"], 2 * l + 2)
            pe.wait_ge(s["xa_y_dve"], 2 * l + 2)
            out_product(p0 + O_WO, DB, hid, lambda t: None)

        pe.wait_ge(s["c_packs"], 2 * 16 * (len(PACK) + 1))
        pe.wait_ge(s["masks"], 1)
        for l in range(2):
            p0, e0 = POS_C + C_TILES * l, EV_C + C_EVS * l
            norm_transposes(4 + 4 * l)
            pe.wait_ge(s["x_ready"], 8 + 8 * l)
            pe.transpose(ps[:, 0, 0:PACK_N], packC[l], ident[0:PACK_N, 0:PACK_N]).then_inc(s["c_cols_T"], 1)
            hT_ready(4 + 4 * l)
            pe.wait_ge(s["c_cols"], l + 1)
            gated_ffn(p0 + O_F1, e0 + E_F1)
            norm_transposes(5 + 4 * l)
            hT_ready(5 + 4 * l)
            mixer_pe(l, p0, e0)
            attention_pe(l, p0, e0)
            norm_transposes(7 + 4 * l)
            hT_ready(7 + 4 * l)
            gated_ffn(p0 + O_F2, e0 + E_F2)

    @block.vector
    def _(dve):
        chain = [0]

        def link(ins):
            chain[0] += 1
            ins.then_inc(s["dve_chain"], 1)
            dve.wait_ge(s["dve_chain"], chain[0])

        def tile_out(pos, ev, dst):
            dve.wait_ge(w_used[pos % R], pos // R + 1)
            dve.tensor_copy(dst, ps[:, 2 * (ev % 2) + 1, 0:512]).then_inc(s["ev_dve"], 1)

        def chan(t0, t):
            return pT[:, t0 + 4 * t + 2:t0 + 4 * t + 4, :].rearrange("p b n -> p (b n)")

        def ada_acc_tile(l, t):
            pos, n = pos_ada(l, t), 12 * l + t
            acc = ada_acc[n % 4 // 2 if l else n % 2]
            dve.wait_ge(w_loaded[pos % R], loaded(pos))
            if n >= ADA_0 + 2:
                dve.wait_ge(s["ada_sum"], t - ADA_0 - 1 if l == 0 else ADA_T - ADA_0 - 1 + t // 2)
            w = ring_k(pos % R, 512)
            link(dve.tensor_scalar(acc, w[:, 0, :], cT[:, 0:1], None, ALU.mult))
            for k in range(1, DB):
                ins = dve.scalar_tensor_tensor(acc, w[:, k, :], cT[:, k:k + 1], acc, ALU.mult, ALU.add)
                if k < DB - 1:
                    link(ins)
            ins.then_inc(w_used[pos % R], 1)

        def ada_out(l, t):
            pos, n = pos_ada(l, t), 12 * l + t
            q = 32 * (t % 4)
            if ada_on_vector(l, t):
                dve.wait_ge(s["ada_sum"], t - ADA_0 + 1 if l == 0 else ADA_T - ADA_0 + 1 + t // 2)
            else:
                dve.wait_ge(w_used[pos % R], pos // R + 1)
            if t == 0:
                dve.wait_ge(s["mod_in"], 64 * (l + 1))
            r = modrow[q:q + 1, t // 4, :]
            dve.tensor_tensor(r, ps[q:q + 1, ADA_BANK[l] + n % 2, :], r, ALU.add).then_inc(s["ada_ev"], 1)

        def bias_out(g):
            dve.wait_ge(s["bias_mm"], g + 1)
            dve.tensor_tensor(biasf[:, :, :].rearrange("p h (x c) -> p (h x) c", x=6)[:, :, 4 * g:4 * g + 4],
                              ps[:, 6 + g % 2, 0:384].rearrange("p (c y) -> p y c", c=4),
                              wmask[:, 4 * g:4 * g + 4].unsqueeze(1).to_broadcast([P, 96, 4]),
                              ALU.add).then_inc(s["bias_ev"], 1)

        def mod_coefs(l, first, norms):
            dve.wait_ge(s["mod_T"], l + 1 + (first > 0 or l > 0))
            last = 16 if norms == (0,) else 48
            link(dve.tensor_copy(modT[:, l, first:last], ps[:, 4 if last == 48 else 0, first:last]))
            for n in norms:
                g = cols[:, C_NG + 32 * l + 16 * n:C_NG + 32 * l + 16 * n + 8]
                ins = dve.scalar_tensor_tensor(coef[:, l, n, :], modT[:, l, 24 * n + 8:24 * n + 16], 1.0, g,
                                               ALU.add, ALU.mult)
            ins.then_inc(s["coef"], 1)

        def gate_gains(l):
            dve.wait_ge(s["gate_bc"], l + 1)
            dve.wait_ge(s["gain_in"], 32 * (l + 1))
            for i in range(4):
                g = gains[:, i // 2, (i % 2) * 512:(i % 2) * 512 + 512]
                ins = dve.tensor_tensor(g, ps[:, i, :], g, ALU.mult)
            ins.then_inc(s["gate_done"], 1)

        def normalise(site, b):
            dve.wait_ge(s["ssq"], 2 * site + b + 1)
            link(dve.reciprocal(stat[:, 2 + b:3 + b], stat[:, 2 + b:3 + b]))
            dve.tensor_scalar(xn[:, b, :], x[:, b, :], stat[:, 2 + b:3 + b], None, ALU.mult).then_inc(s["xn_ready"], 1)

        def gated_site(site, pos, g):
            for b in range(TB):
                dve.wait_ge(s["y_ssq"], 2 * (site - 1) + b + 1)
                link(dve.reciprocal(stat[:, 6 + b:7 + b], stat[:, 6 + b:7 + b]))
                link(dve.scalar_tensor_tensor(xn[:, b, :], ps[:, 2 * b:2 * b + 2, :].rearrange("p c n -> p (c n)"),
                                              stat[:, 6 + b:7 + b], gains[:, g, :], ALU.mult, ALU.mult))
                dve.tensor_tensor(x[:, b, :], x[:, b, :], xn[:, b, :], ALU.add).then_inc(s["x_ready"], 1)
                normalise(site, b)

        def norm_out(site, A, B):
            for b in range(2, 4):
                dve.wait_ge(s["xn_T"], 4 * site + 2 * (b - 2) + 2)
                for u in range(2):
                    k = 2 * b + u
                    o, i = hT[:, k, :], ps[:, 4 + b, u * L:(u + 1) * L]
                    if B is None:
                        ins = dve.tensor_scalar(o, i, A[:, k:k + 1], None, ALU.mult)
                    else:
                        ins = dve.tensor_scalar(o, i, A[:, k:k + 1], B[:, k:k + 1], ALU.mult, ALU.add)
            ins.then_inc(s["hT_dve"], 1)

        dve.wait_ge(s["cols_T"], 1)
        dve.tensor_copy(cols[:, 0:248], ps[:, 4, 0:248]).then_inc(s["cols"], 1)
        dve.tensor_copy(rpbT, ps[0:64, 5, 0:96]).then_inc(s["cols"], 1)
        for g in range(4):
            bias_out(g)
        for t in range(ADA_0):
            ada_out(0, t)
            bias_out(4 + t)
        for b in range(TB):
            normalise(0, b)
        mod_coefs(0, 0, (0,))
        dve.wait_ge(s["coef"], 1)
        norm_out(0, coef[:, 0, 0, :], modT[:, 0, 0:8])
        for t in range(5):
            ada_acc_tile(0, 4 + t)
            tile_out(POS_ZX[t], EV_ZX + t, chan(0, t))
            if t >= 1:
                ada_out(0, 3 + t)
            if t < 4:
                bias_out(8 + 2 * t)
                bias_out(9 + 2 * t)
        dve.wait_ge(s["alog_e"], 1)
        dve.tensor_scalar(small[0:32, 2:3], small[0:32, 2:3], -1.0, None, ALU.mult)
        dve.wait_ge(s["ev_act"], EV_DT + 1)
        dve.scalar_tensor_tensor(dtw[:, 1, :], dtw[:, 0, :], -1.0, dtw[:, 0, :], ALU.mult, ALU.min)\
            .then_inc(s["ev_dve"], 1)
        ada_acc_tile(0, 9)
        ada_out(0, 8)

        def conv_block(j):
            u, o = pT[:, 8 + j, :], cvT[:, j, :]
            tap = lambda d: cols[:, C_CW + 12 * d + j:C_CW + 12 * d + j + 1]
            link(dve.tensor_scalar(o, u, tap(2), cols[:, C_CB + j:C_CB + j + 1], ALU.mult, ALU.add))
            for d in (0, 1, 3, 4):
                k = d - 2
                lo, hi = max(0, -k), L - max(0, k)
                ins = dve.scalar_tensor_tensor(o[:, lo:hi], u[:, lo + k:hi + k], tap(d), o[:, lo:hi], ALU.mult, ALU.add)
                if d < 4:
                    link(ins)
            return ins

        for t in range(4):
            if t < 2:
                ada_acc_tile(0, 10 + t)
            tile_out(POS_QK[t], EV_QK + t, chan(20, t))
            if t < 3:
                ada_out(0, 9 + t)
            if t == 0:
                dve.wait_ge(s["ev_act"], EV_ZX + 5)
            for j in range(4 * t, min(4 * t + 4, CONV_B)):
                ins = conv_block(j)
            if t < 3:
                ins.then_inc(s["conv"], 1)
        dve.wait_ge(s["dt_ln"], 1)
        link(dve.scalar_tensor_tensor(dtw[:, 2, :], dtw[:, 0, :], 0.0, dtw[:, 1, :], ALU.max, ALU.add))
        link(dve.tensor_scalar(dtw[:, 3, :], dtw[:, 2, :], small[0:32, 2:3], None, ALU.mult))
        link(dve.tensor_tensor_scan(dtw[:, 0, :], ones[0:32, 0:1].to_broadcast([32, L]), dtw[:, 3, :], 0.0,
                                    ALU.mult, ALU.add))
        link(dve.tensor_scalar(dtw[:, 3, :], dtw[:, 3, :], dirs[:, 1:2], None, ALU.mult))
        dve.scalar_tensor_tensor(Urow[0:32, :], dtw[:, 0, :], dirs[:, 0:1], dtw[:, 3, :], ALU.mult, ALU.add)\
            .then_inc(s["U_ready"], 2)
        for t in range(2):
            tile_out(POS_V[t], EV_V + t, v_na[:, 1, 512 * t:512 * t + 512])
        gate_gains(0)
        for b in range(2):
            dve.wait_ge(s["X_T"], 3 + b)
            dve.tensor_copy(X[:, 1, 512 * b:512 * b + 512], ps[:, b, :]).then_inc(s["X_ev"], 1)
        dve.wait_ge(s["U_T"], 1)
        v = ps[:, 5, 0:128].rearrange("p (b w r) -> p b w r", b=2, w=2)
        dve.tensor_scalar(Ucol[:, :, 0, :], v[:, :, 0, :], -1.0, None, ALU.mult)
        dve.tensor_copy(Ucol[:, :, 1, :], v[:, :, 1, :]).then_inc(s["U_cols"], 1)
        dve.wait_ge(s["U_cols"], 1)
        mod_coefs(0, 16, (1,))
        dve.wait_ge(s["CB"], 1)
        dve.wait_ge(s["z_silu"], 1)
        t1 = 0
        for i in range(2 * SSD_H):
            h, d = i // 2, i % 2
            g, r, n0 = h // 8, d * 16 + h, (L if d == 0 else P)
            t0 = 0 if d == 1 else P
            dve.wait_ge(s["ss_exp"], i + 1)
            if i >= 2:
                dve.wait_ge(s["ss_y"], i - 1)
            e, m = ssE[:, i % 2, :], ssM[:, i % 2, :]
            dve.scalar_tensor_tensor(m[:, 0:n0], e[:, 0:n0], Ucol[:, 0, 1, r:r + 1], ps[:, 6 + g, 0:n0],
                                     ALU.mult, ALU.mult)
            dve.scalar_tensor_tensor(m[:, n0:384], e[:, n0:384], Ucol[:, 1, 1, r:r + 1],
                                     ps[:, 6 + g, L + t0:2 * L], ALU.mult, ALU.mult).then_inc(s["ss_M"], 1)
            if i % 8 in (1, 4, 6):
                if t1 == 0:
                    ada_acc_tile(1, 0)
                ada_out(1, t1)
                if t1 % 2 == 1 and t1 < 11:
                    ada_acc_tile(1, t1 + 1)
                t1 += 1
            if i % 4 == 3:
                j = i // 4
                dve.wait_ge(s["ss_y"], i + 1)
                link(dve.scalar_tensor_tensor(cvT[:, j, :], cvT[:, j, :], small[:, 4 + j:5 + j],
                                              ps[:, 4 + j % 2, 0:L], ALU.mult, ALU.add))
                dve.tensor_tensor(pT[:, j, :], pT[:, j, :], cvT[:, j, :], ALU.mult).then_inc(s["y_gated"], 1)
        dve.wait_ge(s["y_rs"], 1)
        for j in range(DB):
            ins = dve.scalar_tensor_tensor(hid[:, j, :], pT[:, j, :], cols[:, C_SN + j:C_SN + j + 1], cvT[:, 8, :],
                                           ALU.mult, ALU.mult)
        ins.then_inc(s["y_ssd"], 1)

        def na_bias(h):
            dve.wait_ge(s["na_s"], h + 1)
            if h >= 2:
                dve.wait_ge(s["na_pT"], h - 1)
            for b in range(TB):
                x0 = 64 * (2 - 2 * b)
                ins = dve.scalar_tensor_tensor(naS[:, h % 2, b * L:(b + 1) * L], ps[:, h % 2, b * L:(b + 1) * L],
                                               NA_D ** -0.5, biasf[:, h, x0:x0 + L], ALU.mult, ALU.add)
            link(ins)
            dve.tensor_reduce(naM[:, h % 2, 0:2], naS[:, h % 2, :].rearrange("p (b n) -> p b n", b=2), AX.X, ALU.max,
                              negate=True).then_inc(s["na_max"], 1)

        def na_normalise(h):
            dve.wait_ge(s["na_exp"], h + 1)
            link(dve.reciprocal(naM[:, h % 2, 2:4], naM[:, h % 2, 2:4]))
            for b in range(TB):
                v = naS[:, h % 2, b * L:(b + 1) * L]
                ins = dve.tensor_scalar(v, v, naM[:, h % 2, 2 + b:3 + b], None, ALU.mult)
            ins.then_inc(s["na_p"], 1)

        def na_pair(j):
            dve.wait_ge(s["na_o"], 2 * j + 2)
            dve.tensor_copy(hid[:, 8 + j, :], ps[:, 4 + j % 2, 0:L]).then_inc(s["na_y"], 1)

        for h in range(NA_H + 3):
            if h < NA_H:
                na_bias(h)
            if 1 <= h <= NA_H:
                na_normalise(h - 1)
            if h >= 4 and h % 2 == 0:
                na_pair(h // 2 - 2)
        mod_coefs(1, 0, (0, 1))

        def mlp_out_dve(l):
            def body(j, i, t):
                pos, ev = POS_MLP[l] + j, EV_MLP[l] + j
                dve.wait_ge(w_used[pos % R], pos // R + 1 + i)
                half = [hid[:, bass.ds(t * 4 + 2 * u, 2), :].rearrange("p b n -> p (b n)") for u in range(2)]
                dve.tensor_scalar(half[1], ps[:, 2 * (ev % 2) + 1, :], 0.0, None, ALU.max).then_inc(s["ev_dve"], 1)
                dve.wait_ge(s["ev_act"], EV_MLP[l] + 1 + t)
                dve.tensor_tensor(half[0], relu[:, j, :], relu[:, j, :], ALU.mult)
                dve.wait_ge(s["ev_dve"], EV_MLP[l] + 1 + t)
                dve.tensor_tensor(half[1], half[1], half[1], ALU.mult).then_inc(s["hid"], 1)
            rounds(dve, 8, body)

        gated_site(1, POS_AOUT + 3, 0)
        norm_out(1, coef[:, 0, 1, :], modT[:, 0, 24:32])
        mlp_out_dve(0)
        gated_site(2, POS_MLP[0] + 15, 1)

        gate_gains(1)
        norm_out(2, coef[:, 1, 0, :], modT[:, 1, 0:8])
        for t in range(4):
            tile_out(POS_MQK + t, EV_MQK + t, arena[:, 4 * t + 2:4 * t + 4, :].rearrange("p b n -> p (b n)"))
        for w in range(2):
            for d in range(2):
                c = 16 * d + 8 * w
                dve.tensor_copy(perm[:, w, 8 * d:8 * d + 8], ident[0:32, c:c + 8]).then_inc(s["perm"], 1)
        dve.wait_ge(s["ev_act"], EV_MG + 1)
        dve.wait_ge(s["ev_dve"], EV_MG)
        dve.sem_inc(s["ev_dve"], 1)
        dve.wait_ge(s["g_cols"], 1)
        tile_out(POS_MVO, EV_MVO, mv[:, 1, 0:2, 0:256])
        f = lambda k: gw[0:16, k, :]
        sgn, flag = dirsB[:, 0:1], dirsB[:, 1:2]
        dve.wait_ge(s["g_IF"], 1)
        link(dve.tensor_copy(f(1), ps[0:16, 5, L:2 * L]))
        dve.scalar_tensor_tensor(f(2), f(1), -1.0, f(1), ALU.mult, ALU.min).then_inc(s["g_neg"], 1)
        tile_out(POS_MVO + 1, EV_MVO + 1, mv[:, 1, 2:4, 0:256])
        tile_out(POS_MVO + 2, EV_MVO + 2, mv[:, 1, 4:6, 0:256])
        dve.wait_ge(s["g_ln"], 1)
        link(dve.scalar_tensor_tensor(f(1), f(1), 0.0, f(2), ALU.min, ALU.subtract))
        link(dve.tensor_tensor_scan(f(2), ones[0:16, 0:1].to_broadcast([16, L]), f(1), 0.0, ALU.mult, ALU.add))
        link(dve.tensor_scalar(mtot[:, :], f(2)[:, L - 1:L], flag, None, ALU.mult))
        link(dve.tensor_scalar(f(3), f(1), flag, mtot[:, :], ALU.mult, ALU.add))
        link(dve.scalar_tensor_tensor(f(4), f(2), sgn, f(3), ALU.mult, ALU.add))
        link(dve.tensor_tensor(f(5), ps[0:16, 5, 0:L], f(4), ALU.subtract))
        tile_out(POS_MVO + 3, EV_MVO + 3, mv[:, 1, 6:8, 0:256])
        dve.tensor_tensor_scan(f(1), f(5), f(5), 0.0, ALU.max, ALU.max)
        link(dve.tensor_tensor_scan(f(2)[:, ::-1], f(5)[:, ::-1], f(5)[:, ::-1], 0.0, ALU.max, ALU.max))
        link(dve.tensor_tensor(f(2), f(2), f(1), ALU.subtract))
        link(dve.scalar_tensor_tensor(f(2), f(2), flag, f(1), ALU.mult, ALU.add))
        link(dve.tensor_scalar(nMrow[:, :], f(2), -1.0, None, ALU.mult))
        dve.tensor_tensor(f(3), nMrow[:, :], f(4), ALU.subtract).then_inc(s["g_rows2"], 1)
        for t in range(4):
            tile_out(POS_MVO + 4 + t, EV_MVO + 4 + t, mo[:, 1, 512 * t:512 * t + 512])
        dve.wait_ge(s["g_cols"], 2)

        def ml_weights(i):
            h, d = i // 2, i % 2
            n0, t0 = (L, P) if d == 0 else (P, 0)
            dve.wait_ge(s["ml_exp"], i + 1)
            if d == 0:
                dve.wait_ge(s["ml_S"], h + 1)
            if i >= 2:
                dve.wait_ge(s["ml_num"], i - 1)
            e, m, sc = mE[:, i % 2, :], mM[:, i % 2, :], ps[:, 2 + h % 2, :]
            dve.scalar_tensor_tensor(m[:, 0:n0], sc[:, 0:n0], P ** -0.5, e[:, 0:n0], ALU.mult, ALU.mult)
            dve.scalar_tensor_tensor(m[:, n0:384], sc[:, L + t0:2 * L], P ** -0.5, e[:, n0:384], ALU.mult, ALU.mult)\
                .then_inc(s["ml_M"], 1)

        def ml_head(i):
            h, d = i // 2, i % 2
            r = d * 8 + h
            dve.wait_ge(s["ml_num"], i + 1)
            bank = 4 + 2 * (i % 2)
            link(dve.tensor_copy(mden[:, 0, :], ps[:, bank:bank + 2, 256]))
            link(dve.scalar_tensor_tensor(mden[:, 1, :], mden[:, 0, :], -1.0, mden[:, 0, :], ALU.mult, ALU.max))
            link(dve.tensor_tensor(mden[:, 1, :], mden[:, 1, :], mcol[:, :, 1, r], ALU.max))
            link(dve.reciprocal(mden[:, 1, :], mden[:, 1, :]))
            for b in range(TB):
                o = mh[:, b, 256 * h:256 * h + 256]
                if d == 0:
                    ins = dve.tensor_scalar(o, ps[:, bank + b, 0:256], mden[:, 1, b:b + 1], None, ALU.mult)
                else:
                    ins = dve.scalar_tensor_tensor(o, ps[:, bank + b, 0:256], mden[:, 1, b:b + 1], o, ALU.mult, ALU.add)
            ins.then_inc(s["ml_h"], 1)
            if d == 0:
                dve.wait_ge(s["ml_h"], i + 1)

        for i in range(2 * ML_H + 1):
            if i < 2 * ML_H:
                ml_weights(i)
            if i >= 1:
                ml_head(i - 1)
        dve.wait_ge(s["ml_rs"], 1)
        dve.wait_ge(s["o_gain"], 1)
        for h in range(ML_H):
            for b in range(TB):
                v = slice(256 * h, 256 * h + 256)
                ins = dve.scalar_tensor_tensor(mh[:, b, v], mh[:, b, v], mstat[:, b, h:h + 1], mo[:, b, v],
                                               ALU.mult, ALU.mult)
            ins.then_inc(s["ml_y"], 1)
        for g in range(1, 8, 2):
            dve.wait_ge(s["ml_yT"], g + 1)
            dve.tensor_copy(hid[:, 2 * g:2 * g + 2, :].rearrange("p b n -> p (b n)"), ps[:, g, :])\
                .then_inc(s["ml_yT_dve"], 1)
        gated_site(3, POS_MOUT + 3, 0)
        norm_out(3, coef[:, 1, 1, :], modT[:, 1, 24:32])
        mlp_out_dve(1)
        gated_site(4, POS_MLP[1] + 15, 1)

        def gated_out_dve(ev0):
            def body(j, i, t):
                ev = ev0 + j
                dve.wait_ge(s["ev_act"], ev + 1 + i * R)
                dve.tensor_tensor(hid[:, bass.ds(t * 2, 2), :].rearrange("p b n -> p (b n)"), relu[:, j % 4, :],
                                  ps[:, 2 * (ev % 2) + 1, :], ALU.mult).then_inc(s["ev_dve"], 1)
            rounds(dve, FB // 2, body)

        def residual_site(site, pos, factor=None):
            for b in range(TB):
                if b == 0:
                    dve.wait_ge(s["y_half"], site)
                else:
                    dve.wait_ge(w_used[pos % R], pos // R + 1)
                y = ps[:, 2 * b:2 * b + 2, :].rearrange("p c n -> p (c n)")
                if factor is None:
                    ins = dve.tensor_tensor(x[:, b, :], y, x[:, b, :], ALU.add)
                else:
                    ins = dve.scalar_tensor_tensor(x[:, b, :], y, factor, x[:, b, :], ALU.mult, ALU.add)
                ins.then_inc(s["x_ready"], 1)
                if site < 4 + 4 * 2:
                    normalise(site, b)
                else:
                    dve.wait_ge(s["ssq"], 2 * site + b + 1)
                    link(dve.reciprocal(stat[:, 2 + b:3 + b], stat[:, 2 + b:3 + b]))
                    dve.wait_ge(s["final_in"], 16)
                    dve.scalar_tensor_tensor(xn[:, b, :], x[:, b, :], stat[:, 2 + b:3 + b], gains[:, 0, :],
                                             ALU.mult, ALU.mult).then_inc(s["out_ready"], 1)

        def mixer_dve(l, p0, e0):
            mark = marks["dve"].done
            AV, PV, own = (lambda n: at["act"](n, l)), (lambda n: at["pe"](n, l)), (lambda n: at["dve"](n, l))
            lin = lambda v: v.rearrange("p b n -> p (b n)")
            mats = lambda bank: ps[:, bank:bank + 4, 0:384].rearrange("p b (u n) -> p b u n", n=P)
            four = lambda v: v.rearrange("p (b u) n -> p b u n", b=4)
            every = lambda m: m.unsqueeze(1).unsqueeze(1).to_broadcast([P, 4, HP, P])

            def proj_out(t):
                tile_out(p0 + O_MIX + t, e0 + E_MIX + t, lin(cpT[:, 4 * t + 2:4 * t + 4, :]))

            lg = [cols[:, PACK_LB + 3 * i:PACK_LB + 3 * i + 3] for i in range(2)]
            link(dve.tensor_tensor(lbc[:, 0, :], lg[0], lg[1], ALU.max))
            dve.tensor_tensor(lbc[:, 1, :], lg[0], lbc[:, 0, :], ALU.subtract)
            mark(dve.tensor_tensor(lbc[:, 2, :], lg[1], lbc[:, 0, :], ALU.subtract), "lb_arg")
            tile_out(p0 + O_MIX, e0 + E_MIX, lin(cpT[:, 2:4, :]))
            tile_out(p0 + O_MIX + 1, e0 + E_MIX + 1, lin(cpT[:, 6:8, :]))
            dve.wait_ge(s["act_mix"], AV("lb_exp"))
            link(dve.tensor_tensor(lbc[:, 3, :], lbc[:, 1, :], lbc[:, 2, :], ALU.add))
            link(dve.reciprocal(lbc[:, 3, :], lbc[:, 3, :]))
            dve.tensor_tensor(lbc[:, 4, :], lbc[:, 1, :], lbc[:, 3, :], ALU.mult)
            link(dve.tensor_tensor(lbc[:, 5, :], lbc[:, 2, :], lbc[:, 3, :], ALU.mult))
            run = lbc[:, 4, :]
            if l == 1:
                link(dve.tensor_tensor(lbc[:, 6, :], lbc[:, 4, :], lbc[:, 5, :], ALU.add))
                run = lbc[:, 6, :]
            link(dve.tensor_tensor(lbc[:, 6, :], run, lbc[:, 4, :], ALU.subtract))
            link(dve.tensor_scalar(lbc[:, 6, :], lbc[:, 6, :], 0.0, None, ALU.max))
            dve.tensor_scalar(lbc[:, 7, :], lbc[:, 6, :], -1.0, 1.0, ALU.mult, ALU.add)
            dve.wait_ge(s["ev_act"], e0 + E_MIX + 2)
            dve.wait_ge(s["ev_dve"], e0 + E_MIX + 2)
            z, zc = aa(53, 2), aa(55, 2)
            link(dve.tensor_tensor(z, cpT[:, 2:4, :], cpT[:, 4:6, :], ALU.mult))
            for j in range(2):
                ins = dve.tensor_scalar(zc[:, j, :], z[:, j, :], pc("conv_w", 4 + j), pc("conv_b", j), ALU.mult, ALU.add)
            link(ins)
            for k in (1, 2):
                for j in range(2):
                    ins = dve.scalar_tensor_tensor(zc[:, j, k:L], z[:, j, 0:L - k], pc("conv_w", 2 * (2 - k) + j),
                                                   zc[:, j, k:L], ALU.mult, ALU.add)
                link(ins)
            dve.tensor_tensor(hid[:, 0:2, :], cpT[:, 0:2, :], zc, ALU.mult)
            dve.memset(flat(hh(8, 6)), 0.0)
            tile_out(p0 + O_MIX + 2, e0 + E_MIX + 2, lin(cpT[:, 10:12, :]))
            dve.wait_ge(s["ev_act"], e0 + E_MIX + 3)
            dve.wait_ge(s["ev_dve"], e0 + E_MIX + 3)
            fT, kT, qT = cpT[:, 9:12, :], cpT[:, 9:12, :], cpT[:, 6:9, :]
            link(dve.tensor_scalar(hgA, fT, -1.0, 80.0, ALU.mult, ALU.min))
            link(dve.tensor_scalar(hgB, hgA, 40.0, None, ALU.min))
            link(dve.tensor_scalar(hgA, hgA, 40.0, 0.0, ALU.subtract, ALU.max))
            mark(dve.scalar_tensor_tensor(lin(hgC), lin(fT), -1.0, lin(fT), ALU.mult, ALU.min), "hg_in")
            proj_out(3)
            dve.wait_ge(s["act_mix"], AV("hg_exp"))
            for j in range(HP):
                ins = dve.scalar_tensor_tensor(hgB[:, j, :], hgB[:, j, :], lbc[:, 6, j:j + 1], hgD[:, j, :],
                                               ALU.mult, ALU.add)
            mark(ins, "hg_mix")
            link(dve.scalar_tensor_tensor(lin(hgC), lin(fT), 0.0, lin(hgC), ALU.min, ALU.subtract))
            link(dve.tensor_tensor(hgA, hgA, hgC, ALU.add))
            dve.wait_ge(s["act_mix"], AV("hg_k"))
            for j in range(HP):
                ins = dve.tensor_scalar(kT[:, j, :], hgS[:, j, :], lbc[:, 7, j:j + 1], None, ALU.mult)
            dve.wait_ge(s["act_mix"], AV("hg_ln"))
            link(dve.tensor_tensor(hgA, hgA, hgB, ALU.add))
            for j in range(HP):
                ins = dve.tensor_tensor_scan(hgB[:, j, :], ones[:, 0:1].to_broadcast([P, L]), hgA[:, j, :], 0.0,
                                             ALU.mult, ALU.add)
            link(ins)
            E = (hgD, hgC)
            halves = lambda v, m: lin(v).rearrange("p (i u r) -> p i u r", u=2, r=m)

            def diff(n):
                m = LEVELS[n]
                b, o = halves(hgB, m), halves(E[n % 2], m)
                if n >= 2:
                    dve.wait_ge(s["dve_mix"], own(f"qk{LEVELS[n - 2]}"))
                mid = b[:, :, 0, m - 1:m].to_broadcast([P, HP * L // (2 * m), m])
                dve.tensor_tensor(o[:, :, 1, :], b[:, :, 1, :], mid, ALU.subtract)
                mark(dve.tensor_tensor(o[:, :, 0, :], mid, b[:, :, 0, :], ALU.subtract), f"diff{m}")

            def att(m, bank):
                dve.wait_ge(s["pe_mix"], PV(f"level{m}"))
                if m < 64:
                    dve.wait_ge(s["dve_mix"], own(f"att{2 * m or 1}"))
                mask = LV_MASK[m] if m else ident[:, :]
                mark(dve.copy_predicated(four(hgAtt), every(i32(mask)), mats(bank)), f"att{m}")

            diff(0)
            def operands(n):
                m = LEVELS[n]
                if n >= 2:
                    dve.wait_ge(s["pe_mix"], PV(f"level{LEVELS[n - 2]}"))
                dve.wait_ge(s["act_mix"], AV(f"exp{m}"))
                e = halves(E[n % 2], m)
                dve.tensor_tensor(halves(hgQ[n % 2], m)[:, :, 1, :], halves(qT, m)[:, :, 1, :], e[:, :, 1, :], ALU.mult)
                mark(dve.tensor_tensor(halves(hgK[n % 2], m)[:, :, 0, :], halves(kT, m)[:, :, 0, :], e[:, :, 0, :],
                                       ALU.mult), f"qk{m}")

            for n, m in enumerate(LEVELS):
                if n + 1 < len(LEVELS):
                    diff(n + 1)
                operands(n)
                if n == 1:
                    proj_out(4)
                if n == 3:
                    proj_out(5)
                if n == 5:
                    proj_out(6)
                    dve.wait_ge(s["ev_dve"], e0 + E_MIX + 7)
                    dve.sem_inc(s["ev_dve"], 1)
                if n == 7:
                    dve.wait_ge(s["ev_act"], e0 + E_MIX + 8)
                    pr = cpT[:, 18:29, :]
                    t8 = xnf.rearrange("p (b n) -> p b n", n=L)
                    for d, v in ((t8, pr[:, 0:8, :]), (hT[:, 0:3, :], pr[:, 8:11, :])):
                        dve.tensor_scalar(d[:, :, 0], v[:, :, 0], -1.0, None, ALU.mult)
                        ins = dve.tensor_tensor(d[:, :, 1:L], v[:, :, 0:L - 1], v[:, :, 1:L], ALU.subtract)
                    link(ins)
                    for j in range(11):
                        d = t8[:, j, :] if j < 8 else hT[:, j - 8, :]
                        ins = dve.scalar_tensor_tensor(pr[:, j, :], d, pc("rwkv_mu", j), pr[:, j, :], ALU.mult, ALU.add)
                    mark(ins, "shifted")
                if n >= 2:
                    att(LEVELS[n - 1], 4)
            att(1, 0)
            att(0, 4)
            rT, kr, vT = cpT[:, 18:21, :], cpT[:, 21:24, :], cpT[:, 24:27, :]
            dve.wait_ge(s["dve_mix"], own("shifted"))
            for j in range(HP):
                ins = dve.tensor_scalar(rwKK[:, j, :], kr[:, j, :], pc("rwkv_k_k", j), None, ALU.mult)
            mark(ins, "kk_raw")
            dve.wait_ge(s["act_mix"], AV("hg_rms"))
            link(dve.reciprocal(lin(hgD), lin(hgD)))
            mark(dve.tensor_tensor(lin(hgA), psf[:, 3072:3840], lin(hgD), ALU.mult), "o_norm")
            dve.wait_ge(s["dve_mix"], own("o_norm"))
            for j in range(HP):
                ins = dve.scalar_tensor_tensor(hid[:, 2 + j, :], hgA[:, j, :], pc("hgrn_norm", j), hgSG[:, j, :],
                                               ALU.mult, ALU.mult)
            mark(ins, "y_hg")
            dve.wait_ge(s["act_mix"], AV("sig"))
            for j in range(HP):
                for c in range(2):
                    t = slice(c * P, (c + 1) * P)
                    ins = dve.tensor_tensor_scan(rwS[:, j, t], ones[:, 0:1].to_broadcast([P, P]), rwSig[:, j, t], 0.0,
                                                 ALU.mult, ALU.add)
            link(ins)
            S4 = lin(rwS).rearrange("p (u n) -> p u n", n=P)
            link(dve.tensor_tensor(lin(rwSc).rearrange("p (u n) -> p u n", n=P), S4,
                                   S4[:, :, 63:64].to_broadcast([P, 2 * HP, P]), ALU.subtract))
            mark(dve.tensor_tensor(lin(rwEX), lin(rwSc), lin(rwSig), ALU.subtract), "centred")
            for j in range(HP):
                ins = dve.tensor_scalar(rwT1[:, j, :], rwA[:, j, :], 1.0, pc("rwkv_k_a", j), ALU.subtract, ALU.mult)
            link(ins)
            link(dve.scalar_tensor_tensor(lin(kr), lin(rwT1), 1.0, lin(kr), ALU.add, ALU.mult))
            for j in range(HP):
                ins = dve.scalar_tensor_tensor(rwT1[:, j, :], kr[:, j, :], pc("rwkv_r_k", j), rT[:, j, :],
                                               ALU.mult, ALU.mult)
            mark(ins, "rk")
            dve.wait_ge(s["pe_mix"], PV("kk_ss"))
            mark(dve.tensor_scalar(lin(rwT0), psf[:, 0:768], 1e-24, None, ALU.max), "kk_ss")
            dve.wait_ge(s["act_mix"], AV("decays"))
            dve.tensor_tensor(rwScal[:, 3:6], rwScal[:, 0:3], rt_[:, :, P - 1], ALU.mult)
            link(dve.tensor_tensor(kh_, kr, rwEN, ALU.mult))
            dve.tensor_tensor(rt_, rt_, rT, ALU.mult)
            dve.wait_ge(s["act_mix"], AV("kk_norm"))
            link(dve.reciprocal(lin(rwT0), lin(rwT0)))
            link(dve.tensor_tensor(rwKK, rwKK, rwT0, ALU.mult))
            link(dve.tensor_tensor(bh_, rwKK, rwA, ALU.mult))
            dve.tensor_tensor(bh_, bh_, rwEN, ALU.mult)
            dve.wait_ge(s["pe_mix"], PV("bonus"))
            dve.tensor_tensor(lin(rwBonus), psf[:, 1024:1792], lin(vT), ALU.mult)
            mark(dve.scalar_tensor_tensor(lin(at_), lin(rwKK), -1.0, lin(rwEX), ALU.mult, ALU.mult), "operands")
            dve.wait_ge(s["pe_mix"], PV("Lab"))
            mark(dve.tensor_tensor(four(iN), mats(4), every(m_bdT), ALU.mult), "Lab")
            dve.wait_ge(s["pool_mix"], l + 1)
            dve.wait_ge(s["pe_mix"], PV("LakT"))
            mark(dve.copy_predicated(four(LakT), every(i32(m_su)), mats(0)), "LakT")
            dve.wait_ge(s["act_mix"], AV("LabT"))
            link(dve.tensor_tensor(four(iNT), four(LabT), every(m_bd), ALU.mult))
            dve.wait_ge(s["pe_mix"], PV("LrbT"))
            dve.copy_predicated(four(LrbT), every(i32(m_iu)), mats(4))
            dve.tensor_tensor(four(iX), four(iN), every(ident[:, :]), ALU.add)
            dve.tensor_tensor(four(iXT), four(iNT), every(ident[:, :]), ALU.add)
            dve.wait_ge(s["pe_mix"], PV("LrkT"))
            mark(dve.copy_predicated(four(LrkT), every(i32(m_iu)), mats(0)), "base")
            dve.wait_ge(s["dve_mix"], own("base"))
            half_mats = lambda bank, h: ps[:, bank + 2 * h:bank + 2 * h + 2, 0:384]
            half = lambda v, h: v[:, 6 * h:6 * h + 6, :].rearrange("p (b u) n -> p b (u n)", b=2)
            for p in range(3):
                for h in range(2):
                    if p < 2:
                        dve.wait_ge(s["pe_mix"], PV(f"NT{p}_{h}"))
                        mark(dve.tensor_copy(half(iNT, h), half_mats(4, h)), f"NT{p}_{h}")
                for h in range(2):
                    if p > 0:
                        dve.wait_ge(s["dve_mix"], own(f"XT{p - 1}_{h}"))
                    dve.wait_ge(s["pe_mix"], PV(f"dX{p}_{h}"))
                    dve.tensor_tensor(half(iX, h), half(iX, h), half_mats(0, h), ALU.add)
                    dve.wait_ge(s["pe_mix"], PV(f"dXT{p}_{h}"))
                    mark(dve.tensor_tensor(half(iXT, h), half(iXT, h), half_mats(4, h), ALU.add), f"XT{p}_{h}")
            mark(dve.tensor_tensor(four(iN), four(LabT), every(LV_MASK[16]), ALU.mult), "B0")
            dve.wait_ge(s["dve_mix"], own("XT2_1"))
            for p in range(3):
                if p < 2:
                    dve.wait_ge(s["pe_mix"], PV(f"W{p}_1"))
                    mark(dve.tensor_tensor(four(iN), four(LabT), every(LV_MASK[32 << p]), ALU.mult), f"B{p + 1}")
                for h in range(2):
                    if p > 0:
                        dve.wait_ge(s["dve_mix"], own(f"mXT{p - 1}_{h}"))
                    if p < 2:
                        dve.wait_ge(s["pe_mix"], PV(f"mX{p}_{h}"))
                        dve.tensor_tensor(half(iX, h), half(iX, h), half_mats(0, h), ALU.add)
                    dve.wait_ge(s["pe_mix"], PV(f"mXT{p}_{h}"))
                    mark(dve.tensor_tensor(half(iXT, h), half(iXT, h), half_mats(4, h), ALU.add), f"mXT{p}_{h}")
            dve.wait_ge(s["pe_mix"], PV("state"))
            mark(dve.tensor_tensor(rwState, ps[:, 2, 0:192].rearrange("p (j n) -> p j n", n=64),
                                   rwScal[:, 3:6].unsqueeze(2).to_broadcast([P, HP, 64]), ALU.mult), "state")
            for i in range(2):
                dve.wait_ge(s["mem_T"], 4 * l + i + 1)
                for u in range(2):
                    ins = dve.tensor_scalar(memT[:, 2 * i + u, :], ps[:, 4 + i, u * L:(u + 1) * L],
                                            pc("mem_norm", 2 * i + u), None, ALU.mult)
            ins.then_inc(s["memT_dve"], 1)
            dve.wait_ge(s["pe_mix"], PV("mean"))
            mark(dve.scalar_tensor_tensor(lin(bh_), psf[:, 3072:3840], -1.0 / 64, lin(at_), ALU.mult, ALU.add), "y_centred")
            dve.wait_ge(s["act_mix"], AV("y_rms"))
            link(dve.reciprocal(lin(rt_), lin(rt_)))
            y = hid[:, 5:8, :]
            for j in range(HP):
                ins = dve.scalar_tensor_tensor(y[:, j, :], bh_[:, j, :], pc("rwkv_ln_w", j), rt_[:, j, :],
                                               ALU.mult, ALU.mult)
            link(ins)
            for j in range(HP):
                ins = dve.scalar_tensor_tensor(y[:, j, :], y[:, j, :], pc("rwkv_ln_b", j), rwBonus[:, j, :],
                                               ALU.add, ALU.add)
            link(ins)
            mark(dve.tensor_tensor(y, y, rwG, ALU.mult), "y_rw")
            for t in range(2):
                tile_out(p0 + O_K + t, e0 + E_K + t, flat(xkT[:, 4 * t + 2:4 * t + 4, :]))

        def attention_dve(l, p0, e0):
            for t in range(2):
                pos = p0 + O_V + t
                dve.wait_ge(w_used[pos % R], pos // R + 1)
                dve.tensor_copy(xv[:, 1, 512 * t:512 * t + 512], ps[:, 5 + 2 * t, :]).then_inc(s["ev_dve"], 1)
            norm_out(6 + 4 * l, pc("xattn_norm", 0, 8), None)
            for t in range(2):
                tile_out(p0 + O_Q + t, e0 + E_Q + t, flat(xqT[:, 4 * t + 2:4 * t + 4, :]))
            for h in range(4):
                dve.wait_ge(s["xa_s"], 4 * l + h + 1)
                link(dve.tensor_reduce(xM[:, h, 0:2], ps[:, 4 + h, :].rearrange("p (b n) -> p b n", b=2), AX.X, ALU.max,
                                       negate=True))
                dve.tensor_scalar(xM[:, h, 0:2], xM[:, h, 0:2], 1.0 / 16, None, ALU.mult).then_inc(s["xa_max"], 1)
            for h in range(4):
                dve.wait_ge(s["xa_exp"], 4 * l + h + 1)
                link(dve.reciprocal(xM[:, h, 2:4], xM[:, h, 2:4]))
                for b in range(TB):
                    ins = dve.tensor_scalar(xP[:, h, b, :], xP[:, h, b, :], xM[:, h, 2 + b:3 + b], None, ALU.mult)
                ins.then_inc(s["xa_p"], 1)
            for h in (1, 3):
                dve.wait_ge(s["xa_pT"], 4 * l + h + 1)
                dve.tensor_copy(flat(xPT[:, h, :, :]), ps[:, h, :]).then_inc(s["xa_pT_dve"], 1)
            for h in (1, 3):
                dve.wait_ge(s["xa_o"], 4 * l + h + 1)
                dve.tensor_copy(flat(hid[:, 2 * h:2 * h + 2, :]), ps[:, 4 + h, :]).then_inc(s["xa_y_dve"], 1)

        for l in range(2):
            p0, e0 = POS_C + C_TILES * l, EV_C + C_EVS * l
            dve.wait_ge(s["c_cols_T"], l + 1)
            dve.tensor_copy(cols[:, 0:PACK_N], ps[:, 0, 0:PACK_N]).then_inc(s["c_cols"], 1)
            dve.wait_ge(s["c_cols"], l + 1)
            norm_out(4 + 4 * l, pc("ffn1_norm", 0, 8), None)
            gated_out_dve(e0 + E_F1)
            if l == 0:
                dve.wait_ge(s["mem_ss"], 1)
                link(dve.reciprocal(stat[:, 10:12], stat[:, 10:12]))
                for b in range(TB):
                    ins = dve.tensor_scalar(memn[:, b, :], memn[:, b, :], stat[:, 10 + b:11 + b], None, ALU.mult)
                ins.then_inc(s["mem_xn"], 1)
            residual_site(5 + 4 * l, p0 + O_F1O + 5, 0.5)
            norm_out(5 + 4 * l, pc("mix_norm", 0, 8), None)
            mixer_dve(l, p0, e0)
            residual_site(6 + 4 * l, p0 + O_MO + 1)
            attention_dve(l, p0, e0)
            residual_site(7 + 4 * l, p0 + O_WO + 1)
            norm_out(7 + 4 * l, pc("ffn2_norm", 0, 8), None)
            gated_out_dve(e0 + E_F2)
            residual_site(8 + 4 * l, p0 + O_F2O + 5, 0.5)


def kernel(**inputs):
    import numpy as np
    from contextlib import ExitStack
    from concourse import bacc
    from concourse.bass_utils import run_bass_kernel_spmd

    nc = bacc.Bacc("TRN2", target_bir_lowering=False, num_devices=1)
    arrays, aps = {}, {}
    for name in inputs:
        v = np.ascontiguousarray(inputs[name])
        arrays["in_" + name] = v
        aps[name] = nc.dram_tensor("in_" + name, v.shape, mybir.dt.from_np(v.dtype), kind="ExternalInput").ap()
    out = nc.dram_tensor("out_x", (1, L, D), F32, kind="ExternalOutput").ap()
    with ExitStack() as ctx:
        build(nc, ctx, aps, out[0])
    r = run_bass_kernel_spmd(nc, [arrays], core_ids=[0])
    return r.results[0]["out_x"]
```
